# Optimizing a Trainium2 kernel written in Bass

```python
import math
import jax
import jax.numpy as jnp
from jax import lax
import numpy as np

D_MODEL = 1024
BATCH = 1
SEQ = 512
DEPTH = 2

HEAD_DIM = 64
ROT_DIM = HEAD_DIM // 4
ROPE_THETA = 500000.0
NORM_EPS = 1e-6
Q_BLOCK = 128
NEG_INF = -1e30
FORCED = 1e9

NSA_HEADS = 4
NSA_CMP_LEN = 32
NSA_CMP_STRIDE = 16
NSA_CMP_HIDDEN = 256
NSA_SLC_LEN = 64
NSA_TOPK = 16
NSA_WINDOW = 512
NSA_W = NSA_HEADS * HEAD_DIM

S5_GROUPS = 16
S5_GROUP_CH = 16
S5_W = S5_GROUPS * S5_GROUP_CH
S5_STATE = 64

GDN_HEADS = 4
GDN_CONV = 4
GDN_CHUNK = 64
GDN_W = GDN_HEADS * HEAD_DIM

SB_HEADS = 4
SB_W = SB_HEADS * HEAD_DIM

N_BRANCH = 4
BRANCH_W = NSA_W
D_FF = 256 * math.ceil(8 * D_MODEL / (3 * 256))

IN_SPLITS = (NSA_W, 6 * HEAD_DIM, 3 * NSA_HEADS, S5_W, 3 * GDN_W, GDN_HEADS, GDN_HEADS, GDN_W, 3 * SB_W, N_BRANCH * D_MODEL)
D_IN = sum(IN_SPLITS)
IN_OFFSETS = tuple(int(v) for v in np.cumsum(IN_SPLITS)[:-1])

kernel_name = "hybrid_nsa_s5_gdn_stickbreaking_block"

def rms_norm(x, w):
    xf = x.astype(jnp.float32)
    y = xf * lax.rsqrt(jnp.mean(xf * xf, axis=-1, keepdims=True) + NORM_EPS)
    return (y * w.astype(jnp.float32)).astype(x.dtype)

def l2norm(x):
    return x * lax.rsqrt(jnp.sum(x * x, axis=-1, keepdims=True) + NORM_EPS)

def rope_tables(positions):
    half = ROT_DIM // 2
    inv_freq = ROPE_THETA ** (-jnp.arange(half, dtype=jnp.float32) / half)
    ang = positions.astype(jnp.float32)[..., None] * inv_freq
    return jnp.cos(ang), jnp.sin(ang)

def apply_rope(x, cos, sin):
    half = ROT_DIM // 2
    x1, x2, rest = x[..., :half], x[..., half:ROT_DIM], x[..., ROT_DIM:]
    return jnp.concatenate([x1 * cos - x2 * sin, x2 * cos + x1 * sin, rest], axis=-1).astype(x.dtype)

def masked_softmax(s, mask):
    s = jnp.where(mask, s, NEG_INF)
    m = jnp.max(s, axis=-1, keepdims=True)
    p = jnp.where(mask, jnp.exp(s - m), 0.0)
    return p / jnp.maximum(jnp.sum(p, axis=-1, keepdims=True), 1e-30)

def causal_depthwise_conv(x, w):
    k = w.shape[0]
    return lax.conv_general_dilated(x, w[:, None, :], window_strides=(1,), padding=[(k - 1, 0)],
                                    dimension_numbers=('NWC', 'WIO', 'NWC'), feature_group_count=x.shape[-1])

def nsa_mixer(q, kv, gate_logits, cos, sin, q_norm, k_norm, cmp_pos, ck_w1, ck_w2, cv_w1, cv_w2):
    B_, S_ = q.shape[:2]
    f32 = jnp.float32
    scale = HEAD_DIM ** -0.5
    q = rms_norm(q.reshape(B_, S_, NSA_HEADS, HEAD_DIM), q_norm)
    q_rot = apply_rope(q, cos[:, :, None], sin[:, :, None])
    k_c, v_c, k_s, v_s, k_w, v_w = jnp.split(kv, 6, axis=-1)
    n_cmp = (S_ - NSA_CMP_LEN) // NSA_CMP_STRIDE + 1
    cmp_start = jnp.arange(n_cmp) * NSA_CMP_STRIDE
    cmp_idx = cmp_start[:, None] + jnp.arange(NSA_CMP_LEN)[None, :]

    def compress(t, pos, w1, w2):
        blocks = (t[:, cmp_idx] + pos).reshape(B_, n_cmp, NSA_CMP_LEN * HEAD_DIM)
        return jax.nn.gelu(blocks @ w1) @ w2

    kc = rms_norm(compress(k_c, cmp_pos[0], ck_w1, ck_w2), k_norm[0])
    vc = compress(v_c, cmp_pos[1], cv_w1, cv_w2).astype(f32)
    cmp_end = cmp_start + NSA_CMP_LEN - 1
    n_slc = S_ // NSA_SLC_LEN
    top_n = min(NSA_TOPK, n_slc)
    slc_start = jnp.arange(n_slc) * NSA_SLC_LEN
    overlap = ((cmp_start[:, None] < slc_start[None, :] + NSA_SLC_LEN)
               & (cmp_start[:, None] + NSA_CMP_LEN > slc_start[None, :])).astype(f32)
    ks_blk = apply_rope(rms_norm(k_s, k_norm[1]), cos, sin).reshape(B_, n_slc, NSA_SLC_LEN, HEAD_DIM)
    vs_blk = v_s.reshape(B_, n_slc, NSA_SLC_LEN, HEAD_DIM)
    pad = ((0, 0), (NSA_WINDOW, 0), (0, 0))
    kw = jnp.pad(apply_rope(rms_norm(k_w, k_norm[2]), cos, sin), pad)
    vw = jnp.pad(v_w, pad)
    gates = jax.nn.sigmoid(gate_logits.astype(f32)).reshape(B_, S_, NSA_HEADS, 3)
    b_idx = jnp.arange(B_)[:, None, None]
    within = jnp.arange(NSA_SLC_LEN)

    def block(c):
        t0 = c * Q_BLOCK
        t = t0 + jnp.arange(Q_BLOCK)
        qb = lax.dynamic_slice_in_dim(q, t0, Q_BLOCK, axis=1)
        qrb = lax.dynamic_slice_in_dim(q_rot, t0, Q_BLOCK, axis=1)
        gb = lax.dynamic_slice_in_dim(gates, t0, Q_BLOCK, axis=1)
        s_c = jnp.einsum('bqhd,bnd->bhqn', qb, kc, preferred_element_type=f32) * scale
        p_c = masked_softmax(s_c, cmp_end[None, :] <= t[:, None])
        o_c = jnp.einsum('bhqn,bnd->bqhd', p_c, vc)
        imp = jnp.einsum('bhqn,nj->bqj', p_c, overlap)
        forced = (slc_start[None, :] == ((t // NSA_SLC_LEN) * NSA_SLC_LEN)[:, None]) | (slc_start[None, :] == 0)
        imp = jnp.where(forced, FORCED, jnp.where(slc_start[None, :] <= t[:, None], imp, NEG_INF))
        _, sel = lax.top_k(imp, top_n)
        kg = ks_blk[b_idx, sel].reshape(B_, Q_BLOCK, top_n * NSA_SLC_LEN, HEAD_DIM)
        vg = vs_blk[b_idx, sel].reshape(B_, Q_BLOCK, top_n * NSA_SLC_LEN, HEAD_DIM).astype(f32)
        kpos = (sel[..., None] * NSA_SLC_LEN + within).reshape(B_, Q_BLOCK, top_n * NSA_SLC_LEN)
        s_s = jnp.einsum('bqhd,bqkd->bhqk', qrb, kg, preferred_element_type=f32) * scale
        p_s = masked_softmax(s_s, (kpos <= t[None, :, None])[:, None])
        o_s = jnp.einsum('bhqk,bqkd->bqhd', p_s, vg)
        kwb = lax.dynamic_slice_in_dim(kw, t0, Q_BLOCK + NSA_WINDOW, axis=1)
        vwb = lax.dynamic_slice_in_dim(vw, t0, Q_BLOCK + NSA_WINDOW, axis=1).astype(f32)
        wpos = t0 - NSA_WINDOW + jnp.arange(Q_BLOCK + NSA_WINDOW)
        diff = t[:, None] - wpos[None, :]
        wmask = (diff >= 0) & (diff < NSA_WINDOW) & (wpos[None, :] >= 0)
        s_w = jnp.einsum('bqhd,bkd->bhqk', qrb, kwb, preferred_element_type=f32) * scale
        p_w = masked_softmax(s_w, wmask)
        o_w = jnp.einsum('bhqk,bkd->bqhd', p_w, vwb)
        return gb[..., 0:1] * o_c + gb[..., 1:2] * o_s + gb[..., 2:3] * o_w

    out = lax.map(block, jnp.arange(S_ // Q_BLOCK))
    return jnp.moveaxis(out, 0, 1).reshape(B_, S_, NSA_W).astype(q.dtype)

def s5_mixer(u, lam_re, lam_im, log_dt, b_re, b_im, c_re, c_im, d_skip, glu_w):
    B_, S_ = u.shape[:2]
    f32 = jnp.float32
    uf = u.astype(f32).reshape(B_, S_, S5_GROUPS, S5_GROUP_CH)
    dt = jnp.exp(log_dt.astype(f32))[:, None]
    lr, li = lam_re.astype(f32), lam_im.astype(f32)
    mag = jnp.exp(lr * dt)
    ab_re, ab_im = mag * jnp.cos(li * dt), mag * jnp.sin(li * dt)
    den = lr * lr + li * li
    f_re = ((ab_re - 1.0) * lr + ab_im * li) / den
    f_im = (ab_im * lr - (ab_re - 1.0) * li) / den
    br, bi = b_re.astype(f32), b_im.astype(f32)
    bb_re = f_re[..., None] * br - f_im[..., None] * bi
    bb_im = f_re[..., None] * bi + f_im[..., None] * br
    bu_re = jnp.einsum('bsgc,gpc->bsgp', uf, bb_re)
    bu_im = jnp.einsum('bsgc,gpc->bsgp', uf, bb_im)
    a_re = jnp.broadcast_to(ab_re, bu_re.shape)
    a_im = jnp.broadcast_to(ab_im, bu_im.shape)

    def combine(e1, e2):
        a1r, a1i, b1r, b1i = e1
        a2r, a2i, b2r, b2i = e2
        return (a2r * a1r - a2i * a1i, a2r * a1i + a2i * a1r,
                a2r * b1r - a2i * b1i + b2r, a2r * b1i + a2i * b1r + b2i)

    _, _, x_re, x_im = lax.associative_scan(combine, (a_re, a_im, bu_re, bu_im), axis=1)
    y = (jnp.einsum('gcp,bsgp->bsgc', c_re.astype(f32), x_re)
         - jnp.einsum('gcp,bsgp->bsgc', c_im.astype(f32), x_im)
         + d_skip.astype(f32).reshape(S5_GROUPS, S5_GROUP_CH) * uf)
    y = jax.nn.gelu(y.reshape(B_, S_, S5_W))
    z = y @ glu_w.astype(f32)
    return (z[..., :S5_W] * jax.nn.sigmoid(z[..., S5_W:])).astype(u.dtype)

def chunk_gated_delta_rule(q, k, v, g, beta):
    B_, S_, H, d = q.shape
    C = GDN_CHUNK
    N = S_ // C

    def to_chunks(t):
        return jnp.moveaxis(t.reshape((B_, N, C, H) + t.shape[3:]), 3, 2)

    q, k, v, g, beta = [to_chunks(t) for t in (q, k, v, g, beta)]
    G = jnp.cumsum(g, axis=-1)
    tril = jnp.tril(jnp.ones((C, C), dtype=bool))
    strict = jnp.tril(jnp.ones((C, C), dtype=bool), -1)
    decay = jnp.where(tril, jnp.exp(jnp.where(tril, G[..., :, None] - G[..., None, :], 0.0)), 0.0)
    kb = k * beta[..., None]
    vb = v * beta[..., None]
    L = jnp.where(strict, jnp.einsum('bnhid,bnhjd->bnhij', kb, k) * decay, 0.0)
    eye = jnp.eye(C, dtype=L.dtype)
    T = lax.linalg.triangular_solve(eye + L, jnp.broadcast_to(eye, L.shape), left_side=True,
                                    lower=True, unit_diagonal=True)
    u = jnp.einsum('bnhij,bnhjd->bnhid', T, vb)
    w = jnp.einsum('bnhij,bnhjd->bnhid', T, kb * jnp.exp(G)[..., None])
    a_intra = jnp.where(tril, jnp.einsum('bnhid,bnhjd->bnhij', q, k) * decay, 0.0)
    q_dec = q * jnp.exp(G)[..., None]
    k_dec = k * jnp.exp(G[..., -1:] - G)[..., None]
    g_last = jnp.exp(G[..., -1])

    def step(state, xs):
        u_i, w_i, a_i, qd_i, kd_i, gl_i = xs
        v_new = u_i - jnp.einsum('bhcd,bhde->bhce', w_i, state)
        o = jnp.einsum('bhcd,bhde->bhce', qd_i, state) + jnp.einsum('bhij,bhje->bhie', a_i, v_new)
        state = state * gl_i[..., None, None] + jnp.einsum('bhcd,bhce->bhde', kd_i, v_new)
        return state, o

    xs = tuple(jnp.moveaxis(t, 1, 0) for t in (u, w, a_intra, q_dec, k_dec, g_last))
    state0 = jnp.zeros((B_, H, d, v.shape[-1]), dtype=q.dtype)
    _, o = lax.scan(step, state0, xs)
    return o.transpose(1, 0, 3, 2, 4).reshape(B_, S_, H, v.shape[-1])

def gdn_mixer(qkv, a_in, b_in, z, conv_w, a_log, dt_bias, o_norm):
    B_, S_ = qkv.shape[:2]
    f32 = jnp.float32
    act = jax.nn.silu(causal_depthwise_conv(qkv, conv_w))
    q, k, v = [t.reshape(B_, S_, GDN_HEADS, HEAD_DIM).astype(f32) for t in jnp.split(act, 3, axis=-1)]
    q = l2norm(q) * HEAD_DIM ** -0.5
    k = l2norm(k)
    beta = jax.nn.sigmoid(b_in.astype(f32))
    g = -jnp.exp(a_log.astype(f32)) * jax.nn.softplus(a_in.astype(f32) + dt_bias.astype(f32))
    o = chunk_gated_delta_rule(q, k, v, g, beta)
    o = rms_norm(o, o_norm) * jax.nn.silu(z.astype(f32).reshape(B_, S_, GDN_HEADS, HEAD_DIM))
    return o.reshape(B_, S_, GDN_W).astype(qkv.dtype)

def stickbreaking_mixer(qkv):
    B_, S_ = qkv.shape[:2]
    f32 = jnp.float32
    q, k, v = [t.reshape(B_, S_, SB_HEADS, HEAD_DIM) for t in jnp.split(qkv, 3, axis=-1)]
    scale = HEAD_DIM ** -0.5
    outs = []
    for c in range(S_ // Q_BLOCK):
        t0 = c * Q_BLOCK
        n_k = t0 + Q_BLOCK
        z = jnp.einsum('bqhd,bkhd->bhqk', q[:, t0:n_k], k[:, :n_k], preferred_element_type=f32) * scale
        t = t0 + jnp.arange(Q_BLOCK)
        mask = jnp.arange(n_k)[None, :] < t[:, None]
        log_nb = jnp.where(mask, -jax.nn.softplus(z), 0.0)
        after = lax.cumsum(log_nb, axis=3, reverse=True) - log_nb
        weights = jnp.where(mask, jnp.exp(jax.nn.log_sigmoid(z) + after), 0.0)
        outs.append(jnp.einsum('bhqk,bkhd->bqhd', weights, v[:, :n_k].astype(f32)))
    return jnp.concatenate(outs, axis=1).reshape(B_, S_, SB_W).astype(qkv.dtype)

def swiglu_ffn(x, w_gate, w_up, w_down):
    return (jax.nn.silu(x @ w_gate) * (x @ w_up)) @ w_down

def setup_inputs(seed: int = 0) -> dict:
    key = jax.random.key(seed)
    keys = iter(jax.random.split(key, 40))
    f32 = jnp.float32
    L = DEPTH

    def nrm(shape, scale):
        return jax.random.normal(next(keys), shape, f32) * scale

    def gain(shape):
        return 1.0 + nrm(shape, 0.05)

    def unif(shape, lo, hi):
        return jax.random.uniform(next(keys), shape, f32, minval=lo, maxval=hi)

    x = nrm((BATCH, SEQ, D_MODEL), 1.0)
    positions = (jnp.arange(SEQ, dtype=jnp.int32)[None, :]
                 + jax.random.randint(next(keys), (BATCH, 1), 0, 1024, dtype=jnp.int32))
    dt_g = jnp.exp(unif((L, GDN_HEADS), math.log(1e-3), math.log(1e-1)))
    return {
        'x': x,
        'positions': positions,
        'attn_norm': gain((L, D_MODEL)),
        'w_in': nrm((L, D_MODEL, D_IN), D_MODEL ** -0.5),
        'nsa_q_norm': gain((L, HEAD_DIM)),
        'nsa_k_norm': gain((L, 3, HEAD_DIM)),
        'nsa_cmp_pos': nrm((L, 2, NSA_CMP_LEN, HEAD_DIM), 0.1),
        'nsa_cmp_k_w1': nrm((L, NSA_CMP_LEN * HEAD_DIM, NSA_CMP_HIDDEN), (NSA_CMP_LEN * HEAD_DIM) ** -0.5),
        'nsa_cmp_k_w2': nrm((L, NSA_CMP_HIDDEN, HEAD_DIM), NSA_CMP_HIDDEN ** -0.5),
        'nsa_cmp_v_w1': nrm((L, NSA_CMP_LEN * HEAD_DIM, NSA_CMP_HIDDEN), (NSA_CMP_LEN * HEAD_DIM) ** -0.5),
        'nsa_cmp_v_w2': nrm((L, NSA_CMP_HIDDEN, HEAD_DIM), NSA_CMP_HIDDEN ** -0.5),
        's5_lam_re': -0.5 + nrm((L, S5_GROUPS, S5_STATE), 0.01),
        's5_lam_im': math.pi * jnp.arange(S5_STATE, dtype=f32) + nrm((L, S5_GROUPS, S5_STATE), 0.01),
        's5_log_dt': unif((L, S5_GROUPS), math.log(1e-3), math.log(1e-1)),
        's5_b_re': nrm((L, S5_GROUPS, S5_STATE, S5_GROUP_CH), (2 * S5_GROUP_CH) ** -0.5),
        's5_b_im': nrm((L, S5_GROUPS, S5_STATE, S5_GROUP_CH), (2 * S5_GROUP_CH) ** -0.5),
        's5_c_re': nrm((L, S5_GROUPS, S5_GROUP_CH, S5_STATE), (2 * S5_STATE) ** -0.5),
        's5_c_im': nrm((L, S5_GROUPS, S5_GROUP_CH, S5_STATE), (2 * S5_STATE) ** -0.5),
        's5_d': nrm((L, S5_W), 1.0),
        's5_glu_w': nrm((L, S5_W, 2 * S5_W), S5_W ** -0.5),
        'gdn_conv_w': nrm((L, GDN_CONV, 3 * GDN_W), GDN_CONV ** -0.5),
        'gdn_a_log': jnp.log(unif((L, GDN_HEADS), 1.0, 16.0)),
        'gdn_dt_bias': dt_g + jnp.log(-jnp.expm1(-dt_g)),
        'gdn_o_norm': gain((L, HEAD_DIM)),
        'w_branch': nrm((L, N_BRANCH, BRANCH_W, D_MODEL), BRANCH_W ** -0.5),
        'w_out': nrm((L, D_MODEL, D_MODEL), D_MODEL ** -0.5),
        'ffn_norm': gain((L, D_MODEL)),
        'w_gate': nrm((L, D_MODEL, D_FF), D_MODEL ** -0.5),
        'w_up': nrm((L, D_MODEL, D_FF), D_MODEL ** -0.5),
        'w_down': nrm((L, D_FF, D_MODEL), D_FF ** -0.5),
    }

def reference(x, positions, attn_norm, w_in, nsa_q_norm, nsa_k_norm, nsa_cmp_pos, nsa_cmp_k_w1, nsa_cmp_k_w2,
              nsa_cmp_v_w1, nsa_cmp_v_w2, s5_lam_re, s5_lam_im, s5_log_dt, s5_b_re, s5_b_im, s5_c_re, s5_c_im,
              s5_d, s5_glu_w, gdn_conv_w, gdn_a_log, gdn_dt_bias, gdn_o_norm, w_branch, w_out, ffn_norm,
              w_gate, w_up, w_down):
    B_, S_, _ = x.shape
    cos, sin = rope_tables(positions)
    for l in range(DEPTH):
        h = rms_norm(x, attn_norm[l])
        proj = h @ w_in[l]
        (nsa_q, nsa_kv, nsa_g, s5_u, gdn_qkv, gdn_a, gdn_b, gdn_z, sb_qkv,
         merge_logits) = jnp.split(proj, IN_OFFSETS, axis=-1)
        o_nsa = nsa_mixer(nsa_q, nsa_kv, nsa_g, cos, sin, nsa_q_norm[l], nsa_k_norm[l], nsa_cmp_pos[l],
                          nsa_cmp_k_w1[l], nsa_cmp_k_w2[l], nsa_cmp_v_w1[l], nsa_cmp_v_w2[l])
        o_s5 = s5_mixer(s5_u, s5_lam_re[l], s5_lam_im[l], s5_log_dt[l], s5_b_re[l], s5_b_im[l],
                        s5_c_re[l], s5_c_im[l], s5_d[l], s5_glu_w[l])
        o_gdn = gdn_mixer(gdn_qkv, gdn_a, gdn_b, gdn_z, gdn_conv_w[l], gdn_a_log[l], gdn_dt_bias[l], gdn_o_norm[l])
        o_sb = stickbreaking_mixer(sb_qkv)
        gates = jax.nn.sigmoid(merge_logits.astype(jnp.float32)).reshape(B_, S_, N_BRANCH, D_MODEL).astype(x.dtype)
        merged = jnp.zeros_like(x)
        for m, o_m in enumerate((o_nsa, o_s5, o_gdn, o_sb)):
            merged = merged + gates[:, :, m] * (o_m @ w_branch[l, m])
        x = x + merged @ w_out[l]
        x = x + swiglu_ffn(rms_norm(x, ffn_norm[l]), w_gate[l], w_up[l], w_down[l])
    return x


_drawn_inputs = setup_inputs


def setup_inputs(seed=0):
    import zlib

    import numpy as np

    out = dict(_drawn_inputs(seed))
    spreads = {}
    factors = {'nsa_q_norm': 8.0,
     'nsa_k_norm': 8.0,
     'nsa_cmp_pos': 2.861,
     's5_lam_re': 64.0,
     's5_lam_im': 29.056,
     's5_log_dt': 29.792,
     's5_b_re': 39.912,
     's5_b_im': 41.112,
     's5_c_re': 40.456,
     's5_c_im': 40.736}
    for name, (base, spread) in spreads.items():
        noise = np.random.default_rng([zlib.crc32(name.encode()), seed]).standard_normal(out[name].shape)
        drawn = base * np.exp(spread * noise) if base else spread * noise
        out[name] = jnp.asarray(drawn.astype(out[name].dtype))
    for name, factor in factors.items():
        out[name] = (out[name] * factor).astype(out[name].dtype)
    return out
```

```python
from contextlib import ExitStack

import concourse.bass as bass
import numpy as np
from concourse import mybir

ALU = mybir.AluOpType
ACT = mybir.ActivationFunctionType
AX_X = mybir.AxisListType.X
F32 = mybir.dt.float32
I32 = mybir.dt.int32
BF16 = mybir.dt.bfloat16

P = 128
D = 1024
KT = D // P
S = 512
NT = S // P
DEPTH = 2
HD = 64
FF = 2816
FT = FF // P
H = 4
NCMP = 31
EPS = 1e-6
NEG = -1e30
ROUND = 12582912.0
ROUND12 = 3072.0
TWO_PI = 6.283185307179586
INV_2PI = 1.0 / TWO_PI
C1, C2 = 6.28125, 0.0019340515
C3 = TWO_PI - C1 - C2
SIN_SCALE = 6.2831845
GELU_C = 0.7978845608028654
GELU_A = 0.044715

O_Q, O_KV, O_G, O_U, O_GDN, O_A, O_B, O_Z, O_SB, O_GATE = 0, 256, 640, 652, 908, 1676, 1680, 1684, 1940, 2708
KC, VC, KS, VS, KW, VW = (O_KV + HD * i for i in range(6))

TILES = ([(f"gdn{i}", [(O_GDN + P * i, P)]) for i in range(6)]
         + [("kskw", [(KS, HD), (KW, HD)]), ("vsvw", [(VS, HD), (VW, HD)]), ("kcvc", [(KC, HD), (VC, HD)])]
         + [(f"q{i}", [(O_Q + P * i, P)]) for i in range(2)]
         + [(f"u{i}", [(O_U + P * i, P)]) for i in range(2)]
         + [(f"sb{i}", [(O_SB + P * i, P)]) for i in range(4)]
         + [(f"z{i}", [(O_Z + P * i, P)]) for i in range(2)])
KEPT = [name for name, _ in TILES if name != "kcvc"]
TI = {name: i for i, name in enumerate(KEPT)}
NPJ = len(KEPT)
GLU_AT = 18
EARLY = 24

SLAB = {}


def _slabs():
    names = ["small"] + [n for n, _ in TILES] + ["sbv0", "sbv1"]
    names += [f"ck{i}" for i in range(4)] + [f"cv{i}" for i in range(4)] + ["cw2"]
    names += [f"gate{i}" for i in range(GLU_AT)] + ["glu"] + [f"gate{i}" for i in range(GLU_AT, EARLY)]
    for dt in range(KT):
        names += [f"br{dt}", f"gate{EARLY + dt}"]
    names += [f"out{dt}" for dt in range(KT)]
    for f in range(FT):
        names += [f"fg{f}", f"fu{f}"]
    for dt in range(KT):
        names += [f"dn{dt}_{j}" for j in range(3)]
    while len(names) % RING:
        names.append("pad")
    return names


RING = 4

PK = {}


def _pack_columns():
    at = 0
    for name, n in [("an", KT), ("fn", KT), ("qn", 1), ("kn12", 1), ("kn0", 1), ("on", 1), ("posk", 16),
                    ("posv", 16), ("lre", 8), ("lim", 8), ("ldt", 8), ("bre", 128), ("bim", 128), ("cre", 256),
                    ("cim", 256), ("dsk", 2), ("cw", 24), ("alog", 16), ("dtb", 16)]:
        PK[name] = (at, n)
        at += n
    return at


NPK = _pack_columns()
CK = {}


def _const_columns():
    at = 0
    for name, n in [("ident", P), ("ones", P), ("blk", P), ("le", P), ("ge", P), ("lt", P), ("negq", P),
                    ("negk", P), ("gt", P), ("lev", 7 * P), ("rot", P), ("freq", 1), ("cneg", NT * NCMP),
                    ("c01", NT * NCMP), ("t", S)]:
        CK[name] = (at, n)
        at += n
    return at


NCK = _const_columns()
NAMES = _slabs()
NSLAB = len(NAMES)
for _i, _n in enumerate(NAMES):
    SLAB.setdefault(_n, _i)


def program(nc, a_x, a_pos, a_const, a_pack, a_w, a_out):
    with ExitStack() as ctx:
        def sb(name, shape, dt=F32):
            return ctx.enter_context(nc.sbuf_tensor(name, shape, dt))

        sems = []

        def sem(name):
            s = ctx.enter_context(nc.semaphore(name))
            sems.append(s)
            return s

        PS = [ctx.enter_context(nc.psum_tensor(f"bank{i}", [P, 512], F32)) for i in range(8)]

        const = sb("const", [P, NCK])
        pack = sb("pack", [P, NPK])
        xT = sb("xT", [P, KT, S])
        hT = sb("hT", [P, KT, S])
        ring = sb("ring", [P, RING, KT, P])
        gate = sb("gate", [P, EARLY, S])
        pj = sb("pj", [P, NPJ, S])
        sbv = sb("sbv", [P, NT, 256])
        cosT = sb("cosT", [P, S])
        sinT = sb("sinT", [P, S])
        arena = sb("arena", [P, 12288])
        small = sb("small", [P, 632])
        negm16 = sb("negm16", [P, P], BF16)
        id16 = sb("id16", [P, P], BF16)
        kcv = sb("kcv", [P, 96])
        state = sb("state", [P, 2, HD])

        def cst(name):
            at, n = CK[name]
            return const[:, at:at + n]

        def prm(name):
            at, n = PK[name]
            return pack[:, at:at + n]

        ident, ones, blk = cst("ident"), cst("ones"), cst("blk")
        lev = cst("lev").rearrange("p (l c) -> p l c", l=7)

        s_const = ctx.enter_context(nc.semaphore("const_loaded"))
        s_rope = ctx.enter_context(nc.semaphore("rope_step"))
        s_rope_sin = ctx.enter_context(nc.semaphore("rope_sines"))
        s_x = ctx.enter_context(nc.semaphore("x_loaded"))

        with nc.Block() as block:
            @block.sync
            def _(sp):
                sp.dma_start(const[:, :], a_const).then_inc(s_const, 16)
                sp.dma_start(cosT[:, :].bitcast(I32), a_pos).then_inc(s_const, 16)
                sp.dma_start(xT[:, :, :], a_x).then_inc(s_x, 16)
                sp.wait_ge(s_x, 16)

            @block.vector
            def _(v):
                n = [0]

                def step(ins):
                    n[0] += 1
                    ins.then_inc(s_rope, 1)
                    v.wait_ge(s_rope, n[0])

                v.wait_ge(s_const, 32)
                ang, k, r = arena[:, 0:512], arena[:, 512:1024], arena[:, 1024:1536]
                step(v.tensor_copy(k, cosT[:, :].bitcast(I32)))
                step(v.tensor_scalar(ang, k, cst("freq"), None, ALU.mult))
                step(v.tensor_scalar(r, ang, INV_2PI, ROUND, ALU.mult, ALU.add))
                step(v.tensor_scalar(k, r, ROUND, None, ALU.subtract))
                for c in (C1, C2, C3):
                    step(v.scalar_tensor_tensor(ang, k, -c, ang, ALU.mult, ALU.add))
                step(v.tensor_scalar(ang, ang, -3.1415925, 3.1415925, ALU.max, ALU.min))
                step(v.scalar_tensor_tensor(k, ang, -1.0, ang, ALU.mult, ALU.max))
                step(v.tensor_copy(negm16[:, :], cst("negq")))
                step(v.tensor_copy(id16[:, :], ident))

            @block.scalar
            def _(a):
                a.wait_ge(s_rope, 9)
                a.activation(sinT[:, :], arena[:, 0:512], ACT.Sin).then_inc(s_rope_sin, 1)
                a.activation(cosT[:, :], arena[:, 512:1024], ACT.Sin, bias=TWO_PI / 4, scale=-1.0).then_inc(s_rope_sin, 1)

        slab_loaded = [sem(f"slab_loaded{i}") for i in range(RING)]
        q = {n: sem(n) for n in """
            pack_loaded slab_done proj_taken dve_step act_step pool_step
            bpad_ready bt_ps bt_taken abc_done trig_done
            sq_ready ss_ps rstd_ready h_ready
            blocks_ready cmp1_ps cmp_hid cmp2_ps kc_sq kcss_ps kc_rstd kc_ready
            sig_exp sig_ready xa_neg xa_ln alog_exp g_ready gsum_ps gsum_taken gdec_ready gexp_ready
            conv_ready tanh_ready silu_ready sqk_ready qkss_ps qk_rstd qk_ready
            grow_ps args_ready grow_exp qd_ready tr_ps tr_taken dexp_ready dmask_ready
            skk_ps l_part l_ready skq_ps at_part at_ready y0_ps u0_ready t0_ps t0_ready
            y_ps y_ready du_ps u_ready dt_ps t_ready wt_ps wt_ready
            vn_ps vn_ready o_ps o_taken su_ps st_ready
            osq_ready oss_ps o_rstd z_tanh gdn_done
            tab_ready sin_ready bu_ps m_ready w_ready z_ready n_ready x_ready y5_ps y5_ready y5_sq y5_poly y5_tanh
            gy_ready glu_ps glu_tanh s5_done
            sbz_ps z_copied nb_ready sp_exp sp_ln sp_ready sp_masked cum_ps d_ready d_masked wexp_ready sbpv_ps sb_done
            qsq_ready qss_ps q_rstd qn_ready rot_ps t_sin t_cos rot_ready kdup_ready vt_ps vt_ready
            sc_cmp_ps cmp_arg cmp_exp pc_ready pct_ps pct_ready
            sc_ps nm_ready p_ready pt_ps pt_ready pv_ps onat_ready ot_ps nsa_done
            gate_tanh br_ps br_taken g3_tanh merged_part merged_ready
            xo_ready sq2_ready ss2_ps rstd2_ready h2_ready
            fg_tanh ga_ready hid_ready dn_taken""".split()}

        pjt = {n: pj[:, TI[n], :] for n in KEPT}
        gflat = gate[:, :, :].rearrange("p g s -> p (g s)")
        t2k, t2v = gate[:, 20, :], gate[:, 21, :]
        bk = gate[:, 22, 0:496].rearrange("p (b n) -> p b n", b=16)
        bv = gate[:, 23, 0:496].rearrange("p (b n) -> p b n", b=16)
        aT = gflat[:, 8192:10240].rearrange("p (u c) -> p u c", u=16)
        bt = gate[:, 15, :].rearrange("p (r t s) -> p r t s", r=2, t=2)

        def scol(at, n):
            return small[:, at:at + n]

        sm_all = scol(0, 80).rearrange("p (t c) -> p t c", c=20)
        e_sig = scol(80, 64).rearrange("p (t c) -> p t c", c=16)
        sig = scol(144, 64).rearrange("p (t c) -> p t c", c=16)
        xa, na, ea, g16, gc, gl, egc, egl, kdc, bg, la = (scol(208 + 16 * i, 16) for i in range(11))
        s5c = [scol(384 + 8 * i, 8) for i in range(24)]

        def unit(tt, h):
            return (tt // 2) * 8 + (h % 2) * 4 + (tt % 2) * 2 + h // 2

        UNITS = [(tt, h) for b in range(4) for tt in (2 * (b // 2), 2 * (b // 2) + 1) for h in (b % 2, b % 2 + 2)]
        mats = [arena[:, 2048 * i:2048 * (i + 1)].rearrange("p (u c) -> p u c", u=16) for i in range(4)]
        mL, mU, mT, mY = mats
        cv = arena[:, 8192:11264].rearrange("p (t s) -> p t s", t=6)
        qd = arena[:, 11264:12288].rearrange("p (t s) -> p t s", t=2)
        kbg, vb, kdec = (pj[:, 2 * i:2 * i + 2, :].rearrange("p a (t c) -> p (a t) c", t=2) for i in range(3))
        vn = arena[:, 4096:4352].rearrange("p (h e) -> p h e", h=4)
        wt = arena[:, 4608:5632].rearrange("p (t i c) -> p t i c", t=4, i=2)
        o_raw = arena[:, 0:1024].rearrange("p (i s) -> p i s", i=2)
        o_sq = arena[:, 1024:2048].rearrange("p (i s) -> p i s", i=2)
        o_rs = arena[:, 2048:3072].rearrange("p (i s) -> p i s", i=2)
        z_th = arena[:, 3072:4096].rearrange("p (i s) -> p i s", i=2)
        gdn_out = pj[:, TI["z0"]:TI["z0"] + 2, :]
        s5_out = pj[:, TI["u0"]:TI["u0"] + 2, :]
        sb_out = pj[:, TI["sb0"]:TI["sb0"] + 2, :]
        nsa_out = pj[:, TI["q0"]:TI["q0"] + 2, :]
        mixed = [nsa_out, s5_out, gdn_out, sb_out]

        def half(h):
            return slice(HD * (h % 2), HD * (h % 2) + HD)
        (dt5, theta, lrdt, tmp1, thr, thabs, uh, ul, den, mag, sina, cosa, abr, abi, tmp2, fre, fim) = s5c[:17]
        q8 = scol(384 + 8 * 17, 1)
        nm, nsum, nfac, nc1 = scol(544, 32), scol(576, 32), scol(608, 8), scol(616, 16)
        GC0 = 272
        mL_flat, mU_flat, mT_flat, mY_flat = (arena[:, 2048 * i:2048 * (i + 1)] for i in range(4))
        aT_flat = gflat[:, 8192:10240]
        rs1 = arena[:, 1024:1536]
        th = arena[:, 0:3072].rearrange("p (t s) -> p t s", t=6)
        sqk = mT_flat.rearrange("p (t s) -> p t s", t=4)
        rqk = mY_flat.rearrange("p (t s) -> p t s", t=4)
        cx, ct, cmp_flat = gate[:, 20, 0:124], gate[:, 20, 128:252], gate[:, 20, 256:380]
        cmp_h = cmp_flat.rearrange("p (c n) -> p c n", c=4)
        kc_s, kc_r = gate[:, 20, 384:415], gate[:, 20, 416:447]
        kcT, vc = kcv[:, 0:NCMP], kcv[:, 32:96]

        def tiles(at, n):
            return arena[:, at:at + S * n].rearrange("p (t s) -> p t s", t=n)

        def s5_buf(i, j):
            return arena[:, 4096 * (i % 2) + S * j:4096 * (i % 2) + S * j + S]

        y5a, y5b, gy = tiles(8192, 2), tiles(9216, 2), tiles(10240, 2)

        def sb_z(h, kb):
            return arena[:, 2048 * (h % 2) + S * kb:2048 * (h % 2) + S * kb + S]

        def sb_sp(h, kb):
            return arena[:, 4096 + 2048 * (h % 2) + S * kb:4096 + 2048 * (h % 2) + S * kb + S]

        def sb_e(n):
            return arena[:, 8192 + S * (n % 2):8192 + S * (n % 2) + S]

        nqn, nqr, nsq, nrs, kdup = tiles(0, 3), tiles(1536, 3), tiles(3072, 3), tiles(4608, 3), tiles(6144, 2)
        nts = nsq
        nP, npt = tiles(7168, 4), tiles(9216, 4)
        nvt = arena[:, 11264:11776].rearrange("p (t c) -> p t c", t=4)
        npc_flat = arena[:, 4608:5104]
        npc = npc_flat.rearrange("p (u n) -> p u n", u=16)
        npct = arena[:, 5120:5632]
        nO, nO2 = arena[:, 5632:5888], arena[:, 5888:6144]
        PTN = [sum(m // 2 + 1 for m in range(k)) for k in range(2 * NT + 1)]
        merged = tiles(0, 8)
        mtmp = arena[:, 4096:7168].rearrange("p (a m s) -> p a m s", a=2, m=3)
        g3, ft, fa = tiles(7168, 2), tiles(8192, 2), tiles(9216, 2)
        rs2 = arena[:, 10240:10752]

        with nc.Fori(0, DEPTH) as layer:
            with nc.Block() as block:

                @block.sync
                def _(sp):
                    sp.dma_start(pack[:, :], a_pack[layer]).then_inc(q["pack_loaded"], 16)
                    for s in range(RING):
                        sp.dma_start(ring[:, s], a_w[layer, s].rearrange("p (k c) -> p k c", k=KT)).then_inc(slab_loaded[s], 16)
                    with sp.Fori(1, NSLAB // RING) as r:
                        for s in range(RING):
                            sp.wait_ge(q["slab_done"], r * RING + (s + 1 - RING))
                            sp.dma_start(ring[:, s], a_w[layer, r * RING + s].rearrange("p (k c) -> p k c", k=KT))\
                              .then_inc(slab_loaded[s], 16)
                    for s in range(RING):
                        sp.wait_ge(slab_loaded[s], 16 * (NSLAB // RING))

                @block.tensor
                def _(pe):
                    mm = nc.tensor.matmul
                    used = [0]

                    def slab(name):
                        i = SLAB[name]
                        assert i == used[0], (name, i, used[0])
                        used[0] += 1
                        pe.wait_ge(slab_loaded[i % RING], 16 * (i // RING + 1))
                        return ring[:, i % RING]

                    turn = [0]

                    def stream_bank():
                        n = turn[0]
                        turn[0] += 1
                        if n >= 2:
                            pe.wait_ge(q["proj_taken"], n - 1)
                        return PS[n % 2]

                    def column_tile(name):
                        w = slab(name)
                        b = stream_bank()
                        for k in range(KT):
                            last = mm(b[:, :], w[:, k, :], hT[:, k, :], start=(k == 0), stop=(k == KT - 1))
                        last.then_inc(q["slab_done"], 1)

                    gates_made = [0]

                    def fill(n):
                        for _ in range(n):
                            column_tile(f"gate{gates_made[0]}")
                            gates_made[0] += 1

                    pe.wait_ge(q["bpad_ready"], 1)
                    for r in range(2):
                        for t in range(2):
                            last = nc.tensor.transpose(PS[7][:, (2 * r + t) * P:(2 * r + t + 1) * P],
                                                       arena[:, 256 * r + P * t:256 * r + P * t + P], ident)
                    last.then_inc(q["bt_ps"], 1)
                    for k in range(KT):
                        pe.wait_ge(q["sq_ready"], k + 1)
                        last = mm(PS[6][:, :], ones, hT[:, k, :], start=(k == 0), stop=(k == KT - 1))
                    last.then_inc(q["ss_ps"], 1)
                    pe.wait_ge(q["h_ready"], KT)
                    w = slab("small")
                    b = stream_bank()
                    w20 = w.rearrange("p k c -> p (k c)")[:, 0:KT * 20].rearrange("p (k c) -> p k c", k=KT)
                    for t in range(NT):
                        for k in range(KT):
                            last = mm(b[:, 20 * t:20 * t + 20], hT[:, k, P * t:P * t + P], w20[:, k, :],
                                      start=(k == 0), stop=(k == KT - 1))
                    last.then_inc(q["slab_done"], 1)
                    for name, _ in TILES:
                        column_tile(name)
                    wv = [slab("sbv0"), slab("sbv1")]
                    wv = [x.rearrange("p k c -> p (k c)").rearrange("p (k c) -> p k c", k=4) for x in wv]
                    for tp in range(2):
                        b = stream_bank()
                        for t in range(2):
                            for k in range(KT):
                                last = mm(b[:, 256 * t:256 * t + 256], hT[:, k, P * (2 * tp + t):P * (2 * tp + t) + P],
                                          wv[k // 4][:, k % 4, :], start=(k == 0), stop=(k == KT - 1))
                                if tp == 1 and t == 1 and k == 3:
                                    last.then_inc(q["slab_done"], 1)
                    last.then_inc(q["slab_done"], 1)

                    pe.wait_ge(q["blocks_ready"], 4)
                    pe.wait_ge(q["bt_taken"], 1)
                    for kv, blocks in enumerate((bk, bv)):
                        ws = []
                        for i in range(4):
                            w = slab(f"c{'kv'[kv]}{i}")
                            ws.append(w.rearrange("p k c -> p (k c)").rearrange("p (k c) -> p k c", k=4))
                        for hc in range(2):
                            for i in range(16):
                                last = mm(PS[7][:, 31 * (2 * kv + hc):31 * (2 * kv + hc + 1)],
                                          ws[i // 4][:, i % 4, P * hc:P * hc + P], blocks[:, i, :],
                                          start=(i == 0), stop=(i == 15))
                                if hc == 1 and i % 4 == 3:
                                    last.then_inc(q["slab_done"], 1)
                    w = slab("cw2").rearrange("p k c -> p (k c)")
                    pe.wait_ge(q["cmp_hid"], 1)
                    for hc in range(2):
                        mm(PS[7][:, 128:159], w[:, P * hc:P * hc + P], cmp_h[:, hc, :], start=(hc == 0), stop=(hc == 1))
                    for hc in range(2):
                        last = mm(PS[7][0:31, 192:256], cmp_h[:, 2 + hc, :], w[:, 256 + HD * hc:256 + HD * hc + HD],
                                  start=(hc == 0), stop=(hc == 1))
                    last.then_inc(q["slab_done"], 1)
                    pe.wait_ge(q["kc_sq"], 1)
                    mm(PS[7][:, 320:351], blk, kc_s, start=True, stop=True).then_inc(q["kcss_ps"], 1)

                    fill(1)
                    pe.wait_ge(q["g_ready"], 1)
                    mm(PS[2][:, 0:16], cst("le"), g16, start=True, stop=True)
                    mm(PS[2][:, 16:32], ones, g16, start=True, stop=True).then_inc(q["gsum_ps"], 1)
                    for i in range(4):
                        pe.wait_ge(q["sqk_ready"], i + 1)
                        if i == 3:
                            pe.wait_ge(q["rstd_ready"], 1)
                        mm(PS[3 + i][:, :], blk, mT_flat[:, S * i:S * i + S], start=True, stop=True).then_inc(q["qkss_ps"], 1)
                    fill(2)
                    for b in range(4):
                        pe.wait_ge(q["qk_rstd"], b + 1)
                        for j, (tt, h) in enumerate(UNITS[4 * b:4 * b + 4]):
                            last = mm(PS[3 + b][:, P * j:P * j + P], g16[:, 4 * tt + h:4 * tt + h + 1].broadcast_to([P, P]),
                                      cst("le"), start=True, stop=True)
                        last.then_inc(q["grow_ps"], 1)
                    fill(2)
                    pe.wait_ge(q["qk_ready"], 4)
                    for b in range(4):
                        pe.wait_ge(q["grow_exp"], b + 1)
                        for t in range(2):
                            for i in range(2):
                                tt = 2 * (b % 2) + t
                                last = nc.tensor.transpose(PS[3 + b][:, 256 * t + P * i:256 * t + P * i + P],
                                                           cv[:, 2 + 2 * (b // 2) + i, P * tt:P * tt + P], ident)
                        last.then_inc(q["tr_ps"], 1)
                    fill(1)
                    for other, done in ((2, "skk_ps"), (0, "skq_ps")):
                        for b in range(4):
                            if other == 2:
                                pe.wait_ge(q["tr_taken"], [1, 2, 3, 4][b])
                            else:
                                pe.wait_ge(q["l_part"], b + 1)
                            for j, (tt, h) in enumerate(UNITS[4 * b:4 * b + 4]):
                                last = mm(PS[3 + b][:, P * j:P * j + P], cv[half(h), 2 + h // 2, P * tt:P * tt + P],
                                          cv[half(h), other + h // 2, P * tt:P * tt + P], start=True, stop=True)
                            last.then_inc(q[done], 1)
                    fill(1)
                    for b in range(4):
                        pe.wait_ge(q["at_part"], b + 1)
                        for j in range(4):
                            last = nc.tensor.transpose(PS[3 + b][:, P * j:P * j + P], mL[:, 4 * b + j, :], ident)
                        last.then_inc(q["y0_ps"], 1)
                    for b in range(4):
                        pe.wait_ge(q["u0_ready"], 2 * b + 2)
                        for j in range(4):
                            last = nc.tensor.transpose(PS[3 + b][:, P * j:P * j + P], mY[:, 4 * b + j, :], ident)
                        last.then_inc(q["t0_ps"], 1)

                    def y_product(n):
                        b = n % 4
                        if n >= 4:
                            pe.wait_ge(q["u_ready"], n - 3)
                        else:
                            pe.wait_ge(q["t0_ready"], 4)
                        if n >= 2:
                            pe.wait_ge(q["y_ready"], n - 1)
                        for j in range(4):
                            last = mm(PS[2 + n % 2][:, P * j:P * j + P], mL[:, 4 * b + j, :], mU[:, 4 * b + j, :],
                                      start=True, stop=True)
                        last.then_inc(q["y_ps"], 1)

                    def ut_product(n):
                        b = n % 4
                        pe.wait_ge(q["y_ready"], n + 1)
                        if n >= 4:
                            pe.wait_ge(q["t_ready"], n - 3)
                        if n >= 2:
                            pe.wait_ge(q["u_ready"], n - 1)
                        for j in range(4):
                            last = mm(PS[4 + n % 2][:, P * j:P * j + P], mT[:, 4 * b + j, :], mY[:, 4 * b + j, :],
                                      start=True, stop=True)
                        last.then_inc(q["du_ps"], 1)
                        if n < 20:
                            if n >= 2:
                                pe.wait_ge(q["t_ready"], n - 1)
                            for j in range(4):
                                last = mm(PS[6 + n % 2][:, P * j:P * j + P], mY[:, 4 * b + j, :], mT[:, 4 * b + j, :],
                                          start=True, stop=True)
                            last.then_inc(q["dt_ps"], 1)

                    pe.wait_ge(q["kc_ready"], 1)
                    for lv in range(6):
                        y_product(4 * lv)
                        y_product(4 * lv + 1)
                        ut_product(4 * lv)
                        y_product(4 * lv + 2)
                        ut_product(4 * lv + 1)
                        y_product(4 * lv + 3)
                        ut_product(4 * lv + 2)
                        ut_product(4 * lv + 3)
                        if lv in (0, 2):
                            fill(1)
                    pe.wait_ge(q["u_ready"], 24)
                    for tt in range(NT):
                        bank = PS[2 + tt]
                        for h in range(H):
                            last = mm(bank[half(h), P * (h // 2):P * (h // 2) + P], kbg[:, tt, HD * h:HD * h + HD],
                                      mU[:, unit(tt, h), :], start=True, stop=True)
                        last.then_inc(q["wt_ps"], 1)
                    pe.wait_ge(q["wt_ready"], NT)
                    for tt in range(NT):
                        if tt:
                            pe.wait_ge(q["st_ready"], 4 * tt + 1)
                            pe.wait_ge(q["vn_ready"], 2 * tt)
                            pe.wait_ge(q["o_taken"], 2 * tt)
                        else:
                            pe.wait_ge(q["st_ready"], 1)
                        for h in range(H):
                            out = PS[2 + h % 2][:, HD * (h // 2):HD * (h // 2) + HD]
                            mm(out, mU[:, unit(tt, h), :], vb[:, tt, HD * h:HD * h + HD], start=True, stop=False)
                            last = mm(out, wt[half(h), tt, h // 2, :], state[half(h), h // 2, :], start=False, stop=True)
                        last.then_inc(q["vn_ps"], 1)
                        if tt == 0:
                            pe.wait_ge(q["qd_ready"], 8)
                        pe.wait_ge(q["vn_ready"], 2 * tt + 2)
                        for h in range(H):
                            out = PS[6 + h % 2][half(h), P * (h // 2):P * (h // 2) + P]
                            mm(out, state[half(h), h // 2, :], qd[half(h), h // 2, P * tt:P * tt + P], start=True, stop=False)
                            last = mm(out, vn[:, h, :], aT[:, unit(tt, h), :], start=False, stop=True)
                        last.then_inc(q["o_ps"], 1)
                        for h in range(H):
                            out = PS[4 + h % 2][half(h), HD * (h // 2):HD * (h // 2) + HD]
                            last = mm(out, kdec[:, tt, HD * h:HD * h + HD], vn[:, h, :], start=True, stop=True)
                        last.then_inc(q["su_ps"], 1)
                        fill(1)
                    for i in range(2):
                        pe.wait_ge(q["osq_ready"], i + 1)
                        mm(PS[2 + i][:, :], blk, o_sq[:, i, :], start=True, stop=True).then_inc(q["oss_ps"], 1)
                    fill(1)

                    pe.wait_ge(q["o_rstd"], 2)
                    pe.wait_ge(q["st_ready"], 17)
                    for i in range(9):
                        if i < 8:
                            if i >= 2:
                                pe.wait_ge(q["m_ready"], i - 1)
                            j = 32 * (i % 4)
                            for r in range(2):
                                last = mm(PS[2 + 2 * (i % 2) + r][:, :], bt[j:j + 32, r, i // 4, :],
                                          pj[j:j + 32, TI["u0"] + i // 4, :], start=True, stop=True)
                            last.then_inc(q["bu_ps"], 1)
                            if i == 1:
                                pe.wait_ge(q["o_taken"], 8)
                            if i < 1:
                                fill(1)
                        if i >= 1:
                            k = i - 1
                            pe.wait_ge(q["x_ready"], 2 * k + 2)
                            out = PS[6 + k // 4][32 * (k % 4):32 * (k % 4) + 32, :]
                            mm(out, prm("cre")[:, 32 * k:32 * k + 32], s5_buf(k, 2), start=True, stop=False)
                            mm(out, prm("cim")[:, 32 * k:32 * k + 32], s5_buf(k, 4), start=False, stop=True)\
                                .then_inc(q["y5_ps"], 1)
                    pe.wait_ge(q["gy_ready"], 2)
                    assert gates_made[0] <= 15
                    fill(3)
                    w = slab("glu").rearrange("p k c -> p (k c)").rearrange("p (k c) -> p k c", k=2)
                    for m in range(4):
                        for k in range(2):
                            last = mm(PS[2 + m][:, :], w[:, k, P * m:P * m + P], gy[:, k, :], start=(k == 0), stop=(k == 1))
                    last.then_inc(q["slab_done"], 1)

                    pe.wait_ge(q["s5_done"], 2)

                    def sb_scores(n):
                        h, kb = n // 4, 3 - n % 4
                        if n >= 2:
                            pe.wait_ge(q["z_copied"], n - 1)
                        i = h // 2
                        mm(PS[2 + n % 2][:, 0:S - P * kb], pjt[f"sb{2 + i}"][half(h), P * kb:P * kb + P],
                           pjt[f"sb{i}"][half(h), P * kb:S], start=True, stop=True).then_inc(q["sbz_ps"], 1)

                    def sb_sums(n):
                        h, kb = n // 4, 3 - n % 4
                        pe.wait_ge(q["sp_masked"], n + 1)
                        if n >= 2:
                            pe.wait_ge(q["d_ready"], n - 1)
                        out = PS[4 + n % 2]
                        for j in range(kb, NT):
                            last = mm(out[:, P * (j - kb):S - P * kb], cst("ge") if j == kb else ones,
                                      sb_sp(h, j)[:, P * j:S], start=(j == kb), stop=(j == NT - 1), skip_group_check=True)
                        last.then_inc(q["cum_ps"], 1)

                    def sb_values(h):
                        pe.wait_ge(q["wexp_ready"], 4 * h + 4)
                        if h >= 2:
                            pe.wait_ge(q["sb_done"], h - 1)
                        for kb in range(NT):
                            last = mm(PS[6 + h % 2][half(h), P * kb:S], sbv[:, kb, HD * h:HD * h + HD],
                                      sb_z(h, kb)[:, P * kb:S], start=(kb == 0), stop=(kb == NT - 1), skip_group_check=True)
                        last.then_inc(q["sbpv_ps"], 1)

                    for n in range(16 + 2):
                        if n < 16:
                            sb_scores(n)
                        if n >= 2:
                            sb_sums(n - 2)
                        if n in (3, 8, 12):
                            fill(1)
                        if n >= 5 and n % 4 == 1:
                            if n >= 9:
                                sb_values(n // 4 - 2)
                    fill(1)
                    sb_values(3)

                    for i in range(3):
                        pe.wait_ge(q["qsq_ready"], i + 1)
                        mm(PS[2 + i][:, :], blk, nsq[:, i, :], start=True, stop=True).then_inc(q["qss_ps"], 1)
                    for t in range(NT):
                        last = nc.tensor.transpose(PS[5][:, P * t:P * t + P], pjt["vsvw"][:, P * t:P * t + P], ident)
                    last.then_inc(q["vt_ps"], 1)
                    for i in range(3):
                        pe.wait_ge(q["qn_ready"], i + 1)
                        mm(PS[2 + i][:, :], cst("rot"), nqn[:, i, :], start=True, stop=True).then_inc(q["rot_ps"], 1)
                    for par in range(2):
                        for tt in range(NT):
                            for i in range(2):
                                c = NCMP * (2 * tt + i)
                                last = mm(PS[6 + par][:, c:c + NCMP], nqn[HD * par:HD * par + HD, i, P * tt:P * tt + P],
                                          kcT[HD * par:HD * par + HD, :], start=True, stop=True)
                        last.then_inc(q["sc_cmp_ps"], 1)
                    fill(2)
                    pe.wait_ge(q["kdup_ready"], 2)
                    pe.wait_ge(q["rot_ready"], 4)
                    pe.wait_ge(q["vt_ready"], 1)
                    pe.wait_ge(q["t_sin"], 3)
                    pe.wait_ge(q["pc_ready"], 1)

                    def nsa_transpose(m):
                        qt = m // 2
                        pe.wait_ge(q["p_ready"], 4 * m + 4)
                        for kb in range(qt + 1):
                            x = PTN[m] + kb
                            if x >= 2:
                                pe.wait_ge(q["pt_ready"], x - 1)
                            for h in range(H):
                                last = nc.tensor.transpose(PS[4 + x % 2][:, P * h:P * h + P], nP[:, h, P * kb:P * kb + P], ident)
                            last.then_inc(q["pt_ps"], 1)

                    for m in range(2 * NT):
                        qt, br = m // 2, m % 2
                        wid = P * (qt + 1)
                        for h in range(H):
                            x = 4 * m + h
                            if x >= 2:
                                pe.wait_ge(q["p_ready"], x - 1)
                            out = PS[2 + h % 2]
                            mm(out[:, 0:wid], nqr[half(h), h // 2, P * qt:P * qt + P], kdup[half(h), br, 0:wid],
                               start=True, stop=False, skip_group_check=True)
                            mm(out[:, wid - P:wid], id16[:, :], negm16[:, :], start=False, stop=True,
                               skip_group_check=True).then_inc(q["sc_ps"], 1)
                        if br == 0:
                            if qt:
                                pe.wait_ge(q["onat_ready"], qt)
                            for h in range(H):
                                u = 8 * (h % 2) + 2 * qt + h // 2
                                last = nc.tensor.transpose(PS[7][0:NCMP, P * h:P * h + P], npc[:, u, :], ident)
                            last.then_inc(q["pct_ps"], 1)
                            pe.wait_ge(q["pct_ready"], qt + 1)
                            for h in range(H):
                                last = mm(PS[6][:, 256 + HD * h:256 + HD * h + HD], npct[0:NCMP, P * h:P * h + P],
                                          vc[0:NCMP, :], start=True, stop=True)
                        nsa_transpose(m)
                        pe.wait_ge(q["pt_ready"], PTN[m] + qt + 1)
                        for h in range(H):
                            for kb in range(qt + 1):
                                last = mm(PS[6 + br][:, HD * h:HD * h + HD], npt[:, kb, P * h:P * h + P],
                                          nvt[:, kb, HD * br:HD * br + HD], start=(kb == 0), stop=(kb == qt))
                        last.then_inc(q["pv_ps"], 1)
                        if br == 1:
                            pe.wait_ge(q["onat_ready"], qt + 1)
                            for i in range(2):
                                last = nc.tensor.transpose(PS[6][:, P * i:P * i + P], nO[:, P * i:P * i + P], ident)
                            last.then_inc(q["ot_ps"], 1)
                            pe.wait_ge(q["nsa_done"], qt + 1)
                    assert gates_made[0] == EARLY, gates_made

                    for dt in range(KT):
                        w = slab(f"br{dt}").rearrange("p (m k) c -> p m k c", m=4)
                        for m in range(4):
                            x = 4 * dt + m
                            if x >= 4:
                                pe.wait_ge(q["br_taken"], x - 3)
                            for k in range(2):
                                last = mm(PS[2 + m][:, :], w[:, m, k, :], mixed[m][:, k, :], start=(k == 0), stop=(k == 1))
                            last.then_inc(q["slab_done"] if m == 3 else q["br_ps"], 1)
                        column_tile(f"gate{EARLY + dt}")
                    pe.wait_ge(q["merged_ready"], KT)
                    for dt in range(KT):
                        w = slab(f"out{dt}")
                        b = PS[4 + dt % 4]
                        if dt >= 4:
                            pe.wait_ge(q["xo_ready"], dt - 3)
                        for k in range(KT):
                            last = mm(b[:, :], w[:, k, :], merged[:, k, :], start=(k == 0), stop=(k == KT - 1))
                        last.then_inc(q["slab_done"], 1)
                    for k in range(KT):
                        pe.wait_ge(q["sq2_ready"], k + 1)
                        last = mm(PS[2][:, :], ones, hT[:, k, :], start=(k == 0), stop=(k == KT - 1))
                    last.then_inc(q["ss2_ps"], 1)
                    pe.wait_ge(q["h2_ready"], KT)
                    for f in range(FT):
                        for j, name in enumerate(("fg", "fu")):
                            w = slab(f"{name}{f}")
                            b = PS[2 * (f % 4) + j]
                            if f >= 4:
                                pe.wait_ge(q["hid_ready"], f - 3)
                            for k in range(KT):
                                last = mm(b[:, :], w[:, k, :], hT[:, k, :], start=(k == 0), stop=(k == KT - 1))
                            last.then_inc(q["slab_done"], 1)
                    pe.wait_ge(q["hid_ready"], FT)
                    for dt in range(KT):
                        b = PS[dt % 4]
                        if dt >= 4:
                            pe.wait_ge(q["dn_taken"], dt - 3)
                        for j in range(3):
                            w = slab(f"dn{dt}_{j}")
                            n = min(KT, FT - KT * j)
                            for k in range(n):
                                last = mm(b[:, :], w[:, k, :], gate[:, KT * j + k, :], start=(j == 0 and k == 0),
                                          stop=(j == 2 and k == n - 1))
                            last.then_inc(q["slab_done"], 1)
                    for n in NAMES[used[0]:]:
                        assert n == "pad"
                        pe.sem_inc(q["slab_done"], 1)

                @block.scalar
                def _(a):
                    act = nc.scalar.activation
                    chain = [0]

                    def step(ins):
                        chain[0] += 1
                        ins.then_inc(q["act_step"], 1)
                        a.wait_ge(q["act_step"], chain[0])

                    turn = [0]

                    def stream(name):
                        n = turn[0]
                        turn[0] += 1
                        a.wait_ge(q["slab_done"], SLAB[name] + 1)
                        return PS[n % 2]

                    gates_made = [0]

                    def fill(n):
                        for _ in range(n):
                            g = gates_made[0]
                            gates_made[0] += 1
                            act(gate[:, g, :], stream(f"gate{g}")[:, :], ACT.Copy).then_inc(q["proj_taken"], 1)

                    def rsqrt(out, src, count, done):
                        step(act(out, src, ACT.Ln, bias=EPS, scale=1.0 / count))
                        act(out, out, ACT.Exp, scale=-0.5).then_inc(done, 1)

                    a.wait_ge(q["pack_loaded"], 16)
                    act(dt5, prm("ldt"), ACT.Exp).then_inc(q["trig_done"], 1)
                    for k in range(KT):
                        act(hT[:, k, :], xT[:, k, :], ACT.Square).then_inc(q["sq_ready"], 1)
                    a.wait_ge(q["abc_done"], 1)
                    act(mag, lrdt, ACT.Exp).then_inc(q["trig_done"], 1)
                    act(sina, thr, ACT.Sin).then_inc(q["trig_done"], 1)
                    act(cosa, thabs, ACT.Sin, bias=TWO_PI / 4, scale=-1.0).then_inc(q["trig_done"], 1)
                    a.wait_ge(q["ss_ps"], 1)
                    rsqrt(rs1, PS[6][:, :], D, q["rstd_ready"])
                    act(small[:, 0:80], stream("small")[:, 0:80], ACT.Copy).then_inc(q["proj_taken"], 1)
                    for i, (name, _) in enumerate(TILES):
                        b = stream(name)
                        if name == "kcvc":
                            act(t2k[0:HD, :], b[0:HD, :], ACT.Copy)
                            act(t2k[HD:P, 0:S - 1], b[0:HD, 1:S], ACT.Copy)
                            act(t2v[0:HD, :], b[HD:P, :], ACT.Copy)
                            act(t2v[HD:P, 0:S - 1], b[HD:P, 1:S], ACT.Copy).then_inc(q["proj_taken"], 1)
                        else:
                            act(pjt[name], b[:, :], ACT.Copy, scale=0.125 if name in ("sb0", "sb1") else 1.0)\
                                .then_inc(q["proj_taken"], 1)
                        if i == 1:
                            act(e_sig, sm_all[:, :, 0:16], ACT.Exp, scale=-1.0).then_inc(q["sig_exp"], 1)
                            step(act(ea, prm("alog"), ACT.Exp))
                            a.wait_ge(q["xa_neg"], 1)
                            step(act(na, na, ACT.Exp))
                            act(la, na, ACT.Ln, bias=1.0).then_inc(q["xa_ln"], 1)
                        if i >= 10 and i < 16:
                            a.wait_ge(q["conv_ready"], i - 9)
                            act(th[:, i - 10, :], cv[:, i - 10, :], ACT.Tanh).then_inc(q["tanh_ready"], 1)
                    for tp in range(2):
                        act(sbv[:, 2 * tp:2 * tp + 2, :], stream("sbv1")[:, :].rearrange("p (t c) -> p t c", t=2), ACT.Copy)\
                            .then_inc(q["proj_taken"], 1)
                    for i in range(4):
                        a.wait_ge(q["silu_ready"], i + 1)
                        act(sqk[:, i, :], cv[:, i, :], ACT.Square).then_inc(q["sqk_ready"], 1)
                    a.wait_ge(q["slab_done"], SLAB["cv3"] + 1)
                    act(cx, PS[7][:, 0:124], ACT.Copy).then_inc(q["cmp1_ps"], 1)
                    a.wait_ge(q["cmp_arg"], 1)
                    act(ct, ct, ACT.Tanh, scale=GELU_C).then_inc(q["cmp_exp"], 1)
                    a.wait_ge(q["slab_done"], SLAB["cw2"] + 1)
                    step(act(kcT, PS[7][:, 128:159], ACT.Copy))
                    act(vc[0:NCMP, :], PS[7][0:NCMP, 192:256], ACT.Copy)
                    act(kc_s, kcT, ACT.Square).then_inc(q["kc_sq"], 1)
                    fill(1)
                    a.wait_ge(q["kcss_ps"], 1)
                    rsqrt(kc_r, PS[7][:, 320:351], HD, q["kc_rstd"])
                    for i in range(4):
                        a.wait_ge(q["qkss_ps"], i + 1)
                        step(act(rqk[:, i, :], PS[3 + i][:, :], ACT.Ln, bias=EPS))
                        act(rqk[:, i, :], rqk[:, i, :], ACT.Exp, scale=-0.5).then_inc(q["qk_rstd"], 1)
                    fill(2)
                    a.wait_ge(q["gsum_taken"], 1)
                    act(egc, gc, ACT.Exp)
                    act(egl, gl, ACT.Exp)
                    act(kdc, kdc, ACT.Exp).then_inc(q["gexp_ready"], 1)
                    for b in range(4):
                        a.wait_ge(q["args_ready"], b + 1)
                        act(mT_flat[:, S * b:S * b + S], PS[3 + b][:, :], ACT.Exp).then_inc(q["grow_exp"], 1)
                        act(mL_flat[:, S * b:S * b + S], mL_flat[:, S * b:S * b + S], ACT.Exp, scale=-1.0)\
                            .then_inc(q["dexp_ready"], 1)
                        act(mY_flat[:, S * b:S * b + S], mY_flat[:, S * b:S * b + S], ACT.Exp).then_inc(q["dexp_ready"], 1)
                    fill(2)
                    fill(1)
                    fill(1)
                    fill(2)
                    for tt in range(NT):
                        a.wait_ge(q["wt_ps"], tt + 1)
                        act(wt[:, tt], PS[2 + tt][:, 0:256].rearrange("p (i c) -> p i c", i=2), ACT.Copy, scale=-1.0)\
                            .then_inc(q["wt_ready"], 1)
                    for tt in range(NT):
                        a.wait_ge(q["o_ps"], tt + 1)
                        for par in range(2):
                            act(o_raw[HD * par:HD * par + HD, :, P * tt:P * tt + P],
                                PS[6 + par][HD * par:HD * par + HD, 0:256].rearrange("p (i c) -> p i c", i=2), ACT.Copy)\
                                .then_inc(q["o_taken"], 1)
                        fill(1)
                    a.wait_ge(q["o_taken"], 8)
                    for i in range(2):
                        act(o_sq[:, i, :], o_raw[:, i, :], ACT.Square).then_inc(q["osq_ready"], 1)
                    for i in range(2):
                        act(z_th[:, i, :], pjt[f"z{i}"], ACT.Tanh, scale=0.5).then_inc(q["z_tanh"], 1)
                    for i in range(2):
                        a.wait_ge(q["oss_ps"], i + 1)
                        rsqrt(o_rs[:, i, :], PS[2 + i][:, :], HD, q["o_rstd"])
                    fill(1)
                    for i in range(8):
                        a.wait_ge(q["tab_ready"], 2 * i + 2)
                        act(s5_buf(i, 1), s5_buf(i, 6), ACT.Sin, scale=SIN_SCALE).then_inc(q["sin_ready"], 1)
                        act(s5_buf(i, 0), s5_buf(i, 7), ACT.Sin, scale=-SIN_SCALE, bias=TWO_PI / 4).then_inc(q["sin_ready"], 1)
                        if i < 1:
                            fill(1)
                    for i in range(2):
                        a.wait_ge(q["y5_ready"], i + 1)
                        act(y5b[:, i, :], y5a[:, i, :], ACT.Square).then_inc(q["y5_sq"], 1)
                    for i in range(2):
                        a.wait_ge(q["y5_poly"], i + 1)
                        act(y5b[:, i, :], y5b[:, i, :], ACT.Tanh, scale=GELU_C).then_inc(q["y5_tanh"], 1)
                    fill(3)
                    a.wait_ge(q["slab_done"], SLAB["glu"] + 1)
                    for i in range(2):
                        act(y5b[:, i, :], PS[4 + i][:, :], ACT.Tanh, scale=0.25).then_inc(q["glu_tanh"], 1)
                    def sb_first(n):
                        h, kb = n // 4, 3 - n % 4
                        r = slice(P * kb, S)
                        a.wait_ge(q["sbz_ps"], n + 1)
                        if h >= 2:
                            a.wait_ge(q["sbpv_ps"], h - 1)
                        act(sb_z(h, kb)[:, r], PS[2 + n % 2][:, 0:S - P * kb], ACT.Copy).then_inc(q["z_copied"], 1)
                        a.wait_ge(q["nb_ready"], n + 1)
                        step(act(sb_e(n)[:, r], sb_e(n)[:, r], ACT.Exp))
                        act(sb_e(n)[:, r], sb_e(n)[:, r], ACT.Ln, bias=1.0).then_inc(q["sp_ln"], 1)

                    def sb_last(n):
                        h, kb = n // 4, 3 - n % 4
                        r = slice(P * kb, S)
                        a.wait_ge(q["d_masked"], n + 1)
                        act(sb_z(h, kb)[:, r], sb_z(h, kb)[:, r], ACT.Exp).then_inc(q["wexp_ready"], 1)

                    for n in range(16 + 2):
                        if n < 16:
                            sb_first(n)
                        if n >= 2:
                            sb_last(n - 2)
                        if n in (3, 8, 12):
                            fill(1)
                    fill(1)
                    a.wait_ge(q["sbpv_ps"], 4)
                    for i in range(3):
                        act(nsq[:, i, :], pjt[("q0", "q1", "kskw")[i]], ACT.Square).then_inc(q["qsq_ready"], 1)
                    for i in range(3):
                        a.wait_ge(q["qss_ps"], i + 1)
                        rsqrt(nrs[:, i, :], PS[2 + i][:, :], HD, q["q_rstd"])
                    a.wait_ge(q["vt_ps"], 1)
                    act(nvt[:, :, :], PS[5][:, :].rearrange("p (t c) -> p t c", t=4), ACT.Copy).then_inc(q["vt_ready"], 1)
                    fill(2)
                    a.wait_ge(q["rot_ready"], 4)
                    act(kdup[HD:P, 0, :], kdup[0:HD, 0, :], ACT.Copy).then_inc(q["kdup_ready"], 1)
                    act(kdup[0:HD, 1, :], kdup[HD:P, 1, :], ACT.Copy).then_inc(q["kdup_ready"], 1)
                    a.wait_ge(q["cmp_arg"], 2)
                    act(npc_flat, npc_flat, ACT.Exp).then_inc(q["cmp_exp"], 1)
                    for m in range(2 * NT):
                        qt = m // 2
                        if m:
                            a.wait_ge(q["pt_ps"], PTN[m])
                        for h in range(H):
                            x = 4 * m + h
                            a.wait_ge(q["nm_ready"], x + 1)
                            act(nP[:, h, 0:P * (qt + 1)], PS[2 + h % 2][:, 0:P * (qt + 1)], ACT.Exp,
                                bias=nm[:, x:x + 1], accum_out=nsum[:, x:x + 1]).then_inc(q["p_ready"], 1)
                        if m % 2:
                            a.wait_ge(q["ot_ps"], qt + 1)
                            act(nsa_out[:, :, P * qt:P * qt + P], PS[6][:, 0:256].rearrange("p (i c) -> p i c", i=2),
                                ACT.Copy).then_inc(q["nsa_done"], 1)
                    for dt in range(KT):
                        for m in range(3):
                            act(gate[:, KT * m + dt, :], gate[:, KT * m + dt, :], ACT.Tanh, scale=0.5)\
                                .then_inc(q["gate_tanh"], 1)
                        b = stream(f"gate{EARLY + dt}")
                        if dt >= 2:
                            a.wait_ge(q["br_taken"], 4 * dt - 4)
                        act(g3[:, dt % 2, :], b[:, :], ACT.Tanh, scale=0.5).then_inc(q["proj_taken"], 1)
                    for k in range(KT):
                        a.wait_ge(q["xo_ready"], k + 1)
                        act(hT[:, k, :], xT[:, k, :], ACT.Square).then_inc(q["sq2_ready"], 1)
                    a.wait_ge(q["ss2_ps"], 1)
                    rsqrt(rs2, PS[2][:, :], D, q["rstd2_ready"])
                    for f in range(FT):
                        a.wait_ge(q["slab_done"], SLAB[f"fg{f}"] + 1)
                        if f >= 2:
                            a.wait_ge(q["hid_ready"], f - 1)
                        act(ft[:, f % 2, :], PS[2 * (f % 4)][:, :], ACT.Tanh, scale=0.5).then_inc(q["fg_tanh"], 1)

                @block.vector
                def _(v):
                    chain = [0]
                    tt_, ts, stt = nc.vector.tensor_tensor, nc.vector.tensor_scalar, nc.vector.scalar_tensor_tensor
                    M, A_, SU = ALU.mult, ALU.add, ALU.subtract

                    def step(ins):
                        chain[0] += 1
                        ins.then_inc(q["dve_step"], 1)
                        v.wait_ge(q["dve_step"], chain[0])

                    step(v.memset(arena[:, 0:512], 0.0))
                    v.memset(state[:, :, :], 0.0).then_inc(q["st_ready"], 1)
                    v.wait_ge(q["pack_loaded"], 16)
                    lre, lim = prm("lre"), prm("lim")
                    v.wait_ge(q["trig_done"], 1)
                    step(tt_(theta, lim, dt5, M))
                    step(tt_(lrdt, lre, dt5, M))
                    step(ts(tmp1, theta, INV_2PI, ROUND, M, A_))
                    step(ts(tmp1, tmp1, ROUND, None, SU))
                    step(stt(thr, tmp1, -C1, theta, M, A_))
                    step(stt(thr, tmp1, -C2, thr, M, A_))
                    step(stt(thr, tmp1, -C3, thr, M, A_))
                    step(ts(thr, thr, -3.1415925, 3.1415925, ALU.max, ALU.min))
                    stt(thabs, thr, -1.0, thr, M, ALU.max).then_inc(q["abc_done"], 1)
                    step(ts(uh, thr, INV_2PI, ROUND12, M, A_))
                    step(ts(uh, uh, ROUND12, None, SU))
                    step(stt(ul, uh, -C1, thr, M, A_))
                    step(stt(ul, uh, -C2, ul, M, A_))
                    step(stt(ul, uh, -C3, ul, M, A_))
                    step(ts(ul, ul, INV_2PI, None, M))
                    step(ts(prm("cim"), prm("cim"), -1.0, None, M))
                    step(ts(prm("cw"), prm("cw"), 0.5, None, M))
                    step(ts(q8, prm("qn"), 0.125, None, M))
                    step(tt_(den, lre, lre, M))
                    step(tt_(tmp1, lim, lim, M))
                    step(tt_(den, den, tmp1, A_))
                    step(v.reciprocal(den, den))
                    v.wait_ge(q["trig_done"], 4)
                    step(tt_(abr, mag, cosa, M))
                    step(tt_(abi, mag, sina, M))
                    step(ts(abr, abr, 1.0, None, SU))
                    step(tt_(tmp1, abr, lre, M))
                    step(tt_(tmp2, abi, lim, M))
                    step(tt_(fre, tmp1, tmp2, A_))
                    step(tt_(fre, fre, den, M))
                    step(tt_(tmp1, abi, lre, M))
                    step(tt_(tmp2, abr, lim, M))
                    step(tt_(fim, tmp1, tmp2, SU))
                    step(tt_(fim, fim, den, M))
                    br = prm("bre").rearrange("p (i c) -> p i c", i=8)
                    bi = prm("bim").rearrange("p (i c) -> p i c", i=8)
                    b1 = arena[:, 512:640].rearrange("p (i c) -> p i c", i=8)
                    b2 = arena[:, 640:768].rearrange("p (i c) -> p i c", i=8)
                    bre_pad = arena[:, 0:256].rearrange("p (i c) -> p i c", i=8)
                    bim_pad = arena[:, 256:512].rearrange("p (i c) -> p i c", i=8)
                    freb = fre.unsqueeze(2).broadcast_to([P, 8, 16])
                    fimb = fim.unsqueeze(2).broadcast_to([P, 8, 16])
                    for pad, x, y, op in ((bre_pad, br, bi, SU), (bim_pad, bi, br, A_)):
                        step(tt_(b1, x, freb, M))
                        step(tt_(b2, y, fimb, M))
                        for s in range(2):
                            r, c = slice(HD * s, HD * s + HD), slice(16 * s, 16 * s + 16)
                            last = tt_(pad[r, :, c], b1[r], b2[r], op)
                            if op == A_ and s == 1:
                                last.then_inc(q["bpad_ready"], 1)
                            else:
                                step(last)
                    v.wait_ge(q["bt_ps"], 1)
                    nc.vector.tensor_copy(bt.rearrange("p r t s -> p (r t s)"), PS[7][:, :]).then_inc(q["bt_taken"], 1)
                    v.wait_ge(q["rstd_ready"], 1)
                    for k in range(KT):
                        stt(hT[:, k, :], xT[:, k, :], prm("an")[:, k:k + 1], rs1, M, M).then_inc(q["h_ready"], 1)
                    v.wait_ge(q["proj_taken"], 1)
                    step(tt_(xa.rearrange("p (t c) -> p t c", t=4), sm_all[:, :, 16:20],
                             prm("dtb").rearrange("p (t c) -> p t c", t=4), A_))
                    stt(na, xa, -1.0, xa, M, ALU.min).then_inc(q["xa_neg"], 1)

                    def conv(i):
                        v.wait_ge(q["proj_taken"], 2 + i)
                        w = prm("cw")[:, 4 * i:4 * i + 4]
                        x, o = pj[:, i, :], cv[:, i, :]
                        step(ts(o, x, w[:, 3:4], None, M))
                        for d in (1, 2):
                            step(stt(o[:, d:S], x[:, 0:S - d], w[:, 3 - d:4 - d], o[:, d:S], M, A_))
                        stt(o[:, 3:S], x[:, 0:S - 3], w[:, 0:1], o[:, 3:S], M, A_).then_inc(q["conv_ready"], 1)

                    conv(0)
                    conv(1)
                    v.wait_ge(q["sig_exp"], 1)
                    step(ts(e_sig, e_sig, 1.0, None, A_))
                    v.reciprocal(sig, e_sig).then_inc(q["sig_ready"], 1)
                    v.wait_ge(q["xa_ln"], 1)
                    step(stt(xa, xa, 0.0, la, ALU.max, A_))
                    stt(g16, xa, -1.0, ea, M, M).then_inc(q["g_ready"], 1)
                    for i in range(2, 6):
                        conv(i)
                    for i in range(6):
                        v.wait_ge(q["tanh_ready"], i + 1)
                        stt(cv[:, i, :], th[:, i, :], 1.0, cv[:, i, :], A_, M).then_inc(q["silu_ready"], 1)
                    v.wait_ge(q["cmp1_ps"], 1)
                    step(tt_(ct, cx, cx, M))
                    step(ts(ct, ct, GELU_A, 1.0, M, A_))
                    tt_(ct, ct, cx, M).then_inc(q["cmp_arg"], 1)
                    v.wait_ge(q["cmp_exp"], 1)
                    step(stt(ct, ct, 1.0, cx, A_, M))
                    ts(cmp_flat, ct, 0.5, None, M).then_inc(q["cmp_hid"], 1)
                    v.wait_ge(q["gsum_ps"], 1)
                    step(nc.vector.tensor_copy(small[:, GC0:GC0 + 32], PS[2][:, 0:32]))
                    tt_(kdc, gl, gc, SU).then_inc(q["gsum_taken"], 1)
                    v.wait_ge(q["kc_rstd"], 1)
                    stt(kcT, kcT, prm("kn0"), kc_r, M, M).then_inc(q["kc_ready"], 1)
                    for i in range(4):
                        v.wait_ge(q["qk_rstd"], i + 1)
                        stt(cv[:, i, :], cv[:, i, :], 0.125 if i < 2 else 1.0, rqk[:, i, :], M, M).then_inc(q["qk_ready"], 1)
                    v.wait_ge(q["qk_ready"], 4)
                    for b in range(4):
                        v.wait_ge(q["grow_ps"], b + 1)
                        for j, (tt, h) in enumerate(UNITS[4 * b:4 * b + 4]):
                            c = gc[:, 4 * tt + h:4 * tt + h + 1]
                            ps = PS[3 + b][:, P * j:P * j + P]
                            ts(mL[:, 4 * b + j, :], ps, c, 0.0, SU, ALU.max)
                            last = ts(mY[:, 4 * b + j, :], ps, c, 0.0, SU, ALU.min)
                        last.then_inc(q["args_ready"], 1)
                    v.wait_ge(q["gexp_ready"], 1)
                    v.wait_ge(q["sig_ready"], 1)
                    step(tt_(bg.rearrange("p (t c) -> p t c", t=4), sig[:, :, 12:16], egc.rearrange("p (t c) -> p t c", t=4), M))

                    def per_token(x, tt):
                        return x[:, tt:tt + 2, :].unsqueeze(3).broadcast_to([P, 2, 4, HD])

                    b4 = [x.rearrange("p (t c) -> p t c", t=4) for x in (bg, kdc)] + [sig[:, :, 12:16]]
                    for b in range(4):
                        v.wait_ge(q["tr_ps"], b + 1)
                        tt = 2 * (b % 2)
                        ps = PS[3 + b][:, :].rearrange("p (t h e) -> p t h e", t=2, h=4)
                        if b < 2:
                            tt_(kbg[:, tt:tt + 2, :].rearrange("p t (h e) -> p t h e", h=4), ps, per_token(b4[0], tt), M)
                            tt_(kdec[:, tt:tt + 2, :].rearrange("p t (h e) -> p t h e", h=4), ps, per_token(b4[1], tt), M)\
                                .then_inc(q["tr_taken"], 1)
                        else:
                            tt_(vb[:, tt:tt + 2, :].rearrange("p t (h e) -> p t h e", h=4), ps, per_token(b4[2], tt), M)\
                                .then_inc(q["tr_taken"], 1)
                    for b in range(4):
                        r = slice(S * b, S * b + S)
                        v.wait_ge(q["skk_ps"], b + 1)
                        v.wait_ge(q["dmask_ready"], 3 * b + 3)
                        tt_(mL_flat[:, r], PS[3 + b][:, :], mL_flat[:, r], M).then_inc(q["l_part"], 1)
                    for b in range(4):
                        r = slice(S * b, S * b + S)
                        v.wait_ge(q["skq_ps"], b + 1)
                        tt_(aT_flat[:, r], PS[3 + b][:, :], mY_flat[:, r], M).then_inc(q["at_part"], 1)

                    def four(x):
                        return x.unsqueeze(1).broadcast_to([P, 4, P])

                    def bank4(b):
                        return PS[b][:, :].rearrange("p (u c) -> p u c", u=4)

                    for b in range(4):
                        u = slice(4 * b, 4 * b + 4)
                        v.wait_ge(q["y0_ps"], b + 1)
                        tt_(mY[:, u, :], bank4(3 + b), four(lev[:, 0, :]), M).then_inc(q["u0_ready"], 1)
                        v.wait_ge(q["u0_ready"], 2 * b + 1)
                        tt_(mU[:, u, :], four(ident), mY[:, u, :], SU).then_inc(q["u0_ready"], 1)
                    v.wait_ge(q["qd_ready"], 8)
                    for b in range(4):
                        u = slice(4 * b, 4 * b + 4)
                        v.wait_ge(q["t0_ps"], b + 1)
                        tt_(mT[:, u, :], four(ident), bank4(3 + b), SU).then_inc(q["t0_ready"], 1)

                    def y_mask(n):
                        b = n % 4
                        v.wait_ge(q["y_ps"], n + 1)
                        tt_(mY[:, 4 * b:4 * b + 4, :], bank4(2 + n % 2), four(lev[:, 1 + n // 4, :]), M)\
                            .then_inc(q["y_ready"], 1)

                    def ut_update(n):
                        u = slice(4 * (n % 4), 4 * (n % 4) + 4)
                        v.wait_ge(q["du_ps"], n + 1)
                        tt_(mU[:, u, :], mU[:, u, :], bank4(4 + n % 2), SU).then_inc(q["u_ready"], 1)
                        if n < 20:
                            v.wait_ge(q["dt_ps"], n + 1)
                            tt_(mT[:, u, :], mT[:, u, :], bank4(6 + n % 2), SU).then_inc(q["t_ready"], 1)

                    for lv in range(6):
                        y_mask(4 * lv)
                        y_mask(4 * lv + 1)
                        ut_update(4 * lv)
                        y_mask(4 * lv + 2)
                        ut_update(4 * lv + 1)
                        y_mask(4 * lv + 3)
                        ut_update(4 * lv + 2)
                        ut_update(4 * lv + 3)
                    for tt in range(NT):
                        v.wait_ge(q["vn_ps"], tt + 1)
                        for par in range(2):
                            nc.vector.tensor_copy(vn[:, par::2, :], PS[2 + par][:, 0:P].rearrange("p (i e) -> p i e", i=2))\
                                .then_inc(q["vn_ready"], 1)
                        v.wait_ge(q["su_ps"], tt + 1)
                        for h in range(H):
                            x = state[half(h), h // 2, :]
                            stt(x, x, egl[half(h), 4 * tt + h:4 * tt + h + 1],
                                PS[4 + h % 2][half(h), HD * (h // 2):HD * (h // 2) + HD], M, A_).then_inc(q["st_ready"], 1)
                    for i in range(2):
                        v.wait_ge(q["z_tanh"], i + 1)
                        v.wait_ge(q["o_rstd"], i + 1)
                        step(stt(z_th[:, i, :], z_th[:, i, :], 1.0, pjt[f"z{i}"], A_, M))
                        step(stt(o_raw[:, i, :], o_raw[:, i, :], prm("on"), o_rs[:, i, :], M, M))
                        stt(pjt[f"z{i}"], z_th[:, i, :], 0.5, o_raw[:, i, :], M, M).then_inc(q["gdn_done"], 1)

                    tk = cst("t")
                    v.wait_ge(q["gdn_done"], 2)

                    def s5_table(i):
                        f, g = s5_buf(i, 6), s5_buf(i, 7)
                        step(ts(g, tk, uh[:, i:i + 1], ROUND, M, A_))
                        step(ts(g, g, ROUND, None, SU))
                        step(stt(f, tk, uh[:, i:i + 1], g, M, SU))
                        step(stt(f, tk, ul[:, i:i + 1], f, M, A_))
                        step(ts(g, f, ROUND, None, A_))
                        step(ts(g, g, ROUND, None, SU))
                        tt_(f, f, g, SU).then_inc(q["tab_ready"], 1)
                        v.wait_ge(q["tab_ready"], 2 * i + 1)
                        stt(g, f, -1.0, f, M, ALU.max).then_inc(q["tab_ready"], 1)

                    s5_table(0)
                    for i in range(8):
                        c_, s_, m1, m2, m3, m4, zr, zi = (s5_buf(i, j) for j in range(8))
                        bur, bui = PS[2 + 2 * (i % 2)][:, :], PS[3 + 2 * (i % 2)][:, :]
                        if i < 7:
                            if i >= 1:
                                v.wait_ge(q["y5_ps"], i)
                            s5_table(i + 1)
                        v.wait_ge(q["sin_ready"], 2 * i + 2)
                        v.wait_ge(q["bu_ps"], i + 1)
                        tt_(m1, c_, bur, M)
                        tt_(m2, s_, bui, M)
                        tt_(m3, c_, bui, M)
                        tt_(m4, s_, bur, M).then_inc(q["m_ready"], 1)
                        v.wait_ge(q["w_ready"], 2 * i + 2)
                        mg = mag[:, i:i + 1].broadcast_to([P, S])
                        v.tensor_tensor_scan(zr, mg, m1, 0.0, M, A_).then_inc(q["z_ready"], 1)
                        v.tensor_tensor_scan(zi, mg, m3, 0.0, M, A_).then_inc(q["z_ready"], 1)
                        v.wait_ge(q["z_ready"], 2 * i + 2)
                        tt_(m1, c_, zr, M).then_inc(q["n_ready"], 1)
                        tt_(m2, s_, zi, M).then_inc(q["n_ready"], 1)
                        tt_(m3, s_, zr, M).then_inc(q["n_ready"], 1)
                        tt_(m4, c_, zi, M).then_inc(q["n_ready"], 1)
                    for i in range(2):
                        v.wait_ge(q["y5_ps"], 4 * i + 4)
                        stt(y5a[:, i, :], pjt[f"u{i}"], prm("dsk")[:, i:i + 1], PS[6 + i][:, :], M, A_)\
                            .then_inc(q["y5_ready"], 1)
                    for i in range(2):
                        v.wait_ge(q["y5_sq"], i + 1)
                        step(ts(y5b[:, i, :], y5b[:, i, :], GELU_A, 1.0, M, A_))
                        tt_(y5b[:, i, :], y5b[:, i, :], y5a[:, i, :], M).then_inc(q["y5_poly"], 1)
                    for i in range(2):
                        v.wait_ge(q["y5_tanh"], i + 1)
                        stt(gy[:, i, :], y5b[:, i, :], 1.0, y5a[:, i, :], A_, M).then_inc(q["gy_ready"], 1)
                    for i in range(2):
                        v.wait_ge(q["glu_tanh"], i + 1)
                        step(stt(y5b[:, i, :], y5b[:, i, :], 1.0, PS[2 + i][:, :], A_, M))
                        ts(s5_out[:, i, :], y5b[:, i, :], 0.25, None, M).then_inc(q["s5_done"], 1)

                    def sb_first(n):
                        h, kb = n // 4, 3 - n % 4
                        r = slice(P * kb, S)
                        v.wait_ge(q["z_copied"], n + 1)
                        stt(sb_e(n)[:, r], sb_z(h, kb)[:, r], -1.0, sb_z(h, kb)[:, r], M, ALU.min).then_inc(q["nb_ready"], 1)
                        v.wait_ge(q["sp_ln"], n + 1)
                        if h >= 2:
                            v.wait_ge(q["cum_ps"], 4 * h - 4)
                        stt(sb_sp(h, kb)[:, r], sb_z(h, kb)[:, r], 0.0, sb_e(n)[:, r], ALU.max, A_).then_inc(q["sp_ready"], 1)
                        v.wait_ge(q["sp_ready"], n + 1)
                        c = slice(P * kb, P * kb + P)
                        tt_(sb_sp(h, kb)[:, c], sb_sp(h, kb)[:, c], cst("lt"), M).then_inc(q["sp_masked"], 1)

                    def sb_last(n):
                        h, kb = n // 4, 3 - n % 4
                        r = slice(P * kb, S)
                        v.wait_ge(q["cum_ps"], n + 1)
                        stt(sb_z(h, kb)[:, r], PS[4 + n % 2][:, 0:S - P * kb], -1.0, sb_z(h, kb)[:, r], M, A_)\
                            .then_inc(q["d_ready"], 1)
                        v.wait_ge(q["d_ready"], n + 1)
                        c = slice(P * kb, P * kb + P)
                        tt_(sb_z(h, kb)[:, c], sb_z(h, kb)[:, c], cst("negk"), A_).then_inc(q["d_masked"], 1)

                    def sb_store(h):
                        v.wait_ge(q["sbpv_ps"], h + 1)
                        nc.vector.tensor_copy(sb_out[half(h), h // 2, :], PS[6 + h % 2][half(h), :])\
                            .then_inc(q["sb_done"], 1)

                    for n in range(16 + 2):
                        if n < 16:
                            sb_first(n)
                        if n >= 2:
                            sb_last(n - 2)
                        if n >= 9 and n % 4 == 1:
                            sb_store(n // 4 - 2)
                    sb_store(3)
                    for i in range(3):
                        v.wait_ge(q["q_rstd"], i + 1)
                        stt(nqn[:, i, :], pjt[("q0", "q1", "kskw")[i]], q8 if i < 2 else prm("kn12"), nrs[:, i, :], M, M)\
                            .then_inc(q["qn_ready"], 1)
                    for i in range(3):
                        v.wait_ge(q["rot_ps"], i + 1)
                        tt_(nts[:, i, :], PS[2 + i][:, :], sinT[:, :], M).then_inc(q["t_sin"], 1)
                    cm = [cst(n).rearrange("p (t n) -> p t n", t=NT).unsqueeze(2).broadcast_to([P, NT, 2, NCMP])
                          for n in ("cneg", "c01")]
                    for par in range(2):
                        v.wait_ge(q["sc_cmp_ps"], par + 1)
                        step(tt_(npc[:, 8 * par:8 * par + 8, :].rearrange("p (t i) n -> p t i n", i=2),
                                 PS[6 + par][:, 0:248].rearrange("p (t i n) -> p t i n", t=NT, i=2), cm[0], A_))
                    step(v.tensor_reduce(nc1, npc, AX_X, ALU.max))
                    tt_(npc, npc, nc1.unsqueeze(2).broadcast_to([P, 16, NCMP]), SU).then_inc(q["cmp_arg"], 1)
                    v.wait_ge(q["cmp_exp"], 2)
                    for par in range(2):
                        x = npc[:, 8 * par:8 * par + 8, :].rearrange("p (t i) n -> p t i n", i=2)
                        step(tt_(x, x, cm[1], M))
                    step(v.tensor_reduce(nc1, npc, AX_X, A_))
                    step(ts(nc1, nc1, 1e-30, None, ALU.max))
                    step(v.reciprocal(nc1, nc1))
                    gates = sig[:, :, 0:12].rearrange("p t (i r b) -> p t i r b", i=2, r=2)
                    for par in range(2):
                        x = nc1[:, 8 * par:8 * par + 8].rearrange("p (t i) -> p t i", i=2)
                        step(tt_(x, x, gates[:, :, :, par, 0], M))
                    tt_(npc, npc, nc1.unsqueeze(2).broadcast_to([P, 16, NCMP]), M).then_inc(q["pc_ready"], 1)

                    def combine(qt):
                        v.wait_ge(q["p_ready"], 8 * qt + 8)
                        step(v.reciprocal(nfac, nsum[:, 8 * qt:8 * qt + 8]))
                        f = nfac.rearrange("p (b h) -> p b h", b=2)
                        gt = sig[:, qt, 0:12].rearrange("p (h b) -> p b h", b=3)
                        step(tt_(f, f, gt[:, 1:3, :], M))
                        v.wait_ge(q["pv_ps"], 2 * qt + 2)
                        o4 = nO.rearrange("p (h e) -> p h e", h=4)
                        w4 = nO2.rearrange("p (h e) -> p h e", h=4)
                        step(tt_(o4, PS[6][:, 0:256].rearrange("p (h e) -> p h e", h=4),
                                 f[:, 0, :].unsqueeze(2).broadcast_to([P, 4, HD]), M))
                        step(tt_(nO, nO, PS[6][:, 256:512], A_))
                        step(tt_(w4, PS[7][:, 0:256].rearrange("p (h e) -> p h e", h=4),
                                 f[:, 1, :].unsqueeze(2).broadcast_to([P, 4, HD]), M))
                        tt_(nO, nO, nO2, A_).then_inc(q["onat_ready"], 1)

                    for m in range(2 * NT):
                        qt = m // 2
                        for h in range(H):
                            v.wait_ge(q["sc_ps"], 4 * m + h + 1)
                            v.tensor_reduce(nm[:, 4 * m + h:4 * m + h + 1], PS[2 + h % 2][:, 0:P * (qt + 1)], AX_X,
                                            ALU.max, negate=True).then_inc(q["nm_ready"], 1)
                        if m % 2 == 0:
                            v.wait_ge(q["pct_ps"], qt + 1)
                            nc.vector.tensor_copy(npct[0:NCMP, :], PS[7][0:NCMP, :]).then_inc(q["pct_ready"], 1)
                        if m:
                            v.wait_ge(q["pv_ps"], m)
                        for kb in range(qt + 1):
                            x = PTN[m] + kb
                            v.wait_ge(q["pt_ps"], x + 1)
                            nc.vector.tensor_copy(npt[:, kb, :], PS[4 + x % 2][:, :]).then_inc(q["pt_ready"], 1)
                        if m % 2:
                            combine(qt)
                    for dt in range(KT):
                        if dt >= 2:
                            v.wait_ge(q["merged_ready"], dt - 1)
                        for m in range(4):
                            if m < 3:
                                v.wait_ge(q["br_ps"], 3 * dt + m + 1)
                                v.wait_ge(q["gate_tanh"], 3 * dt + m + 1)
                                g = gate[:, KT * m + dt, :]
                            else:
                                v.wait_ge(q["slab_done"], SLAB[f"br{dt}"] + 1)
                                v.wait_ge(q["proj_taken"], 1 + len(TILES) + 2 + EARLY + dt + 1)
                                g = g3[:, dt % 2, :]
                            o = merged[:, dt, :] if m == 0 else mtmp[:, dt % 2, m - 1, :]
                            stt(o, g, 1.0, PS[2 + m][:, :], A_, M).then_inc(q["br_taken"], 1)
                    for dt in range(KT):
                        v.wait_ge(q["slab_done"], SLAB[f"out{dt}"] + 1)
                        stt(xT[:, dt, :], PS[4 + dt % 4][:, :], 0.5, xT[:, dt, :], M, A_).then_inc(q["xo_ready"], 1)
                    v.wait_ge(q["rstd2_ready"], 1)
                    for k in range(KT):
                        stt(hT[:, k, :], xT[:, k, :], prm("fn")[:, k:k + 1], rs2, M, M).then_inc(q["h2_ready"], 1)
                    for f in range(FT):
                        v.wait_ge(q["fg_tanh"], f + 1)
                        stt(fa[:, f % 2, :], ft[:, f % 2, :], 1.0, PS[2 * (f % 4)][:, :], A_, M).then_inc(q["ga_ready"], 1)
                        v.wait_ge(q["ga_ready"], f + 1)
                        v.wait_ge(q["slab_done"], SLAB[f"fu{f}"] + 1)
                        stt(gate[:, f, :], fa[:, f % 2, :], 0.5, PS[2 * (f % 4) + 1][:, :], M, M).then_inc(q["hid_ready"], 1)
                    for dt in range(KT):
                        v.wait_ge(q["slab_done"], SLAB[f"dn{dt}_2"] + 1)
                        tt_(xT[:, dt, :], xT[:, dt, :], PS[dt % 4][:, :], A_).then_inc(q["dn_taken"], 1)

                @block.gpsimd
                def _(g):
                    tt_, M, A_, SU = nc.gpsimd.tensor_tensor, ALU.mult, ALU.add, ALU.subtract
                    g.wait_ge(q["proj_taken"], 1 + 9)
                    g.wait_ge(q["pack_loaded"], 16)
                    for src, dst, pos in ((t2k, bk, prm("posk")), (t2v, bv, prm("posv"))):
                        for x in range(2):
                            view = src[:, 16 * x:16 * x + 496].rearrange("p (n b t) -> p b n t", b=8, t=2)[:, :, :, 0]
                            tt_(dst[:, 8 * x:8 * x + 8, :], view,
                                pos[:, 8 * x:8 * x + 8].unsqueeze(2).broadcast_to([P, 8, NCMP]), A_)\
                                .then_inc(q["blocks_ready"], 1)
                    g.wait_ge(q["sig_ready"], 1)
                    for b in range(4):
                        u = slice(4 * b, 4 * b + 4)
                        g.wait_ge(q["dexp_ready"], 2 * b + 2)
                        tt_(mL[:, u, :], mL[:, u, :], cst("gt").unsqueeze(1).broadcast_to([P, 4, P]), M)\
                            .then_inc(q["dmask_ready"], 1)
                        tt_(mY[:, u, :], mY[:, u, :], cst("le").unsqueeze(1).broadcast_to([P, 4, P]), M)\
                            .then_inc(q["dmask_ready"], 1)
                        g.wait_ge(q["dmask_ready"], 3 * b + 2)
                        t0, par = 2 * (b // 2), b % 2
                        for x in range(2):
                            be = sig[:, t0 + x, 12 + par:15 + par:2] if par == 0 else sig[:, t0 + x, 13:16:2]
                            last = tt_(mL[:, 4 * b + 2 * x:4 * b + 2 * x + 2, :], mL[:, 4 * b + 2 * x:4 * b + 2 * x + 2, :],
                                       be.unsqueeze(2).broadcast_to([P, 2, P]), M)
                        last.then_inc(q["dmask_ready"], 1)
                    g.wait_ge(q["grow_exp"], 4)
                    g.wait_ge(q["qk_ready"], 4)
                    g.wait_ge(q["dmask_ready"], 12)
                    for tt in range(NT):
                        for par in range(2):
                            r = slice(HD * par, HD * par + HD)
                            u = unit(tt, par)
                            if tt + par:
                                g.wait_ge(q["qd_ready"], 2 * tt + par)
                            tt_(qd[r, :, P * tt:P * tt + P], cv[r, 0:2, P * tt:P * tt + P], mT[r, u:u + 2, :], M)\
                                .then_inc(q["qd_ready"], 1)
                    for i in range(8):
                        _, _, m1, m2, m3, m4, _, _ = (s5_buf(i, j) for j in range(8))
                        if i == 0:
                            g.wait_ge(q["qd_ready"], 8)
                        g.wait_ge(q["m_ready"], i + 1)
                        tt_(m1, m1, m2, A_).then_inc(q["w_ready"], 1)
                        tt_(m3, m3, m4, SU).then_inc(q["w_ready"], 1)
                        g.wait_ge(q["n_ready"], 4 * i + 2)
                        tt_(m1, m1, m2, SU).then_inc(q["x_ready"], 1)
                        g.wait_ge(q["n_ready"], 4 * i + 4)
                        tt_(m3, m3, m4, A_).then_inc(q["x_ready"], 1)
                    for i in range(3):
                        g.wait_ge(q["qn_ready"], i + 1)
                        tt_(nqr[:, i, :], nqn[:, i, :], cosT[:, :], M).then_inc(q["t_cos"], 1)
                        g.wait_ge(q["t_cos"], i + 1)
                        g.wait_ge(q["t_sin"], i + 1)
                        if i < 2:
                            tt_(nqr[:, i, :], nqr[:, i, :], nts[:, i, :], A_).then_inc(q["rot_ready"], 1)
                        else:
                            for x in range(2):
                                r = slice(HD * x, HD * x + HD)
                                g.wait_ge(q["rot_ready"], 2 + x)
                                tt_(kdup[r, x, :], nqr[r, i, :], nts[r, i, :], A_).then_inc(q["rot_ready"], 1)
                    g.wait_ge(q["rot_ready"], 4)
                    for dt in range(KT):
                        for m in range(1, 4):
                            g.wait_ge(q["br_taken"], 4 * dt + m + 1)
                            ins = tt_(merged[:, dt, :], merged[:, dt, :], mtmp[:, dt % 2, m - 1, :], A_)
                            ins.then_inc(q["merged_ready"] if m == 3 else q["merged_part"], 1)
                            if m < 3:
                                g.wait_ge(q["merged_part"], 2 * dt + m)
            nc.all_engine_barrier(sems_to_clear=range(sems[0].num, sems[-1].num + 1))

        with nc.Block() as block:
            @block.sync
            def _(sp):
                sp.dma_start(a_out, xT[:, :, :]).then_inc(s_x, 16)
                sp.wait_ge(s_x, 32)


def _slab_cols(w, ranges):
    x = np.concatenate([w[:, a:a + n] for a, n in ranges], axis=1)
    return x.reshape(KT, P, -1).transpose(1, 0, 2)


def _stream(i, l):
    out = np.zeros((NSLAB, P, KT * P), np.float32)

    def put(name, x):
        x = x.reshape(P, -1)
        out[SLAB[name], :, :x.shape[1]] = x

    w_in = i["w_in"][l]
    put("small", _slab_cols(w_in, [(O_G, 12), (O_B, 4), (O_A, 4)]))
    for name, ranges in TILES:
        put(name, _slab_cols(w_in, ranges))
    v = _slab_cols(w_in, [(O_SB + 512, 256)])
    put("sbv0", v[:, 0:4])
    put("sbv1", v[:, 4:8])
    for kv in "kv":
        w1 = i[f"nsa_cmp_{kv}_w1"][l].reshape(16, P, 256).transpose(1, 0, 2)
        for j in range(4):
            put(f"c{kv}{j}", w1[:, 4 * j:4 * j + 4])
    w2k = i["nsa_cmp_k_w2"][l].reshape(2, P, HD).transpose(1, 0, 2)
    w2v = i["nsa_cmp_v_w2"][l].reshape(2, P, HD).transpose(1, 0, 2)
    put("cw2", np.concatenate([np.concatenate([w2k, w2k], axis=2).reshape(P, 256), w2v.reshape(P, 128)], axis=1))
    put("glu", i["s5_glu_w"][l].reshape(2, P, 512).transpose(1, 0, 2))
    for g in range(4 * KT):
        put(f"gate{g}", _slab_cols(w_in, [(O_GATE + P * g, P)]))
    br = i["w_branch"][l].reshape(4, 2, P, D).transpose(2, 0, 1, 3)
    for dt in range(KT):
        c = slice(P * dt, P * dt + P)
        put(f"br{dt}", np.ascontiguousarray(br[:, :, :, c]))
        put(f"out{dt}", _slab_cols(i["w_out"][l], [(P * dt, P)]))
        dn = i["w_down"][l][:, c].reshape(FT, P, P).transpose(1, 0, 2)
        for j in range(3):
            put(f"dn{dt}_{j}", dn[:, KT * j:KT * j + KT])
    for f in range(FT):
        put(f"fg{f}", _slab_cols(i["w_gate"][l], [(P * f, P)]))
        put(f"fu{f}", _slab_cols(i["w_up"][l], [(P * f, P)]))
    return out


def _pack(i, l):
    out = np.zeros((P, NPK), np.float32)

    def put(name, x):
        at, n = PK[name]
        out[:, at:at + n] = x.reshape(P, n)

    two = lambda x: np.concatenate([x, x])
    put("an", i["attn_norm"][l].reshape(KT, P).T)
    put("fn", i["ffn_norm"][l].reshape(KT, P).T)
    put("qn", two(i["nsa_q_norm"][l]))
    kn = i["nsa_k_norm"][l]
    put("kn12", np.concatenate([kn[1], kn[2]]))
    put("kn0", two(kn[0]))
    put("on", two(i["gdn_o_norm"][l]))
    for name, x in (("posk", i["nsa_cmp_pos"][l, 0]), ("posv", i["nsa_cmp_pos"][l, 1])):
        put(name, x.reshape(16, P).T)

    def states(x):
        return np.moveaxis(x.reshape((8, P) + x.shape[2:]), 0, 1)

    put("lre", states(i["s5_lam_re"][l]))
    put("lim", states(i["s5_lam_im"][l]))
    put("ldt", states(np.repeat(i["s5_log_dt"][l][:, None], HD, axis=1)))
    put("bre", states(i["s5_b_re"][l]))
    put("bim", states(i["s5_b_im"][l]))
    for name in ("cre", "cim"):
        c = states(i[f"s5_c_{name[1:]}"][l].transpose(0, 2, 1))
        pad = np.zeros((P, 8, 32), np.float32)
        pad[0:HD, :, 0:16] = c[0:HD]
        pad[HD:P, :, 16:32] = c[HD:P]
        put(name, pad)
    put("dsk", i["s5_d"][l].reshape(2, P).T)
    put("cw", i["gdn_conv_w"][l].T.reshape(6, P, 4).transpose(1, 0, 2))
    for name, x in (("alog", i["gdn_a_log"][l]), ("dtb", i["gdn_dt_bias"][l])):
        put(name, np.broadcast_to(np.tile(x, NT), (P, 4 * NT)))
    return out


def _constants():
    out = np.zeros((P, NCK), np.float32)

    def put(name, x):
        at, n = CK[name]
        out[:, at:at + n] = np.asarray(x, np.float32).reshape(P, n)

    r, c = np.arange(P)[:, None], np.arange(P)[None, :]
    put("ident", r == c)
    put("ones", np.ones((P, P)))
    put("blk", r // HD == c // HD)
    put("le", r <= c)
    put("ge", r >= c)
    put("lt", r < c)
    put("gt", r > c)
    put("negq", np.where(c > r, NEG, 0.0))
    put("negk", np.where(r >= c, NEG, 0.0))
    lev = np.zeros((P, 7, P))
    for n in range(7):
        s = 1 << n
        lev[:, n] = (r // (2 * s) == c // (2 * s)) & (r % (2 * s) < s) & (c % (2 * s) >= s)
    put("lev", lev)
    rot = np.zeros((P, P))
    for b in (0, HD):
        for m in range(8):
            rot[b + m + 8, b + m] = -1.0
            rot[b + m, b + m + 8] = 1.0
    put("rot", rot)
    half = 8
    f = np.float32(500000.0) ** (-np.arange(half, dtype=np.float32) / np.float32(half))
    freq = np.zeros(P, np.float32)
    for b in (0, 8, HD, HD + 8):
        freq[b:b + 8] = f
    put("freq", freq)
    t = P * np.arange(NT)[None, :, None] + np.arange(P)[:, None, None]
    ok = 16 * np.arange(NCMP)[None, None, :] + 31 <= t
    put("c01", ok)
    put("cneg", np.where(ok, 0.0, NEG))
    put("t", np.broadcast_to(np.arange(S), (P, S)))
    return out


def kernel(**inputs):
    import concourse.bacc as bacc
    from concourse.bass_utils import run_bass_kernel_spmd

    i = {k: np.asarray(v) for k, v in inputs.items()}
    arrays = {
        "x": np.ascontiguousarray(i["x"][0].T.reshape(KT, P, S).transpose(1, 0, 2)),
        "pos": np.ascontiguousarray(np.broadcast_to(i["positions"].reshape(1, S), (P, S))),
        "constants": _constants(),
        "params": np.stack([_pack(i, l) for l in range(DEPTH)]),
        "weights": np.stack([_stream(i, l) for l in range(DEPTH)]),
    }
    nc = bacc.Bacc("TRN2", target_bir_lowering=False, num_devices=1)
    args = [nc.dram_tensor(n, a.shape, mybir.dt.from_np(a.dtype), kind="ExternalInput").ap() for n, a in arrays.items()]
    args.append(nc.dram_tensor("out", (P, KT, S), F32, kind="ExternalOutput").ap())
    program(nc, *args)
    got = run_bass_kernel_spmd(nc, [arrays], core_ids=[0]).results[0]["out"]
    return np.ascontiguousarray(np.asarray(got).transpose(1, 0, 2).reshape(D, S).T)[None]
```

```python
from contextlib import ExitStack

import concourse.bass as bass
import numpy as np
from concourse import mybir

ALU = mybir.AluOpType
ACT = mybir.ActivationFunctionType
AX_X = mybir.AxisListType.X
F32 = mybir.dt.float32
I32 = mybir.dt.int32
BF16 = mybir.dt.bfloat16
F32R = mybir.dt.float32r

P = 128
D = 1024
KT = D // P
S = 512
NT = S // P
DEPTH = 2
HD = 64
FF = 2816
FT = FF // P
H = 4
NCMP = 31
EPS = 1e-6
NEG = -1e30
ROUND = 12582912.0
ROUND12 = 3072.0
TWO_PI = 6.283185307179586
INV_2PI = 1.0 / TWO_PI
C1, C2 = 6.28125, 0.0019340515
C3 = TWO_PI - C1 - C2
SIN_SCALE = 6.2831845
GELU_C = 0.7978845608028654
GELU_A = 0.044715

O_Q, O_KV, O_G, O_U, O_GDN, O_A, O_B, O_Z, O_SB, O_GATE = 0, 256, 640, 652, 908, 1676, 1680, 1684, 1940, 2708
KC, VC, KS, VS, KW, VW = (O_KV + HD * i for i in range(6))

FIRST = ([(f"gdn{i}", [(O_GDN + P * i, P)]) for i in range(6)] + [("kcvc", [(KC, HD), (VC, HD)])])
LATER = ([(f"z{i}", [(O_Z + P * i, P)]) for i in range(2)]
         + [(f"u{i}", [(O_U + P * i, P)]) for i in range(2)]
         + [("kskw", [(KS, HD), (KW, HD)]), ("vsvw", [(VS, HD), (VW, HD)])]
         + [(f"q{i}", [(O_Q + P * i, P)]) for i in range(2)]
         + [(f"sb{i}", [(O_SB + P * i, P)]) for i in range(4)])
TILES = FIRST + LATER
KEPT = [f"gdn{i}" for i in range(6)] + ["kskw", "vsvw", "q0", "q1", "u0", "u1", "sb0", "sb1", "sb2", "sb3", "z0", "z1"]
TI = {name: i for i, name in enumerate(KEPT)}
NPJ = len(KEPT)

FILLERS = [name for name, _ in LATER] + ["sbv"] + [f"gate{g}" for g in range(4 * KT)]
FILL = {"blocks": [1] * 8, "hidden": 1, "gelu": 1, "gsum": 2, "qk": 1, "grow": 1, "turn": 1, "skq": 1,
        "level": [0] * 6, "chunk": [1] * NT, "oss": 1, "s5": [1] * 8, "glu": 2,
        "sb": [1, 1, 1, 1, 1], "norms": 1, "rot": 2, "nsa": [0, 1, 1, 1, 1, 1, 0, 1]}
BEFORE_GELU = sum(FILL["blocks"]) + FILL["hidden"]
BEFORE_GROW = BEFORE_GELU + FILL["gelu"] + FILL["gsum"] + FILL["qk"]
BEFORE_SKK = BEFORE_GROW + FILL["grow"] + FILL["turn"]
BEFORE_S5 = BEFORE_SKK + FILL["skq"] + sum(FILL["level"]) + sum(FILL["chunk"]) + FILL["oss"]
GLU_AT = BEFORE_S5 + sum(FILL["s5"]) + FILL["glu"]
BEFORE_NSA = GLU_AT + sum(FILL["sb"])
assert BEFORE_NSA + FILL["norms"] + FILL["rot"] + sum(FILL["nsa"]) == len(FILLERS)

SLAB = {}
RAW = [f"ck{i}" for i in range(4)] + [f"cv{i}" for i in range(4)] + ["cw2", "glu"]


def _slabs():
    names = ["small"] + [n for n, _ in FIRST]
    at = [sum(FILL["blocks"][:i + 1]) for i in range(8)] + [BEFORE_GELU + FILL["gelu"], GLU_AT]
    for i, n in enumerate(FILLERS):
        names += [r for r, x in zip(RAW, at) if x == i]
        names += ["sbv0", "sbv1"] if n == "sbv" else [n]
    names += [f"br{dt}" for dt in range(KT)] + [f"out{dt}" for dt in range(KT)]
    for f in range(FT):
        names += [f"fg{f}", f"fu{f}"]
    for dt in range(KT):
        names += [f"dn{dt}_{j}" for j in range(3)]
    return names


RING = 2
SPLIT = 3

PK = {}


def _pack_columns():
    at = 0
    for name, n in [("an", KT), ("fn", KT), ("qn", 1), ("kn12", 1), ("kn0", 1), ("on", 1), ("posk", 16),
                    ("posv", 16), ("lre", 8), ("lim", 8), ("ldt", 8), ("bre", 128), ("bim", 128), ("cre", 256),
                    ("cim", 256), ("dsk", 2), ("cw", 24), ("alog", 16), ("dtb", 16)]:
        PK[name] = (at, n)
        at += n
    return at


NPK = _pack_columns()
CK = {}


def _const_columns():
    at = 0
    for name, n in [("ident", P), ("ones", P), ("blk", P), ("le", P), ("ge", P), ("lt", P), ("negq", P),
                    ("negk", P), ("gt", P), ("lev", 7 * P), ("rot", P), ("freq", 1), ("cneg", NT * NCMP),
                    ("c01", NT * NCMP), ("t", P), ("tc", 8 * NT)]:
        CK[name] = (at, n)
        at += n
    return at


NCK = _const_columns()
NAMES = _slabs()
NSLAB = len(NAMES)
assert NSLAB % RING == 0
for _i, _n in enumerate(NAMES):
    SLAB[_n] = _i
ORD = [sum(n not in RAW for n in NAMES[:i]) for i in range(NSLAB + 1)]
POOL_END = SLAB["br3"]


def last_slab(unit):
    return SLAB["sbv1" if FILLERS[unit] == "sbv" else FILLERS[unit]]


def ahead(i):
    end = i + 1
    while end < NSLAB and ORD[end] - ORD[i + 1] < SPLIT:
        if NAMES[end] not in RAW and end >= 2 and end - 2 > i and NAMES[end - 2] in RAW:
            break
        end += 1
    return end


def program(nc, a_x, a_pos, a_const, a_pack, a_w, a_gates, a_out):
    with ExitStack() as ctx:
        sems = []

        def sem(name):
            s = ctx.enter_context(nc.semaphore(name))
            sems.append(s)
            return s

        PS = [ctx.enter_context(nc.psum_tensor(f"bank{i}", [P, 512], F32)) for i in range(8)]

        place = {}
        top = [nc.sbuf_base]

        def sb(name, shape, dt=F32, at=None, skip=0):
            size = int(np.prod(shape[1:])) * (2 if dt == BF16 else 4)
            if at is None:
                place[name] = top[0] = -(-top[0] // 32) * 32
                top[0] += size
            else:
                place[name] = place[at] + skip
            return nc.alloc_sbuf_tensor_at(name, shape, dt, offset=place[name])

        const = sb("const", [P, NCK])
        pack = sb("pack", [P, NPK])
        xT = sb("xT", [P, KT, S])
        hH = sb("hH", [P, KT, S], F32R)
        hL = sb("hL", [P, KT, S], F32R)
        gload = sb("gload", [P, 4, 4, S], at="hH")
        raw = sb("raw", [P, RING, KT, P])
        wH = sb("wH", [P, SPLIT, KT, P], F32R)
        wL = sb("wL", [P, SPLIT, KT, P], F32R)
        cosT = sb("cosT", [P, S])
        sinT = sb("sinT", [P, S])
        small = sb("small", [P, 632])
        negm16 = sb("negm16", [P, P], BF16)
        id16 = sb("id16", [P, P], BF16)
        kcv = sb("kcv", [P, 96])
        state = sb("state", [P, 2, HD])
        crot = sb("crot", [P, 2, 3, 256])
        turn4 = sb("turn4", [P, 2, 32])
        arena = sb("arena", [P, 12288])
        comp = sb("comp", [P, 4, S])
        bt = sb("bt", [P, NT, 2, 2, P], at="comp")
        pj = sb("pj", [P, NPJ, S])
        sbv = sb("sbv", [P, NT, 256])
        gst = sb("gst", [P, 2, S])
        oH = sb("oH", [P, 8, S], F32R, at="arena")
        oL = sb("oL", [P, 8, S], F32R, at="arena", skip=4 * 4096)
        mH = sb("mH", [P, KT, S], F32R, at="pj")
        mL_ = sb("mLow", [P, KT, S], F32R, at="pj", skip=4 * 4096)
        hidH = sb("hidH", [P, FT, S], F32R, at="arena")
        hidL = sb("hidL", [P, FT, S], F32R, at="pj")
        assert place["gst"] == place["pj"] + 4 * (NPJ * S + NT * 256) and top[0] <= nc.sbuf_usable_end

        def cst(name):
            at, n = CK[name]
            return const[:, at:at + n]

        def prm(name):
            at, n = PK[name]
            return pack[:, at:at + n]

        ident, ones, blk = cst("ident"), cst("ones"), cst("blk")
        lev = cst("lev").rearrange("p (l c) -> p l c", l=7)

        s_const = ctx.enter_context(nc.semaphore("const_loaded"))
        s_rope = ctx.enter_context(nc.semaphore("rope_step"))
        s_rope_sin = ctx.enter_context(nc.semaphore("rope_sines"))
        s_x = ctx.enter_context(nc.semaphore("x_loaded"))

        with nc.Block() as block:
            @block.sync
            def _(sp):
                sp.dma_start(const[:, :], a_const).then_inc(s_const, 16)
                sp.dma_start(cosT[:, :].bitcast(I32), a_pos).then_inc(s_const, 16)
                sp.dma_start(xT[:, :, :], a_x).then_inc(s_x, 16)
                sp.wait_ge(s_x, 16)

            @block.vector
            def _(v):
                n = [0]

                def step(ins):
                    n[0] += 1
                    ins.then_inc(s_rope, 1)
                    v.wait_ge(s_rope, n[0])

                v.wait_ge(s_const, 32)
                ang, k, r = arena[:, 0:512], arena[:, 512:1024], arena[:, 1024:1536]
                step(v.tensor_copy(k, cosT[:, :].bitcast(I32)))
                step(v.tensor_scalar(ang, k, cst("freq"), None, ALU.mult))
                step(v.tensor_scalar(r, ang, INV_2PI, ROUND, ALU.mult, ALU.add))
                step(v.tensor_scalar(k, r, ROUND, None, ALU.subtract))
                for c in (C1, C2, C3):
                    step(v.scalar_tensor_tensor(ang, k, -c, ang, ALU.mult, ALU.add))
                step(v.tensor_scalar(ang, ang, -3.1415925, 3.1415925, ALU.max, ALU.min))
                step(v.scalar_tensor_tensor(k, ang, -1.0, ang, ALU.mult, ALU.max))
                step(v.tensor_copy(negm16[:, :], cst("negq")))
                step(v.tensor_copy(id16[:, :], ident))

            @block.scalar
            def _(a):
                a.wait_ge(s_rope, 9)
                a.activation(sinT[:, :], arena[:, 0:512], ACT.Sin).then_inc(s_rope_sin, 1)
                a.activation(cosT[:, :], arena[:, 512:1024], ACT.Sin, bias=TWO_PI / 4, scale=-1.0).then_inc(s_rope_sin, 1)

        slab_loaded = [sem(f"slab_loaded{i}") for i in range(RING)]
        slab_taken = [sem(f"slab_taken{i}") for i in range(RING)]
        gate_stored = [sem(f"gate_stored{i}") for i in range(2)]
        gate_back = [sem(f"gate_back{i}") for i in range(4)]
        q = {n: sem(n) for n in """
            pack_loaded slab_done proj_taken dve_step act_step 
            bpad_ready bt_ps bt_taken abc_done sm_ps sm_ready trig_done
            sq_ready ss_ps rstd_ready h_tmp h_high h_ready
            w_high sbv_half
            blocks_ready cmp_nat cmp_nat_ready cmp_hid cmp1_ps  kc_ready
            sig_exp sig_ready xa_neg xa_ln g_ready gsum_ps gsum_taken gexp_ready
            conv_ready tanh_ready silu_ready sqk_ready qkss_ps qk_rstd qk_ready
            grow_ps args_ready grow_exp qd_ready tr_ps tr_taken dexp_ready dmask_ready
            skk_ps l_part skq_ps at_part y0_ps u0_ready t0_ps t0_ready
            y_ps y_ready du_ps u_ready dt_ps t_ready wt_ps wt_ready
            vn_ps vn_ready o_ps o_taken su_ps st_ready
            head_sq head_ss head_rstd z_tanh gdn_done
            tab_ready sin_ready bu_ps m_ready w_ready z_ready n_ready x_ready y5_ps y5_ready y5_sq y5_tanh
            gy_ready s5_done
            sbz_ps z_copied nb_ready sp_exp sp_ln sp_ready sp_masked cum_ps d_ready d_masked wexp_ready sbpv_ps sb_done
            qn_ready rot_ps t_sin t_cos rot_ready kdup_ready vt_ps vt_ready
            sc_cmp_ps cmp_arg cmp_exp pc_ready pct_ps pct_ready
            sc_ps nm_ready p_ready pt_ps pt_ready pv_ps onat_ready ot_ps nsa_done
            gate_tanh br_ps br_taken merged_part merged_sum merged_high merged_ready o_high o_low
            xo_ready
            fg_tanh ga_ready hid_tmp hid_high hid_ready dn_taken""".split()}

        pjt = {n: pj[:, TI[n], :] for n in KEPT}
        t2k, t2v = comp[:, 0, :], comp[:, 1, :]
        bk = comp[:, 2, 0:496].rearrange("p (b n) -> p b n", b=16)
        bv = comp[:, 3, 0:496].rearrange("p (b n) -> p b n", b=16)

        def scol(at, n):
            return small[:, at:at + n]

        sm_all = scol(0, 80).rearrange("p (t c) -> p t c", c=20)
        e_sig = scol(80, 64).rearrange("p (t c) -> p t c", c=16)
        sig = scol(144, 64).rearrange("p (t c) -> p t c", c=16)
        xa, na, ea, g16, gc, gl, egc, egl, kdc, bg, la = (scol(208 + 16 * i, 16) for i in range(11))
        s5c = [scol(384 + 8 * i, 8) for i in range(24)]

        def unit(tt, h):
            return (tt // 2) * 8 + (h % 2) * 4 + (tt % 2) * 2 + h // 2

        UNITS = [(tt, h) for b in range(4) for tt in (2 * (b // 2), 2 * (b // 2) + 1) for h in (b % 2, b % 2 + 2)]
        mats = [arena[:, 2048 * i:2048 * (i + 1)].rearrange("p (u c) -> p u c", u=16) for i in range(4)]
        mL, mU, mT, mY = mats
        cv = arena[:, 8192:11264].rearrange("p (t s) -> p t s", t=6)
        aT = arena[:, 8192:10240].rearrange("p (u c) -> p u c", u=16)
        qd = arena[:, 11264:12288].rearrange("p (t s) -> p t s", t=2)
        kbg, vb, kdec = (pj[:, 2 * i:2 * i + 2, :].rearrange("p a (t c) -> p (a t) c", t=2) for i in range(3))
        vn = arena[:, 4096:4352].rearrange("p (h e) -> p h e", h=4)
        wt = arena[:, 4608:5632].rearrange("p (t i c) -> p t i c", t=4, i=2)
        o_raw = arena[:, 0:1024].rearrange("p (i s) -> p i s", i=2)
        o_sq = arena[:, 1024:2048].rearrange("p (i s) -> p i s", i=2)
        o_rs = arena[:, 2048:3072].rearrange("p (i s) -> p i s", i=2)
        z_th = arena[:, 3072:4096].rearrange("p (i s) -> p i s", i=2)
        gdn_out = pj[:, TI["z0"]:TI["z0"] + 2, :]
        s5_out = pj[:, TI["u0"]:TI["u0"] + 2, :]
        sb_out = pj[:, TI["sb0"]:TI["sb0"] + 2, :]
        nsa_out = pj[:, TI["q0"]:TI["q0"] + 2, :]
        mixed = [nsa_out, s5_out, gdn_out, sb_out]

        def half(h):
            return slice(HD * (h % 2), HD * (h % 2) + HD)
        (dt5, theta, lrdt, tmp1, thr, thabs, uh, ul, den, mag, sina, cosa, abr, abi, tmp2, fre, fim) = s5c[:17]
        q8 = scol(384 + 8 * 17, 1)
        nm, nsum, nfac, nc1 = scol(544, 32), scol(576, 32), scol(608, 8), scol(616, 16)
        GC0 = 272
        mL_flat, mU_flat, mT_flat, mY_flat = (arena[:, 2048 * i:2048 * (i + 1)] for i in range(4))
        aT_flat = arena[:, 8192:10240]
        rs1 = arena[:, 1024:1536]
        hs = arena[:, 4096:8192].rearrange("p (k s) -> p k s", k=KT)
        th = arena[:, 0:3072].rearrange("p (t s) -> p t s", t=6)
        sqk = mT_flat.rearrange("p (t s) -> p t s", t=4)
        rqk = mY_flat.rearrange("p (t s) -> p t s", t=4)
        cx, ct, cmp_flat = comp[:, 0, 0:124], comp[:, 0, 128:252], comp[:, 0, 256:380]
        cmp_h = cmp_flat.rearrange("p (c n) -> p c n", c=4)
        cmpT = comp[:, 1, :]
        kc_s, kc_r = comp[:, 0, 384:415], comp[:, 0, 416:447]
        kcT, vc = kcv[:, 0:NCMP], kcv[:, 32:96]

        def tiles(at, n):
            return arena[:, at:at + S * n].rearrange("p (t s) -> p t s", t=n)

        s5_sin, s5_cos = (arena[:, 6144 + 1024 * i:7168 + 1024 * i].rearrange("p (i t) -> p i t", i=8) for i in range(2))
        s5_tmp = arena[:, 10240:11264].rearrange("p (i t) -> p i t", i=8)
        sin4, cos4, tmp4 = (x.rearrange("p (c i) -> p c i", c=NT)
                            for x in (turn4[:, 0, :], turn4[:, 1, :], arena[:, 3072:3104]))
        bpad = arena[:, 2048:4096].rearrange("p (c r i s) -> p c r i s", c=NT, r=2, i=8)
        smT = arena[:, 0:512]

        def s5_m(i, j):
            return arena[:, 2048 * (i % 3) + S * j:2048 * (i % 3) + S * j + S]

        def s5_z(i, j):
            return arena[:, 8192 + 1024 * (i % 2) + S * j:8192 + 1024 * (i % 2) + S * j + S]

        y5a, y5b, gy = tiles(8192, 2), tiles(9216, 2), tiles(10240, 2)

        def sb_z(h, kb):
            return arena[:, 2048 * (h % 2) + S * kb:2048 * (h % 2) + S * kb + S]

        def sb_sp(h, kb):
            return arena[:, 4096 + 2048 * (h % 2) + S * kb:4096 + 2048 * (h % 2) + S * kb + S]

        def sb_e(n):
            return pj[:, n % 4, :]

        nqn, nqr, nsq, nrs, kdup = tiles(0, 3), tiles(1536, 3), tiles(3072, 3), tiles(4608, 3), tiles(6144, 2)
        nts = nsq
        nP, npt = (tiles(7168, 4), pj[:, 0:4, :]), tiles(9216, 4)
        nvt = arena[:, 11264:11776].rearrange("p (t c) -> p t c", t=4)
        npc_flat = arena[:, 4608:5104]
        npc = npc_flat.rearrange("p (u n) -> p u n", u=16)
        npct = arena[:, 5120:5632]
        nO, nO2 = arena[:, 5632:5888], arena[:, 5888:6144]
        PTN = [sum(m // 2 + 1 for m in range(k)) for k in range(2 * NT + 1)]
        mtmp = arena[:, 8192:12288].rearrange("p (a m s) -> p a m s", a=2, m=4)
        hs2 = arena[:, 8192:12288].rearrange("p (k s) -> p k s", k=KT)
        rs2 = arena[:, 0:512]
        ft, fa, fh = comp[:, 0:2, :], comp[:, 2:4, :], tiles(11264, 2)

        with nc.Fori(0, DEPTH) as layer:
            with nc.Block() as block:

                @block.sync
                def _(sp):
                    sp.dma_start(pack[:, :], a_pack[layer]).then_inc(q["pack_loaded"], 16)
                    for s in range(RING):
                        sp.dma_start(raw[:, s], a_w[layer, s].rearrange("p (k c) -> p k c", k=KT)).then_inc(slab_loaded[s], 16)
                    with sp.Fori(1, NSLAB // RING) as r:
                        for s in range(RING):
                            sp.wait_ge(slab_taken[s], r)
                            sp.dma_start(raw[:, s], a_w[layer, r * RING + s].rearrange("p (k c) -> p k c", k=KT))\
                              .then_inc(slab_loaded[s], 16)
                    for s in range(RING):
                        sp.wait_ge(slab_loaded[s], 16 * (NSLAB // RING))

                @block.tensor
                def _(pe):
                    mm = nc.tensor.matmul
                    used = [0]

                    def raw_slab(name):
                        i = SLAB[name]
                        assert i == used[0] and name in RAW, (name, i, used[0])
                        used[0] += 1
                        pe.wait_ge(slab_loaded[i % RING], 16 * (i // RING + 1))
                        return raw[:, i % RING].rearrange("p k c -> p (k c)")

                    def raw_used(ins, name):
                        ins.then_inc(q["slab_done"], 1)
                        pe.wait_ge(q["slab_done"], SLAB[name] + 1)
                        pe.sem_inc(slab_taken[SLAB[name] % RING], 1)

                    def slab(name):
                        i = SLAB[name]
                        assert i == used[0] and name not in RAW, (name, i, used[0])
                        used[0] += 1
                        pe.wait_ge(slab_taken[i % RING], i // RING + 1)
                        return wH[:, ORD[i] % SPLIT], wL[:, ORD[i] % SPLIT]

                    def mm3(out, a, b, start, stop):
                        mm(out, a[0], b[0], start=start, stop=False)
                        mm(out, a[0], b[1], start=False, stop=False)
                        return mm(out, a[1], b[0], start=False, stop=stop)

                    def parts(pair, *at):
                        return pair[0][at], pair[1][at]

                    h2p = (hH[:, :, :], hL[:, :, :])
                    ALLP = slice(None)

                    turn = [0]

                    def stream_bank():
                        n = turn[0]
                        turn[0] += 1
                        if n >= 2:
                            pe.wait_ge(q["proj_taken"], n - 1)
                        return PS[n % 2]

                    def column_tile(name):
                        w = slab(name)
                        b = stream_bank()
                        for k in range(KT):
                            last = mm3(b[:, :], parts(w, ALLP, k), parts(h2p, ALLP, k), k == 0, k == KT - 1)
                        last.then_inc(q["slab_done"], 1)

                    def values():
                        wv = [[x.rearrange("p k c -> p (k c)").rearrange("p (k c) -> p k c", k=4) for x in slab(n)]
                              for n in ("sbv0", "sbv1")]
                        for tp in range(2):
                            b = stream_bank()
                            for t in range(2):
                                for k in range(KT):
                                    c = slice(P * (2 * tp + t), P * (2 * tp + t) + P)
                                    last = mm3(b[:, 256 * t:256 * t + 256], parts(h2p, ALLP, k, c),
                                               parts(wv[k // 4], ALLP, k % 4), k == 0, k == KT - 1)
                                    if tp == 1 and t == 1 and k == 3:
                                        last.then_inc(q["slab_done"], 1)
                            if tp == 0:
                                last.then_inc(q["sbv_half"], 1)
                        last.then_inc(q["slab_done"], 1)

                    filled = [0]

                    def fill(n):
                        for _ in range(n):
                            name = FILLERS[filled[0]]
                            values() if name == "sbv" else column_tile(name)
                            filled[0] += 1

                    for k in range(KT):
                        pe.wait_ge(q["sq_ready"], k + 1)
                        last = mm(PS[6][:, :], ones, hs[:, k, :], start=(k == 0), stop=(k == KT - 1))
                    last.then_inc(q["ss_ps"], 1)
                    w = [x.rearrange("p k c -> p (k c)")[:, 0:KT * 20].rearrange("p (k c) -> p k c", k=KT)
                         for x in slab("small")]
                    b = stream_bank()
                    w0 = slab(FIRST[0][0])
                    b0 = stream_bank()
                    for k in range(KT):
                        pe.wait_ge(q["h_ready"], k + 1)
                        last = mm3(b[0:20, :], parts(w, ALLP, k), parts(h2p, ALLP, k), k == 0, k == KT - 1)
                        if k == KT - 1:
                            last.then_inc(q["slab_done"], 1)
                        last = mm3(b0[:, :], parts(w0, ALLP, k), parts(h2p, ALLP, k), k == 0, k == KT - 1)
                    last.then_inc(q["slab_done"], 1)
                    for i, (name, _) in enumerate(FIRST):
                        if i:
                            column_tile(name)
                        if i == 1:
                            pe.wait_ge(q["proj_taken"], 1)
                            for t in range(NT):
                                last = nc.tensor.transpose(PS[7][:, 20 * t:20 * t + 20], smT[0:20, P * t:P * t + P],
                                                           ident[0:20, 0:20])
                            last.then_inc(q["sm_ps"], 1)

                    for kv, blocks in enumerate((bk, bv)):
                        for j in range(4):
                            fill(FILL["blocks"][4 * kv + j])
                            if kv + j == 0:
                                pe.wait_ge(q["blocks_ready"], 4)
                                pe.wait_ge(q["sm_ready"], 1)
                            name = f"c{'kv'[kv]}{j}"
                            w = raw_slab(name).rearrange("p (k c) -> p k c", k=4)
                            for i in range(4 * j, 4 * j + 4):
                                last = mm(PS[6 + kv][0:NCMP, 0:256], blocks[:, i, :], w[:, i % 4, :],
                                          start=(i == 0), stop=(i == 15))
                            raw_used(last, name)
                    fill(FILL["hidden"])
                    pe.wait_ge(q["cmp_nat_ready"], 2)
                    for c in range(4):
                        last = nc.tensor.transpose(PS[5][:, 31 * c:31 * c + 31], cmpT[0:NCMP, P * c:P * c + P],
                                                   ident[0:NCMP, 0:NCMP])
                    last.then_inc(q["cmp_nat"], 1)
                    fill(FILL["gelu"])
                    w = raw_slab("cw2")
                    pe.wait_ge(q["cmp_hid"], 1)
                    for hc in range(2):
                        mm(PS[7][:, 128:159], w[:, P * hc:P * hc + P], cmp_h[:, hc, :], start=(hc == 0), stop=(hc == 1))
                    for hc in range(2):
                        last = mm(PS[7][0:31, 192:256], cmp_h[:, 2 + hc, :], w[:, 256 + HD * hc:256 + HD * hc + HD],
                                  start=(hc == 0), stop=(hc == 1))
                    raw_used(last, "cw2")
                    pe.wait_ge(q["head_sq"], 1)
                    mm(PS[7][:, 320:351], blk, kc_s, start=True, stop=True).then_inc(q["head_ss"], 1)

                    def turn_inputs(c):
                        if c == 0:
                            pe.wait_ge(q["bpad_ready"], 1)
                            pe.wait_ge(q["head_rstd"], 1)
                        else:
                            pe.wait_ge(q["bt_taken"], c)
                        for r in range(2):
                            for t in range(2):
                                last = nc.tensor.transpose(PS[7][:, (2 * r + t) * P:(2 * r + t + 1) * P],
                                                           bpad[:, c, r, 4 * t:4 * t + 4, :].rearrange("p i s -> p (i s)"),
                                                           ident)
                        last.then_inc(q["bt_ps"], 1)

                    fill(FILL["gsum"])
                    pe.wait_ge(q["g_ready"], 1)
                    mm(PS[2][:, 0:16], cst("le"), g16, start=True, stop=True)
                    mm(PS[2][:, 16:32], ones, g16, start=True, stop=True).then_inc(q["gsum_ps"], 1)
                    for i in range(4):
                        pe.wait_ge(q["sqk_ready"], i + 1)
                        if i == 3:
                            pe.wait_ge(q["rstd_ready"], 1)
                        mm(PS[3 + i][:, :], blk, mT_flat[:, S * i:S * i + S], start=True, stop=True).then_inc(q["qkss_ps"], 1)
                    fill(FILL["qk"])
                    turn_inputs(0)
                    for b in range(4):
                        pe.wait_ge(q["qk_rstd"], b + 1)
                        for j, (tt, h) in enumerate(UNITS[4 * b:4 * b + 4]):
                            last = mm(PS[3 + b][:, P * j:P * j + P], g16[:, 4 * tt + h:4 * tt + h + 1].broadcast_to([P, P]),
                                      cst("le"), start=True, stop=True)
                        last.then_inc(q["grow_ps"], 1)
                    fill(FILL["grow"])
                    turn_inputs(1)
                    pe.wait_ge(q["qk_ready"], 4)
                    for b in range(4):
                        pe.wait_ge(q["grow_exp"], b + 1)
                        for t in range(2):
                            for i in range(2):
                                tt = 2 * (b % 2) + t
                                last = nc.tensor.transpose(PS[3 + b][:, 256 * t + P * i:256 * t + P * i + P],
                                                           cv[:, 2 + 2 * (b // 2) + i, P * tt:P * tt + P], ident)
                        last.then_inc(q["tr_ps"], 1)
                    fill(FILL["turn"])
                    turn_inputs(2)
                    for other, done in ((2, "skk_ps"), (0, "skq_ps")):
                        for b in range(4):
                            if other == 2:
                                pe.wait_ge(q["tr_taken"], [1, 2, 3, 4][b])
                            else:
                                pe.wait_ge(q["l_part"], b + 1)
                            for j, (tt, h) in enumerate(UNITS[4 * b:4 * b + 4]):
                                last = mm(PS[3 + b][:, P * j:P * j + P], cv[half(h), 2 + h // 2, P * tt:P * tt + P],
                                          cv[half(h), other + h // 2, P * tt:P * tt + P], start=True, stop=True)
                            last.then_inc(q[done], 1)
                    fill(FILL["skq"])
                    turn_inputs(3)
                    for b in range(4):
                        pe.wait_ge(q["at_part"], b + 1)
                        for j in range(4):
                            last = nc.tensor.transpose(PS[3 + b][:, P * j:P * j + P], mL[:, 4 * b + j, :], ident)
                        last.then_inc(q["y0_ps"], 1)
                    for b in range(4):
                        pe.wait_ge(q["u0_ready"], 2 * b + 2)
                        for j in range(4):
                            last = nc.tensor.transpose(PS[3 + b][:, P * j:P * j + P], mY[:, 4 * b + j, :], ident)
                        last.then_inc(q["t0_ps"], 1)

                    def y_product(n):
                        b = n % 4
                        if n >= 4:
                            pe.wait_ge(q["u_ready"], n - 3)
                        else:
                            pe.wait_ge(q["t0_ready"], 4)
                        if n >= 2:
                            pe.wait_ge(q["y_ready"], n - 1)
                        for j in range(4):
                            last = mm(PS[2 + n % 2][:, P * j:P * j + P], mL[:, 4 * b + j, :], mU[:, 4 * b + j, :],
                                      start=True, stop=True)
                        last.then_inc(q["y_ps"], 1)

                    def ut_product(n):
                        b = n % 4
                        pe.wait_ge(q["y_ready"], n + 1)
                        if n >= 4:
                            pe.wait_ge(q["t_ready"], n - 3)
                        if n >= 2:
                            pe.wait_ge(q["u_ready"], n - 1)
                        for j in range(4):
                            last = mm(PS[4 + n % 2][:, P * j:P * j + P], mT[:, 4 * b + j, :], mY[:, 4 * b + j, :],
                                      start=True, stop=True)
                        last.then_inc(q["du_ps"], 1)
                        if n < 20:
                            if n >= 2:
                                pe.wait_ge(q["t_ready"], n - 1)
                            for j in range(4):
                                last = mm(PS[6 + n % 2][:, P * j:P * j + P], mY[:, 4 * b + j, :], mT[:, 4 * b + j, :],
                                          start=True, stop=True)
                            last.then_inc(q["dt_ps"], 1)

                    pe.wait_ge(q["kc_ready"], 1)
                    pe.wait_ge(q["bt_taken"], NT)
                    for lv in range(6):
                        y_product(4 * lv)
                        y_product(4 * lv + 1)
                        ut_product(4 * lv)
                        y_product(4 * lv + 2)
                        ut_product(4 * lv + 1)
                        y_product(4 * lv + 3)
                        ut_product(4 * lv + 2)
                        ut_product(4 * lv + 3)
                        fill(FILL["level"][lv])
                    pe.wait_ge(q["u_ready"], 24)
                    for tt in range(NT):
                        bank = PS[2 + tt]
                        for h in range(H):
                            last = mm(bank[half(h), P * (h // 2):P * (h // 2) + P], kbg[:, tt, HD * h:HD * h + HD],
                                      mU[:, unit(tt, h), :], start=True, stop=True)
                        last.then_inc(q["wt_ps"], 1)
                    pe.wait_ge(q["wt_ready"], NT)
                    for tt in range(NT):
                        if tt:
                            pe.wait_ge(q["st_ready"], 4 * tt + 1)
                            pe.wait_ge(q["vn_ready"], 2 * tt)
                            pe.wait_ge(q["o_taken"], 2 * tt)
                        else:
                            pe.wait_ge(q["st_ready"], 1)
                        for h in range(H):
                            out = PS[2 + h % 2][:, HD * (h // 2):HD * (h // 2) + HD]
                            mm(out, mU[:, unit(tt, h), :], vb[:, tt, HD * h:HD * h + HD], start=True, stop=False)
                            last = mm(out, wt[half(h), tt, h // 2, :], state[half(h), h // 2, :], start=False, stop=True)
                        last.then_inc(q["vn_ps"], 1)
                        if tt == 0:
                            pe.wait_ge(q["qd_ready"], 8)
                        pe.wait_ge(q["vn_ready"], 2 * tt + 2)
                        for h in range(H):
                            out = PS[6 + h % 2][half(h), P * (h // 2):P * (h // 2) + P]
                            mm(out, state[half(h), h // 2, :], qd[half(h), h // 2, P * tt:P * tt + P], start=True, stop=False)
                            last = mm(out, vn[:, h, :], aT[:, unit(tt, h), :], start=False, stop=True)
                        last.then_inc(q["o_ps"], 1)
                        for h in range(H):
                            out = PS[4 + h % 2][half(h), HD * (h // 2):HD * (h // 2) + HD]
                            last = mm(out, kdec[:, tt, HD * h:HD * h + HD], vn[:, h, :], start=True, stop=True)
                        last.then_inc(q["su_ps"], 1)
                        fill(FILL["chunk"][tt])
                    for i in range(2):
                        pe.wait_ge(q["head_sq"], 1 + i + 1)
                        mm(PS[2 + i][:, :], blk, o_sq[:, i, :], start=True, stop=True).then_inc(q["head_ss"], 1)
                    fill(FILL["oss"])

                    pe.wait_ge(q["head_rstd"], 3)
                    pe.wait_ge(q["st_ready"], 17)
                    pe.wait_ge(q["bpad_ready"], 2)

                    def s5_inputs(i):
                        if i >= 2:
                            pe.wait_ge(q["m_ready"], i - 1)
                        j = 32 * (i % 4)
                        for r in range(2):
                            for c in range(NT):
                                last = mm(PS[2 + 2 * (i % 2) + r][:, P * c:P * c + P], bt[j:j + 32, c, r, i // 4, :],
                                          pj[j:j + 32, TI["u0"] + i // 4, P * c:P * c + P], start=True, stop=True)
                        last.then_inc(q["bu_ps"], 1)

                    def s5_outputs(k):
                        pe.wait_ge(q["x_ready"], 2 * k + 2)
                        for c in range(NT):
                            out = PS[6 + k // 4][32 * (k % 4):32 * (k % 4) + 32, P * c:P * c + P]
                            for r, (name, m) in enumerate((("cre", 0), ("cim", 2))):
                                w = crot[:, r, c - 1, 32 * k:32 * k + 32] if c else prm(name)[:, 32 * k:32 * k + 32]
                                last = mm(out, w, s5_m(k, m)[:, P * c:P * c + P], start=(r == 0), stop=(r == 1))
                        last.then_inc(q["y5_ps"], 1)

                    s5_inputs(0)
                    for i in range(8):
                        if i < 7:
                            s5_inputs(i + 1)
                        fill(FILL["s5"][i])
                        if i == 0:
                            pe.wait_ge(q["o_taken"], 8)
                        else:
                            s5_outputs(i - 1)
                    s5_outputs(7)
                    fill(FILL["glu"])
                    pe.wait_ge(q["gy_ready"], 2)
                    w = raw_slab("glu").rearrange("p (k c) -> p k c", k=2)
                    for m in range(4):
                        for k in range(2):
                            last = mm(PS[4 + m][:, :], w[:, k, P * m:P * m + P], gy[:, k, :], start=(k == 0), stop=(k == 1))
                    raw_used(last, "glu")

                    def sb_scores(n):
                        h, kb = n // 4, 3 - n % 4
                        if n >= 2:
                            pe.wait_ge(q["z_copied"], n - 1)
                        i = h // 2
                        mm(PS[2 + n % 2][:, 0:S - P * kb], pjt[f"sb{2 + i}"][half(h), P * kb:P * kb + P],
                           pjt[f"sb{i}"][half(h), P * kb:S], start=True, stop=True).then_inc(q["sbz_ps"], 1)

                    def sb_sums(n):
                        h, kb = n // 4, 3 - n % 4
                        pe.wait_ge(q["sp_masked"], n + 1)
                        if n >= 2:
                            pe.wait_ge(q["d_ready"], n - 1)
                        out = PS[4 + n % 2]
                        for j in range(kb, NT):
                            last = mm(out[:, P * (j - kb):S - P * kb], cst("ge") if j == kb else ones,
                                      sb_sp(h, j)[:, P * j:S], start=(j == kb), stop=(j == NT - 1), skip_group_check=True)
                        last.then_inc(q["cum_ps"], 1)

                    def sb_values(h):
                        pe.wait_ge(q["wexp_ready"], 4 * h + 4)
                        if h >= 2:
                            pe.wait_ge(q["sb_done"], h - 1)
                        for kb in range(NT):
                            last = mm(PS[6 + h % 2][half(h), P * kb:S], sbv[:, kb, HD * h:HD * h + HD],
                                      sb_z(h, kb)[:, P * kb:S], start=(kb == 0), stop=(kb == NT - 1), skip_group_check=True)
                        last.then_inc(q["sbpv_ps"], 1)

                    for h in range(H + 1):
                        if h < H:
                            for j in range(4):
                                sb_scores(4 * h + j)
                        if h == 1:
                            pe.wait_ge(q["s5_done"], 2)
                        if h:
                            for j in range(4):
                                sb_sums(4 * h - 4 + j)
                        fill(FILL["sb"][h])
                        if h:
                            sb_values(h - 1)

                    for i in range(3):
                        pe.wait_ge(q["head_sq"], 3 + i + 1)
                        mm(PS[2 + i][:, :], blk, nsq[:, i, :], start=True, stop=True).then_inc(q["head_ss"], 1)
                    for t in range(NT):
                        last = nc.tensor.transpose(PS[5][:, P * t:P * t + P], pjt["vsvw"][:, P * t:P * t + P], ident)
                    last.then_inc(q["vt_ps"], 1)
                    fill(FILL["norms"])
                    for i in range(3):
                        pe.wait_ge(q["qn_ready"], i + 1)
                        mm(PS[2 + i][:, :], cst("rot"), nqn[:, i, :], start=True, stop=True).then_inc(q["rot_ps"], 1)
                    for par in range(2):
                        for tt in range(NT):
                            for i in range(2):
                                c = NCMP * (2 * tt + i)
                                last = mm(PS[6 + par][:, c:c + NCMP], nqn[HD * par:HD * par + HD, i, P * tt:P * tt + P],
                                          kcT[HD * par:HD * par + HD, :], start=True, stop=True)
                        last.then_inc(q["sc_cmp_ps"], 1)
                    fill(FILL["rot"])
                    pe.wait_ge(q["kdup_ready"], 2)
                    pe.wait_ge(q["rot_ready"], 4)
                    pe.wait_ge(q["vt_ready"], 1)
                    pe.wait_ge(q["t_sin"], 3)
                    pe.wait_ge(q["pc_ready"], 1)

                    def nsa_transpose(m):
                        qt = m // 2
                        pe.wait_ge(q["p_ready"], 4 * m + 4)
                        for kb in range(qt + 1):
                            x = PTN[m] + kb
                            if x >= 2:
                                pe.wait_ge(q["pt_ready"], x - 1)
                            for h in range(H):
                                last = nc.tensor.transpose(PS[4 + x % 2][:, P * h:P * h + P], nP[m % 2][:, h, P * kb:P * kb + P], ident)
                            last.then_inc(q["pt_ps"], 1)

                    def nsa_scores(m, heads):
                        qt, br = m // 2, m % 2
                        wid = P * (qt + 1)
                        for h in heads:
                            x = 4 * m + h
                            if x >= 2:
                                pe.wait_ge(q["p_ready"], x - 1)
                            out = PS[2 + h % 2]
                            mm(out[:, 0:wid], nqr[half(h), h // 2, P * qt:P * qt + P], kdup[half(h), br, 0:wid],
                               start=True, stop=False, skip_group_check=True)
                            mm(out[:, wid - P:wid], id16[:, :], negm16[:, :], start=False, stop=True,
                               skip_group_check=True).then_inc(q["sc_ps"], 1)

                    def nsa_output(qt):
                        pe.wait_ge(q["onat_ready"], qt + 1)
                        for i in range(2):
                            last = nc.tensor.transpose(PS[6][:, P * i:P * i + P], nO[:, P * i:P * i + P], ident)
                        last.then_inc(q["ot_ps"], 1)

                    nsa_scores(0, range(H))
                    for m in range(2 * NT):
                        qt, br = m // 2, m % 2
                        if m + 1 < 2 * NT:
                            nsa_scores(m + 1, (0, 1))
                        nsa_transpose(m)
                        if m + 1 < 2 * NT:
                            nsa_scores(m + 1, (2, 3))
                        if br == 0:
                            if qt:
                                nsa_output(qt - 1)
                            for h in range(H):
                                u = 8 * (h % 2) + 2 * qt + h // 2
                                last = nc.tensor.transpose(PS[7][0:NCMP, P * h:P * h + P], npc[:, u, :], ident)
                            last.then_inc(q["pct_ps"], 1)
                        fill(FILL["nsa"][m])
                        if br == 0:
                            pe.wait_ge(q["pct_ready"], qt + 1)
                            if qt:
                                pe.wait_ge(q["nsa_done"], qt)
                            for h in range(H):
                                last = mm(PS[6][:, 256 + HD * h:256 + HD * h + HD], npct[0:NCMP, P * h:P * h + P],
                                          vc[0:NCMP, :], start=True, stop=True)
                        pe.wait_ge(q["pt_ready"], PTN[m] + qt + 1)
                        for h in range(H):
                            for kb in range(qt + 1):
                                last = mm(PS[6 + br][:, HD * h:HD * h + HD], npt[:, kb, P * h:P * h + P],
                                          nvt[:, kb, HD * br:HD * br + HD], start=(kb == 0), stop=(kb == qt))
                        last.then_inc(q["pv_ps"], 1)
                    nsa_output(NT - 1)
                    assert filled[0] == len(FILLERS)

                    for dt in range(KT):
                        w = [x.rearrange("p (m k) c -> p m k c", m=4) for x in slab(f"br{dt}")]
                        for m in range(4):
                            x = 4 * dt + m
                            if x >= 6:
                                pe.wait_ge(q["br_taken"], x - 5)
                            for k in range(2):
                                if dt == 0:
                                    pe.wait_ge(q["o_low"], 2 * m + k + 1)
                                last = mm3(PS[2 + x % 6][:, :], parts(w, ALLP, m, k), parts((oH, oL), ALLP, 2 * m + k),
                                           k == 0, k == 1)
                            last.then_inc(q["slab_done"] if m == 3 else q["br_ps"], 1)
                    for dt in range(KT):
                        w = slab(f"out{dt}")
                        b = PS[dt % 2]
                        if dt >= 2:
                            pe.wait_ge(q["xo_ready"], dt - 1)
                        for k in range(KT):
                            if dt == 0:
                                pe.wait_ge(q["merged_ready"], k + 1)
                            last = mm3(b[:, :], parts(w, ALLP, k), parts((mH, mL_), ALLP, k), k == 0, k == KT - 1)
                        last.then_inc(q["slab_done"], 1)
                    for k in range(KT):
                        pe.wait_ge(q["sq_ready"], KT + k + 1)
                        last = mm(PS[2][:, :], ones, hs2[:, k, :], start=(k == 0), stop=(k == KT - 1))
                    last.then_inc(q["ss_ps"], 1)
                    w = [slab("fg0"), slab("fu0")]
                    for k in range(KT):
                        pe.wait_ge(q["h_ready"], KT + k + 1)
                        for j in range(2):
                            last = mm3(PS[j][:, :], parts(w[j], ALLP, k), parts(h2p, ALLP, k), k == 0, k == KT - 1)
                            if k == KT - 1:
                                last.then_inc(q["slab_done"], 1)
                    for f in range(1, FT):
                        for j, name in enumerate(("fg", "fu")):
                            w = slab(f"{name}{f}")
                            b = PS[2 * (f % 4) + j]
                            if f >= 4:
                                pe.wait_ge(q["hid_tmp"], f - 3)
                            for k in range(KT):
                                last = mm3(b[:, :], parts(w, ALLP, k), parts(h2p, ALLP, k), k == 0, k == KT - 1)
                            last.then_inc(q["slab_done"], 1)
                    for dt in range(KT):
                        b = PS[4 + dt % 4]
                        if dt >= 4:
                            pe.wait_ge(q["dn_taken"], dt - 3)
                        elif dt == 0:
                            pe.wait_ge(q["hid_tmp"], FT - 2)
                        for j in range(3):
                            w = slab(f"dn{dt}_{j}")
                            n = min(KT, FT - KT * j)
                            for k in range(n):
                                if dt == 0:
                                    pe.wait_ge(q["hid_ready"], KT * j + k + 1)
                                last = mm3(b[:, :], parts(w, ALLP, k), parts((hidH, hidL), ALLP, KT * j + k),
                                           j == 0 and k == 0, j == 2 and k == n - 1)
                            last.then_inc(q["slab_done"], 1)
                    assert used[0] == NSLAB

                @block.scalar
                def _(a):
                    act = nc.scalar.activation
                    chain = [0]

                    def step(ins):
                        chain[0] += 1
                        ins.then_inc(q["act_step"], 1)
                        a.wait_ge(q["act_step"], chain[0])

                    turn = [0]

                    def stream(name):
                        n = turn[0]
                        turn[0] += 1
                        a.wait_ge(q["slab_done"], SLAB[name] + 1)
                        return PS[n % 2]

                    split = [0]

                    def high_to(end):
                        while split[0] < end:
                            i = split[0]
                            split[0] += 1
                            if NAMES[i] in RAW:
                                continue
                            a.wait_ge(slab_loaded[i % RING], 16 * (i // RING + 1))
                            if ORD[i] >= SPLIT:
                                a.wait_ge(q["slab_done"], ORD.index(ORD[i] - SPLIT + 1))
                            act(wH[:, ORD[i] % SPLIT], raw[:, i % RING], ACT.Copy).then_inc(q["w_high"], 1)

                    def evacuate(out, name, scale=1.0):
                        act(out, stream(name)[:, :], ACT.Copy, scale=scale).then_inc(q["proj_taken"], 1)
                        high_to(ahead(SLAB[name]))

                    filled = [0]

                    def fill(n):
                        for _ in range(n):
                            name = FILLERS[filled[0]]
                            filled[0] += 1
                            if name == "sbv":
                                for tp in range(2):
                                    if tp == 0:
                                        a.wait_ge(q["sbv_half"], 1)
                                        b = PS[turn[0] % 2]
                                        turn[0] += 1
                                    else:
                                        b = stream("sbv1")
                                    act(sbv[:, 2 * tp:2 * tp + 2, :], b[:, :].rearrange("p (t c) -> p t c", t=2), ACT.Copy)\
                                        .then_inc(q["proj_taken"], 1)
                                high_to(ahead(SLAB["sbv1"]))
                            elif name in TI:
                                evacuate(pjt[name], name, 0.125 if name in ("sb0", "sb1") else 1.0)
                            else:
                                g = int(name[4:])
                                if g >= 2:
                                    a.wait_ge(gate_stored[g % 2], 16 * (g // 2))
                                evacuate(gst[:, g % 2, :], name)
                                a.wait_ge(q["proj_taken"], turn[0])
                                a.dma_start(a_gates[g // 4, :, g % 4, :], gst[:, g % 2, :]).then_inc(gate_stored[g % 2], 16)

                    def rsqrt(out, src, count, done):
                        step(act(out, src, ACT.Ln, bias=EPS, scale=1.0 / count))
                        act(out, out, ACT.Exp, scale=-0.5).then_inc(done, 1)

                    def rsqrts(out, n, count, before):
                        for i in range(n):
                            a.wait_ge(q["head_ss"], before + i + 1)
                            last = act(out[:, i, :], PS[2 + i][:, :], ACT.Ln, bias=EPS, scale=1.0 / count)
                        step(last)
                        for i in range(n):
                            act(out[:, i, :], out[:, i, :], ACT.Exp, scale=-0.5).then_inc(q["head_rstd"], 1)

                    for k in range(KT):
                        act(hs[:, k, :], xT[:, k, :], ACT.Square).then_inc(q["sq_ready"], 1)
                    high_to(RING)
                    a.wait_ge(q["ss_ps"], 1)
                    rsqrt(rs1, PS[6][:, :], D, q["rstd_ready"])
                    for k in range(KT):
                        a.wait_ge(q["h_tmp"], k + 1)
                        act(hH[:, k, :], hs[:, k, :], ACT.Copy).then_inc(q["h_high"], 1)
                    high_to(SPLIT)
                    a.wait_ge(q["pack_loaded"], 16)
                    act(dt5, prm("ldt"), ACT.Exp).then_inc(q["trig_done"], 1)
                    a.wait_ge(q["abc_done"], 1)
                    act(mag, lrdt, ACT.Exp).then_inc(q["trig_done"], 1)
                    act(sina, thr, ACT.Sin).then_inc(q["trig_done"], 1)
                    act(cosa, thabs, ACT.Sin, bias=TWO_PI / 4, scale=-1.0).then_inc(q["trig_done"], 1)
                    act(smT[0:20, :], stream("small")[0:20, :], ACT.Copy).then_inc(q["proj_taken"], 1)
                    high_to(ahead(SLAB["small"]))
                    for i, (name, _) in enumerate(FIRST):
                        if name == "kcvc":
                            b = stream(name)
                            act(t2k[0:HD, :], b[0:HD, :], ACT.Copy)
                            act(t2k[HD:P, 0:S - 1], b[0:HD, 1:S], ACT.Copy)
                            act(t2v[0:HD, :], b[HD:P, :], ACT.Copy)
                            act(t2v[HD:P, 0:S - 1], b[HD:P, 1:S], ACT.Copy).then_inc(q["proj_taken"], 1)
                            high_to(ahead(SLAB[name]))
                        else:
                            evacuate(pjt[name], name)
                        if i == 1:
                            a.wait_ge(q["sm_ps"], 1)
                            act(small[:, 0:80], PS[7][:, 0:80], ACT.Copy).then_inc(q["sm_ready"], 1)
                            a.wait_ge(q["sm_ready"], 1)
                            act(e_sig, sm_all[:, :, 0:16], ACT.Exp, scale=-1.0).then_inc(q["sig_exp"], 1)
                            step(act(ea, prm("alog"), ACT.Exp))
                            a.wait_ge(q["xa_neg"], 1)
                            step(act(na, na, ACT.Exp))
                            act(la, na, ACT.Ln, bias=1.0).then_inc(q["xa_ln"], 1)
                        if i == 3:
                            a.wait_ge(q["abc_done"], 2)
                            act(turn4[:, 0, :], turn4[:, 0, :], ACT.Sin, scale=SIN_SCALE).then_inc(q["trig_done"], 1)
                            act(turn4[:, 1, :], turn4[:, 1, :], ACT.Sin, scale=-SIN_SCALE, bias=TWO_PI / 4)\
                                .then_inc(q["trig_done"], 1)
                    for j in range(8):
                        fill(FILL["blocks"][j])
                        if j in (1, 2):
                            for i in range(3 * j - 3, 3 * j):
                                a.wait_ge(q["conv_ready"], i + 1)
                                act(th[:, i, :], cv[:, i, :], ACT.Tanh).then_inc(q["tanh_ready"], 1)
                        if j == 3:
                            for i in range(4):
                                a.wait_ge(q["silu_ready"], i + 1)
                                act(sqk[:, i, :], cv[:, i, :], ACT.Square).then_inc(q["sqk_ready"], 1)
                    for kv in range(2):
                        a.wait_ge(q["slab_done"], SLAB[f"c{'kv'[kv]}3"] + 1)
                        act(cmpT[0:NCMP, 256 * kv:256 * kv + 256], PS[6 + kv][0:NCMP, 0:256], ACT.Copy)\
                            .then_inc(q["cmp_nat_ready"], 1)
                    high_to(ahead(SLAB["cv3"]))
                    fill(FILL["hidden"])
                    a.wait_ge(q["cmp_nat"], 1)
                    act(cx, PS[5][:, 0:124], ACT.Copy).then_inc(q["cmp1_ps"], 1)
                    a.wait_ge(q["cmp_arg"], 1)
                    act(ct, ct, ACT.Tanh, scale=GELU_C).then_inc(q["cmp_exp"], 1)
                    fill(FILL["gelu"])
                    a.wait_ge(q["slab_done"], SLAB["cw2"] + 1)
                    step(act(kcT, PS[7][:, 128:159], ACT.Copy))
                    act(vc[0:NCMP, :], PS[7][0:NCMP, 192:256], ACT.Copy)
                    act(kc_s, kcT, ACT.Square).then_inc(q["head_sq"], 1)
                    a.wait_ge(q["head_ss"], 1)
                    rsqrt(kc_r, PS[7][:, 320:351], HD, q["head_rstd"])
                    high_to(ahead(SLAB["cw2"]))
                    fill(FILL["gsum"])
                    for i in range(4):
                        a.wait_ge(q["qkss_ps"], i + 1)
                        last = act(rqk[:, i, :], PS[3 + i][:, :], ACT.Ln, bias=EPS)
                    step(last)
                    for i in range(4):
                        act(rqk[:, i, :], rqk[:, i, :], ACT.Exp, scale=-0.5).then_inc(q["qk_rstd"], 1)
                    fill(FILL["qk"])
                    a.wait_ge(q["gsum_taken"], 1)
                    act(egc, gc, ACT.Exp)
                    act(egl, gl, ACT.Exp)
                    act(kdc, kdc, ACT.Exp).then_inc(q["gexp_ready"], 1)
                    for b in range(4):
                        a.wait_ge(q["args_ready"], b + 1)
                        act(mT_flat[:, S * b:S * b + S], PS[3 + b][:, :], ACT.Exp).then_inc(q["grow_exp"], 1)
                        act(mL_flat[:, S * b:S * b + S], mL_flat[:, S * b:S * b + S], ACT.Exp, scale=-1.0)\
                            .then_inc(q["dexp_ready"], 1)
                        act(mY_flat[:, S * b:S * b + S], mY_flat[:, S * b:S * b + S], ACT.Exp).then_inc(q["dexp_ready"], 1)
                    fill(FILL["grow"] + FILL["turn"] + FILL["skq"] + sum(FILL["level"]))
                    for tt in range(NT):
                        a.wait_ge(q["wt_ps"], tt + 1)
                        act(wt[:, tt], PS[2 + tt][:, 0:256].rearrange("p (i c) -> p i c", i=2), ACT.Copy, scale=-1.0)\
                            .then_inc(q["wt_ready"], 1)
                    for tt in range(NT):
                        a.wait_ge(q["o_ps"], tt + 1)
                        for par in range(2):
                            act(o_raw[HD * par:HD * par + HD, :, P * tt:P * tt + P],
                                PS[6 + par][HD * par:HD * par + HD, 0:256].rearrange("p (i c) -> p i c", i=2), ACT.Copy)\
                                .then_inc(q["o_taken"], 1)
                        fill(FILL["chunk"][tt])
                    a.wait_ge(q["o_taken"], 8)
                    for i in range(2):
                        act(o_sq[:, i, :], o_raw[:, i, :], ACT.Square).then_inc(q["head_sq"], 1)
                    for i in range(2):
                        act(z_th[:, i, :], pjt[f"z{i}"], ACT.Tanh, scale=0.5).then_inc(q["z_tanh"], 1)
                    rsqrts(o_rs, 2, HD, 1)
                    fill(FILL["oss"])
                    a.wait_ge(q["tab_ready"], 1)
                    act(s5_sin, s5_sin, ACT.Sin, scale=SIN_SCALE).then_inc(q["sin_ready"], 1)
                    act(s5_cos, s5_cos, ACT.Sin, scale=-SIN_SCALE, bias=TWO_PI / 4).then_inc(q["sin_ready"], 1)
                    for i in range(8):
                        fill(FILL["s5"][i])
                    for i in range(2):
                        a.wait_ge(q["y5_ready"], i + 1)
                        act(y5b[:, i, :], y5a[:, i, :], ACT.Square).then_inc(q["y5_sq"], 1)
                    for i in range(2):
                        a.wait_ge(q["y5_ready"], 2 + i + 1)
                        act(y5b[:, i, :], y5b[:, i, :], ACT.Tanh, scale=GELU_C).then_inc(q["y5_tanh"], 1)
                    fill(FILL["glu"])
                    a.wait_ge(q["slab_done"], SLAB["glu"] + 1)
                    for i in range(2):
                        act(y5b[:, i, :], PS[6 + i][:, :], ACT.Tanh, scale=0.25).then_inc(q["y5_tanh"], 1)
                    def sb_tile(n):
                        kb = 3 - n % 4
                        return sb_z(n // 4, kb)[:, P * kb:S], sb_e(n)[:, P * kb:S]

                    for h in range(H + 1):
                        now = range(4 * h, 4 * h + 4) if h < H else ()
                        for n in now:
                            a.wait_ge(q["sbz_ps"], n + 1)
                            if h >= 2:
                                a.wait_ge(q["sbpv_ps"], h - 1)
                            z, _ = sb_tile(n)
                            act(z, PS[2 + n % 2][:, 0:S - P * (3 - n % 4)], ACT.Copy).then_inc(q["z_copied"], 1)
                        for n in now:
                            a.wait_ge(q["nb_ready"], n + 1)
                            _, e = sb_tile(n)
                            act(e, e, ACT.Exp).then_inc(q["sp_exp"], 1)
                        if h == 0:
                            high_to(ahead(SLAB["glu"]))
                        if h:
                            for n in range(4 * h - 4, 4 * h):
                                a.wait_ge(q["d_masked"], n + 1)
                                z, _ = sb_tile(n)
                                act(z, z, ACT.Exp).then_inc(q["wexp_ready"], 1)
                        for n in now:
                            a.wait_ge(q["sp_exp"], n + 1)
                            _, e = sb_tile(n)
                            act(e, e, ACT.Ln, bias=1.0).then_inc(q["sp_ln"], 1)
                        fill(FILL["sb"][h])
                    a.wait_ge(q["sbpv_ps"], 4)
                    for i in range(3):
                        act(nsq[:, i, :], pjt[("q0", "q1", "kskw")[i]], ACT.Square).then_inc(q["head_sq"], 1)
                    rsqrts(nrs, 3, HD, 3)
                    a.wait_ge(q["vt_ps"], 1)
                    act(nvt[:, :, :], PS[5][:, :].rearrange("p (t c) -> p t c", t=4), ACT.Copy).then_inc(q["vt_ready"], 1)
                    fill(FILL["norms"])
                    a.wait_ge(q["rot_ready"], 4)
                    act(kdup[HD:P, 0, :], kdup[0:HD, 0, :], ACT.Copy).then_inc(q["kdup_ready"], 1)
                    act(kdup[0:HD, 1, :], kdup[HD:P, 1, :], ACT.Copy).then_inc(q["kdup_ready"], 1)
                    a.wait_ge(q["cmp_arg"], 2)
                    act(npc_flat, npc_flat, ACT.Exp).then_inc(q["cmp_exp"], 1)
                    fill(FILL["rot"])

                    def nsa_exps(m, heads):
                        wid = P * (m // 2 + 1)
                        if m >= 2:
                            a.wait_ge(q["pt_ps"], PTN[m - 1])
                        for h in heads:
                            x = 4 * m + h
                            a.wait_ge(q["nm_ready"], x + 1)
                            act(nP[m % 2][:, h, 0:wid], PS[2 + h % 2][:, 0:wid], ACT.Exp,
                                bias=nm[:, x:x + 1], accum_out=nsum[:, x:x + 1]).then_inc(q["p_ready"], 1)

                    def nsa_store(qt):
                        a.wait_ge(q["ot_ps"], qt + 1)
                        act(nsa_out[:, :, P * qt:P * qt + P], PS[6][:, 0:256].rearrange("p (i c) -> p i c", i=2),
                            ACT.Copy).then_inc(q["nsa_done"], 1)

                    nsa_exps(0, range(H))
                    for m in range(2 * NT):
                        if m + 1 < 2 * NT:
                            nsa_exps(m + 1, (0, 1))
                        if m + 1 < 2 * NT:
                            nsa_exps(m + 1, (2, 3))
                        if m and m % 2 == 0:
                            nsa_store(m // 2 - 1)
                        fill(FILL["nsa"][m])
                    nsa_store(NT - 1)
                    for i in range(2):
                        a.wait_ge(gate_stored[i], 16 * 2 * KT)
                    for dt in range(4):
                        a.dma_start(gload[:, dt], a_gates[dt]).then_inc(gate_back[dt], 16)
                    a.wait_ge(q["nsa_done"], NT)
                    for j in range(8):
                        act(oH[:, j, :], mixed[j // 2][:, j % 2, :], ACT.Copy).then_inc(q["o_high"], 1)
                    for dt in range(KT):
                        a.wait_ge(gate_back[dt % 4], 16 * (dt // 4 + 1))
                        act(gload[:, dt % 4], gload[:, dt % 4], ACT.Tanh, scale=0.5).then_inc(q["gate_tanh"], 1)
                        if dt:
                            a.wait_ge(q["merged_sum"], dt)
                            act(mH[:, dt - 1, :], mtmp[:, (dt - 1) % 2, 0, :], ACT.Copy).then_inc(q["merged_high"], 1)
                            if dt + 3 < KT:
                                a.wait_ge(q["br_taken"], 4 * dt)
                                a.dma_start(gload[:, (dt + 3) % 4], a_gates[dt + 3]).then_inc(gate_back[(dt + 3) % 4], 16)
                        high_to(ahead(SLAB[f"br{dt}"]))
                    a.wait_ge(q["merged_sum"], KT)
                    act(mH[:, KT - 1, :], mtmp[:, (KT - 1) % 2, 0, :], ACT.Copy).then_inc(q["merged_high"], 1)
                    for k in range(KT):
                        high_to(ahead(SLAB[f"out{k}"]))
                        a.wait_ge(q["xo_ready"], k + 1)
                        act(hs2[:, k, :], xT[:, k, :], ACT.Square).then_inc(q["sq_ready"], 1)
                    a.wait_ge(q["ss_ps"], 2)
                    rsqrt(rs2, PS[2][:, :], D, q["rstd_ready"])
                    for k in range(KT):
                        a.wait_ge(q["h_tmp"], KT + k + 1)
                        act(hH[:, k, :], hs2[:, k, :], ACT.Copy).then_inc(q["h_high"], 1)
                    for f in range(FT):
                        a.wait_ge(q["slab_done"], SLAB[f"fg{f}"] + 1)
                        if f >= 2:
                            a.wait_ge(q["ga_ready"], f - 1)
                        act(ft[:, f % 2, :], PS[2 * (f % 4)][:, :], ACT.Tanh, scale=0.5).then_inc(q["fg_tanh"], 1)
                        high_to(ahead(SLAB[f"fg{f}"]))
                        a.wait_ge(q["hid_tmp"], f + 1)
                        act(hidH[:, f, :], fh[:, f % 2, :], ACT.Copy).then_inc(q["hid_high"], 1)
                        high_to(ahead(SLAB[f"fu{f}"]))
                    high_to(NSLAB)

                @block.vector
                def _(v):
                    chain = [0]
                    tt_, ts, stt = nc.vector.tensor_tensor, nc.vector.tensor_scalar, nc.vector.scalar_tensor_tensor
                    M, A_, SU = ALU.mult, ALU.add, ALU.subtract

                    def step(ins):
                        chain[0] += 1
                        ins.then_inc(q["dve_step"], 1)
                        v.wait_ge(q["dve_step"], chain[0])

                    split = [POOL_END]

                    def low_to(end):
                        while split[0] < end:
                            i = split[0]
                            split[0] += 1
                            v.wait_ge(q["w_high"], ORD[i] + 1)
                            tt_(wL[:, ORD[i] % SPLIT], raw[:, i % RING], wH[:, ORD[i] % SPLIT].bitcast(F32), SU)\
                                .then_inc(slab_taken[i % RING], 1)

                    def low(out, x, high):
                        return tt_(out, x, high.bitcast(F32), SU)

                    v.wait_ge(q["rstd_ready"], 1)
                    for k in range(KT):
                        stt(hs[:, k, :], xT[:, k, :], prm("an")[:, k:k + 1], rs1, M, M).then_inc(q["h_tmp"], 1)
                        if k:
                            v.wait_ge(q["h_high"], k)
                            low(hL[:, k - 1, :], hs[:, k - 1, :], hH[:, k - 1, :]).then_inc(q["h_ready"], 1)
                    v.wait_ge(q["h_high"], KT)
                    low(hL[:, KT - 1, :], hs[:, KT - 1, :], hH[:, KT - 1, :]).then_inc(q["h_ready"], 1)
                    v.memset(state[:, :, :], 0.0).then_inc(q["st_ready"], 1)
                    v.wait_ge(q["pack_loaded"], 16)
                    lre, lim = prm("lre"), prm("lim")
                    v.wait_ge(q["trig_done"], 1)
                    step(tt_(theta, lim, dt5, M))
                    step(tt_(lrdt, lre, dt5, M))
                    step(ts(tmp1, theta, INV_2PI, ROUND, M, A_))
                    step(ts(tmp1, tmp1, ROUND, None, SU))
                    step(stt(thr, tmp1, -C1, theta, M, A_))
                    step(stt(thr, tmp1, -C2, thr, M, A_))
                    step(stt(thr, tmp1, -C3, thr, M, A_))
                    step(ts(thr, thr, -3.1415925, 3.1415925, ALU.max, ALU.min))
                    stt(thabs, thr, -1.0, thr, M, ALU.max).then_inc(q["abc_done"], 1)
                    step(ts(uh, thr, INV_2PI, ROUND12, M, A_))
                    step(ts(uh, uh, ROUND12, None, SU))
                    step(stt(ul, uh, -C1, thr, M, A_))
                    step(stt(ul, uh, -C2, ul, M, A_))
                    step(stt(ul, uh, -C3, ul, M, A_))
                    step(ts(ul, ul, INV_2PI, None, M))
                    step(ts(prm("cim"), prm("cim"), -1.0, None, M))
                    step(ts(prm("cw"), prm("cw"), 0.5, None, M))
                    step(ts(q8, prm("qn"), 0.125, None, M))
                    step(tt_(den, lre, lre, M))
                    step(tt_(tmp1, lim, lim, M))
                    step(tt_(den, den, tmp1, A_))
                    step(v.reciprocal(den, den))
                    v.wait_ge(q["trig_done"], 4)
                    step(tt_(abr, mag, cosa, M))
                    step(tt_(abi, mag, sina, M))
                    step(ts(abr, abr, 1.0, None, SU))
                    step(tt_(tmp1, abr, lre, M))
                    step(tt_(tmp2, abi, lim, M))
                    step(tt_(fre, tmp1, tmp2, A_))
                    step(tt_(fre, fre, den, M))
                    step(tt_(tmp1, abi, lre, M))
                    step(tt_(tmp2, abr, lim, M))
                    step(tt_(fim, tmp1, tmp2, SU))
                    step(tt_(fim, fim, den, M))

                    def turns(stage, f, g, tmp, t, hi, lo):
                        if stage == 0:
                            step(tt_(tmp, t, hi, M))
                        elif stage == 1:
                            step(ts(g, tmp, ROUND, None, A_))
                            step(ts(g, g, ROUND, None, SU))
                        elif stage == 2:
                            step(tt_(f, tmp, g, SU))
                        elif stage == 3:
                            step(tt_(tmp, t, lo, M))
                            step(tt_(f, f, tmp, A_))
                        elif stage == 4:
                            step(ts(g, f, ROUND, None, A_))
                            step(ts(g, g, ROUND, None, SU))
                        elif stage == 5:
                            step(tt_(f, f, g, SU))
                        else:
                            return stt(g, f, -1.0, f, M, ALU.max)

                    tc4 = cst("tc").rearrange("p (c i) -> p c i", c=NT)
                    u4 = [x.unsqueeze(1).broadcast_to([P, NT, 8]) for x in (uh, ul)]
                    for stage in range(6):
                        turns(stage, sin4, cos4, tmp4, tc4, *u4)
                    turns(6, sin4, cos4, tmp4, tc4, *u4).then_inc(q["abc_done"], 1)
                    v.wait_ge(q["sm_ready"], 1)
                    step(tt_(xa.rearrange("p (t c) -> p t c", t=4), sm_all[:, :, 16:20],
                             prm("dtb").rearrange("p (t c) -> p t c", t=4), A_))
                    stt(na, xa, -1.0, xa, M, ALU.min).then_inc(q["xa_neg"], 1)

                    def conv(i):
                        v.wait_ge(q["proj_taken"], 2 + i)
                        w = prm("cw")[:, 4 * i:4 * i + 4]
                        x, o = pj[:, i, :], cv[:, i, :]
                        step(ts(o, x, w[:, 3:4], None, M))
                        for d in (1, 2):
                            step(stt(o[:, d:S], x[:, 0:S - d], w[:, 3 - d:4 - d], o[:, d:S], M, A_))
                        stt(o[:, 3:S], x[:, 0:S - 3], w[:, 0:1], o[:, 3:S], M, A_).then_inc(q["conv_ready"], 1)

                    conv(0)
                    conv(1)
                    v.wait_ge(q["sig_exp"], 1)
                    step(ts(e_sig, e_sig, 1.0, None, A_))
                    v.reciprocal(sig, e_sig).then_inc(q["sig_ready"], 1)
                    v.wait_ge(q["xa_ln"], 1)
                    step(stt(xa, xa, 0.0, la, ALU.max, A_))
                    stt(g16, xa, -1.0, ea, M, M).then_inc(q["g_ready"], 1)
                    for i in range(2, 6):
                        conv(i)
                    for i in range(6):
                        v.wait_ge(q["tanh_ready"], i + 1)
                        stt(cv[:, i, :], th[:, i, :], 1.0, cv[:, i, :], A_, M).then_inc(q["silu_ready"], 1)
                    def rotate(out_re, out_im, re, im, done=None):
                        def wide(x):
                            return x.unsqueeze(1).broadcast_to([P, 3, 8, 32])

                        cs, sn = (x[:, 1:NT, :].unsqueeze(3).broadcast_to([P, 3, 8, 32]) for x in (cos4, sin4))
                        r1, r2 = (pads[:, 768 * j:768 * j + 768].rearrange("p (c i s) -> p c i s", c=3, i=8)
                                  for j in range(2))
                        step(tt_(r1, wide(re), cs, M))
                        step(tt_(r2, wide(im), sn, M))
                        step(tt_(out_re, r1, r2, A_))
                        step(tt_(r1, wide(im), cs, M))
                        step(tt_(r2, wide(re), sn, M))
                        return tt_(out_im, r1, r2, SU)

                    pads = arena[:, 0:1536]
                    v.wait_ge(q["silu_ready"], 6)
                    step(v.memset(bpad[:, 0, :, :, :], 0.0))
                    v.wait_ge(q["trig_done"], 6)
                    br = prm("bre").rearrange("p (i c) -> p i c", i=8)
                    bi = prm("bim").rearrange("p (i c) -> p i c", i=8)
                    b1 = pads[:, 0:128].rearrange("p (i c) -> p i c", i=8)
                    b2 = pads[:, 128:256].rearrange("p (i c) -> p i c", i=8)
                    freb = fre.unsqueeze(2).broadcast_to([P, 8, 16])
                    fimb = fim.unsqueeze(2).broadcast_to([P, 8, 16])
                    for pad, x, y, op in ((bpad[:, 0, 0], br, bi, SU), (bpad[:, 0, 1], bi, br, A_)):
                        step(tt_(b1, x, freb, M))
                        step(tt_(b2, y, fimb, M))
                        for s in range(2):
                            r, c = slice(HD * s, HD * s + HD), slice(16 * s, 16 * s + 16)
                            step(tt_(pad[r, :, c], b1[r], b2[r], op))
                    rotate(bpad[:, 1:NT, 0], bpad[:, 1:NT, 1], bpad[:, 0, 0], bpad[:, 0, 1]).then_inc(q["bpad_ready"], 1)
                    v.wait_ge(q["bpad_ready"], 1)
                    cc = [prm(n).rearrange("p (i s) -> p i s", i=8) for n in ("cre", "cim")]
                    rotate(*(crot[:, r].rearrange("p c (i s) -> p c i s", i=8) for r in range(2)), *cc)\
                        .then_inc(q["bpad_ready"], 1)
                    v.wait_ge(q["cmp1_ps"], 1)
                    step(tt_(ct, cx, cx, M))
                    step(ts(ct, ct, GELU_A, 1.0, M, A_))
                    tt_(ct, ct, cx, M).then_inc(q["cmp_arg"], 1)
                    v.wait_ge(q["cmp_exp"], 1)
                    step(stt(ct, ct, 1.0, cx, A_, M))
                    ts(cmp_flat, ct, 0.5, None, M).then_inc(q["cmp_hid"], 1)
                    v.wait_ge(q["gsum_ps"], 1)
                    step(nc.vector.tensor_copy(small[:, GC0:GC0 + 32], PS[2][:, 0:32]))
                    tt_(kdc, gl, gc, SU).then_inc(q["gsum_taken"], 1)
                    v.wait_ge(q["head_rstd"], 1)
                    stt(kcT, kcT, prm("kn0"), kc_r, M, M).then_inc(q["kc_ready"], 1)
                    for i in range(4):
                        v.wait_ge(q["qk_rstd"], i + 1)
                        stt(cv[:, i, :], cv[:, i, :], 0.125 if i < 2 else 1.0, rqk[:, i, :], M, M).then_inc(q["qk_ready"], 1)

                    def take_inputs(c):
                        v.wait_ge(q["bt_ps"], c + 1)
                        nc.vector.tensor_copy(bt[:, c].rearrange("p r t s -> p (r t s)"), PS[7][:, :])\
                            .then_inc(q["bt_taken"], 1)

                    v.wait_ge(q["kc_ready"], 1)
                    take_inputs(0)
                    v.wait_ge(q["qk_ready"], 4)
                    for b in range(4):
                        v.wait_ge(q["grow_ps"], b + 1)
                        for j, (tt, h) in enumerate(UNITS[4 * b:4 * b + 4]):
                            c = gc[:, 4 * tt + h:4 * tt + h + 1]
                            ps = PS[3 + b][:, P * j:P * j + P]
                            ts(mL[:, 4 * b + j, :], ps, c, 0.0, SU, ALU.max)
                            last = ts(mY[:, 4 * b + j, :], ps, c, 0.0, SU, ALU.min)
                        last.then_inc(q["args_ready"], 1)
                    take_inputs(1)
                    v.wait_ge(q["gexp_ready"], 1)
                    v.wait_ge(q["sig_ready"], 1)
                    step(tt_(bg.rearrange("p (t c) -> p t c", t=4), sig[:, :, 12:16], egc.rearrange("p (t c) -> p t c", t=4), M))

                    def per_token(x, tt):
                        return x[:, tt:tt + 2, :].unsqueeze(3).broadcast_to([P, 2, 4, HD])

                    b4 = [x.rearrange("p (t c) -> p t c", t=4) for x in (bg, kdc)] + [sig[:, :, 12:16]]
                    for b in range(4):
                        v.wait_ge(q["tr_ps"], b + 1)
                        tt = 2 * (b % 2)
                        ps = PS[3 + b][:, :].rearrange("p (t h e) -> p t h e", t=2, h=4)
                        if b < 2:
                            tt_(kbg[:, tt:tt + 2, :].rearrange("p t (h e) -> p t h e", h=4), ps, per_token(b4[0], tt), M)
                            tt_(kdec[:, tt:tt + 2, :].rearrange("p t (h e) -> p t h e", h=4), ps, per_token(b4[1], tt), M)\
                                .then_inc(q["tr_taken"], 1)
                        else:
                            tt_(vb[:, tt:tt + 2, :].rearrange("p t (h e) -> p t h e", h=4), ps, per_token(b4[2], tt), M)\
                                .then_inc(q["tr_taken"], 1)
                    take_inputs(2)
                    for b in range(4):
                        r = slice(S * b, S * b + S)
                        v.wait_ge(q["skk_ps"], b + 1)
                        v.wait_ge(q["dmask_ready"], 3 * b + 3)
                        tt_(mL_flat[:, r], PS[3 + b][:, :], mL_flat[:, r], M).then_inc(q["l_part"], 1)
                    v.wait_ge(q["skq_ps"], 4)
                    v.wait_ge(q["qd_ready"], 8)
                    for b in range(4):
                        r = slice(S * b, S * b + S)
                        tt_(aT_flat[:, r], PS[3 + b][:, :], mY_flat[:, r], M).then_inc(q["at_part"], 1)

                    take_inputs(3)

                    def four(x):
                        return x.unsqueeze(1).broadcast_to([P, 4, P])

                    def bank4(b):
                        return PS[b][:, :].rearrange("p (u c) -> p u c", u=4)

                    for b in range(4):
                        u = slice(4 * b, 4 * b + 4)
                        v.wait_ge(q["y0_ps"], b + 1)
                        tt_(mY[:, u, :], bank4(3 + b), four(lev[:, 0, :]), M).then_inc(q["u0_ready"], 1)
                        v.wait_ge(q["u0_ready"], 2 * b + 1)
                        tt_(mU[:, u, :], four(ident), mY[:, u, :], SU).then_inc(q["u0_ready"], 1)
                    v.wait_ge(q["qd_ready"], 8)
                    for b in range(4):
                        u = slice(4 * b, 4 * b + 4)
                        v.wait_ge(q["t0_ps"], b + 1)
                        tt_(mT[:, u, :], four(ident), bank4(3 + b), SU).then_inc(q["t0_ready"], 1)

                    def y_mask(n):
                        b = n % 4
                        v.wait_ge(q["y_ps"], n + 1)
                        tt_(mY[:, 4 * b:4 * b + 4, :], bank4(2 + n % 2), four(lev[:, 1 + n // 4, :]), M)\
                            .then_inc(q["y_ready"], 1)

                    def ut_update(n):
                        u = slice(4 * (n % 4), 4 * (n % 4) + 4)
                        v.wait_ge(q["du_ps"], n + 1)
                        tt_(mU[:, u, :], mU[:, u, :], bank4(4 + n % 2), SU).then_inc(q["u_ready"], 1)
                        if n < 20:
                            v.wait_ge(q["dt_ps"], n + 1)
                            tt_(mT[:, u, :], mT[:, u, :], bank4(6 + n % 2), SU).then_inc(q["t_ready"], 1)

                    for lv in range(6):
                        y_mask(4 * lv)
                        y_mask(4 * lv + 1)
                        ut_update(4 * lv)
                        y_mask(4 * lv + 2)
                        ut_update(4 * lv + 1)
                        y_mask(4 * lv + 3)
                        ut_update(4 * lv + 2)
                        ut_update(4 * lv + 3)
                    s5_turns = [s5_sin, s5_cos, s5_tmp, cst("t").unsqueeze(1).broadcast_to([P, 8, P])]
                    s5_turns += [x.unsqueeze(2).broadcast_to([P, 8, P]) for x in (uh, ul)]
                    for tt in range(NT):
                        v.wait_ge(q["vn_ps"], tt + 1)
                        for par in range(2):
                            nc.vector.tensor_copy(vn[:, par::2, :], PS[2 + par][:, 0:P].rearrange("p (i e) -> p i e", i=2))\
                                .then_inc(q["vn_ready"], 1)
                        v.wait_ge(q["su_ps"], tt + 1)
                        for h in range(H):
                            x = state[half(h), h // 2, :]
                            stt(x, x, egl[half(h), 4 * tt + h:4 * tt + h + 1],
                                PS[4 + h % 2][half(h), HD * (h // 2):HD * (h // 2) + HD], M, A_).then_inc(q["st_ready"], 1)
                        for stage in ((0, 1), (2, 3), (4, 5), ())[tt]:
                            turns(stage, *s5_turns)
                    turns(6, *s5_turns).then_inc(q["tab_ready"], 1)
                    for i in range(2):
                        v.wait_ge(q["z_tanh"], i + 1)
                        v.wait_ge(q["head_rstd"], 1 + i + 1)
                        step(stt(z_th[:, i, :], z_th[:, i, :], 1.0, pjt[f"z{i}"], A_, M))
                        step(stt(o_raw[:, i, :], o_raw[:, i, :], prm("on"), o_rs[:, i, :], M, M))
                        stt(pjt[f"z{i}"], z_th[:, i, :], 0.5, o_raw[:, i, :], M, M).then_inc(q["gdn_done"], 1)

                    v.wait_ge(q["gdn_done"], 2)

                    def chunks(x):
                        return x.rearrange("p (c t) -> p c t", c=NT)

                    def s5_cs(i):
                        return (x[:, i, :].unsqueeze(1).broadcast_to([P, NT, P]) for x in (s5_cos, s5_sin))

                    def s5_turn_in(i):
                        c_, s_ = s5_cs(i)
                        bur, bui = (chunks(PS[2 + 2 * (i % 2) + r][:, :]) for r in range(2))
                        m1, m2, m3, m4 = (chunks(s5_m(i, j)) for j in range(4))
                        if i >= 3:
                            v.wait_ge(q["y5_ps"], i - 2)
                        v.wait_ge(q["bu_ps"], i + 1)
                        tt_(m1, c_, bur, M)
                        tt_(m2, s_, bui, M)
                        tt_(m3, c_, bui, M)
                        tt_(m4, s_, bur, M).then_inc(q["m_ready"], 1)

                    v.wait_ge(q["sin_ready"], 2)
                    s5_turn_in(0)
                    for i in range(8):
                        if i < 7:
                            s5_turn_in(i + 1)
                        v.wait_ge(q["w_ready"], 2 * i + 2)
                        if i >= 2:
                            v.wait_ge(q["n_ready"], 4 * i - 4)
                        mg = mag[:, i:i + 1].broadcast_to([P, S])
                        for j in range(2):
                            v.tensor_tensor_scan(s5_z(i, j), mg, s5_m(i, 2 * j), 0.0, M, A_).then_inc(q["z_ready"], 1)
                        v.wait_ge(q["z_ready"], 2 * i + 2)
                        c_, s_ = s5_cs(i)
                        zr, zi = (chunks(s5_z(i, j)) for j in range(2))
                        for j, (x, z) in enumerate(((c_, zr), (s_, zi), (s_, zr), (c_, zi))):
                            tt_(chunks(s5_m(i, j)), x, z, M).then_inc(q["n_ready"], 1)
                    for i in range(2):
                        v.wait_ge(q["y5_ps"], 4 * i + 4)
                        stt(y5a[:, i, :], pjt[f"u{i}"], prm("dsk")[:, i:i + 1], PS[6 + i][:, :], M, A_)\
                            .then_inc(q["y5_ready"], 1)
                    for i in range(2):
                        v.wait_ge(q["y5_sq"], i + 1)
                        step(ts(y5b[:, i, :], y5b[:, i, :], GELU_A, 1.0, M, A_))
                        tt_(y5b[:, i, :], y5b[:, i, :], y5a[:, i, :], M).then_inc(q["y5_ready"], 1)
                    for i in range(2):
                        v.wait_ge(q["y5_tanh"], i + 1)
                        stt(gy[:, i, :], y5b[:, i, :], 1.0, y5a[:, i, :], A_, M).then_inc(q["gy_ready"], 1)
                    for i in range(2):
                        v.wait_ge(q["y5_tanh"], 2 + i + 1)
                        step(stt(y5b[:, i, :], y5b[:, i, :], 1.0, PS[4 + i][:, :], A_, M))
                        ts(s5_out[:, i, :], y5b[:, i, :], 0.25, None, M).then_inc(q["s5_done"], 1)

                    def sb_abs(n):
                        h, kb = n // 4, 3 - n % 4
                        r = slice(P * kb, S)
                        v.wait_ge(q["z_copied"], n + 1)
                        if h:
                            v.wait_ge(q["sp_ready"], n - 3)
                        stt(sb_e(n)[:, r], sb_z(h, kb)[:, r], -1.0, sb_z(h, kb)[:, r], M, ALU.min).then_inc(q["nb_ready"], 1)

                    def sb_softplus(n):
                        h, kb = n // 4, 3 - n % 4
                        r = slice(P * kb, S)
                        v.wait_ge(q["sp_ln"], n + 1)
                        if h >= 2:
                            v.wait_ge(q["cum_ps"], 4 * h - 4)
                        stt(sb_sp(h, kb)[:, r], sb_z(h, kb)[:, r], 0.0, sb_e(n)[:, r], ALU.max, A_).then_inc(q["sp_ready"], 1)

                    def sb_softplus_mask(n):
                        h, kb = n // 4, 3 - n % 4
                        c = slice(P * kb, P * kb + P)
                        v.wait_ge(q["sp_ready"], n + 1)
                        tt_(sb_sp(h, kb)[:, c], sb_sp(h, kb)[:, c], cst("lt"), M).then_inc(q["sp_masked"], 1)

                    def sb_weight(n):
                        h, kb = n // 4, 3 - n % 4
                        v.wait_ge(q["cum_ps"], n + 1)
                        z = sb_z(h, kb)[:, P * kb:S]
                        stt(z, PS[4 + n % 2][:, 0:S - P * kb], -1.0, z, M, A_).then_inc(q["d_ready"], 1)

                    def sb_weight_mask(n):
                        h, kb = n // 4, 3 - n % 4
                        c = slice(P * kb, P * kb + P)
                        v.wait_ge(q["d_ready"], n + 1)
                        tt_(sb_z(h, kb)[:, c], sb_z(h, kb)[:, c], cst("negk"), A_).then_inc(q["d_masked"], 1)

                    def sb_store(h):
                        v.wait_ge(q["sbpv_ps"], h + 1)
                        nc.vector.tensor_copy(sb_out[half(h), h // 2, :], PS[6 + h % 2][half(h), :])\
                            .then_inc(q["sb_done"], 1)

                    for h in range(H + 1):
                        if h < H:
                            for n in range(4 * h, 4 * h + 4):
                                sb_abs(n)
                        if h:
                            for n in range(4 * h - 4, 4 * h):
                                sb_weight(n)
                                sb_weight_mask(n)
                        if h < H:
                            for n in range(4 * h, 4 * h + 4):
                                sb_softplus(n)
                                sb_softplus_mask(n)
                        if h:
                            sb_store(h - 1)
                    for i in range(3):
                        v.wait_ge(q["head_rstd"], 3 + i + 1)
                        stt(nqn[:, i, :], pjt[("q0", "q1", "kskw")[i]], q8 if i < 2 else prm("kn12"), nrs[:, i, :], M, M)\
                            .then_inc(q["qn_ready"], 1)
                    for i in range(3):
                        v.wait_ge(q["rot_ps"], i + 1)
                        tt_(nts[:, i, :], PS[2 + i][:, :], sinT[:, :], M).then_inc(q["t_sin"], 1)
                    cm = [cst(n).rearrange("p (t n) -> p t n", t=NT).unsqueeze(2).broadcast_to([P, NT, 2, NCMP])
                          for n in ("cneg", "c01")]
                    for par in range(2):
                        v.wait_ge(q["sc_cmp_ps"], par + 1)
                        step(tt_(npc[:, 8 * par:8 * par + 8, :].rearrange("p (t i) n -> p t i n", i=2),
                                 PS[6 + par][:, 0:248].rearrange("p (t i n) -> p t i n", t=NT, i=2), cm[0], A_))
                    step(v.tensor_reduce(nc1, npc, AX_X, ALU.max))
                    tt_(npc, npc, nc1.unsqueeze(2).broadcast_to([P, 16, NCMP]), SU).then_inc(q["cmp_arg"], 1)
                    v.wait_ge(q["cmp_exp"], 2)
                    for par in range(2):
                        x = npc[:, 8 * par:8 * par + 8, :].rearrange("p (t i) n -> p t i n", i=2)
                        step(tt_(x, x, cm[1], M))
                    step(v.tensor_reduce(nc1, npc, AX_X, A_))
                    step(ts(nc1, nc1, 1e-30, None, ALU.max))
                    step(v.reciprocal(nc1, nc1))
                    gates = sig[:, :, 0:12].rearrange("p t (i r b) -> p t i r b", i=2, r=2)
                    for par in range(2):
                        x = nc1[:, 8 * par:8 * par + 8].rearrange("p (t i) -> p t i", i=2)
                        step(tt_(x, x, gates[:, :, :, par, 0], M))
                    tt_(npc, npc, nc1.unsqueeze(2).broadcast_to([P, 16, NCMP]), M).then_inc(q["pc_ready"], 1)

                    def combine(qt):
                        v.wait_ge(q["p_ready"], 8 * qt + 8)
                        step(v.reciprocal(nfac, nsum[:, 8 * qt:8 * qt + 8]))
                        f = nfac.rearrange("p (b h) -> p b h", b=2)
                        gt = sig[:, qt, 0:12].rearrange("p (h b) -> p b h", b=3)
                        step(tt_(f, f, gt[:, 1:3, :], M))
                        v.wait_ge(q["pv_ps"], 2 * qt + 2)
                        if qt:
                            v.wait_ge(q["ot_ps"], qt)
                        o4 = nO.rearrange("p (h e) -> p h e", h=4)
                        w4 = nO2.rearrange("p (h e) -> p h e", h=4)
                        step(tt_(o4, PS[6][:, 0:256].rearrange("p (h e) -> p h e", h=4),
                                 f[:, 0, :].unsqueeze(2).broadcast_to([P, 4, HD]), M))
                        step(tt_(nO, nO, PS[6][:, 256:512], A_))
                        step(tt_(w4, PS[7][:, 0:256].rearrange("p (h e) -> p h e", h=4),
                                 f[:, 1, :].unsqueeze(2).broadcast_to([P, 4, HD]), M))
                        tt_(nO, nO, nO2, A_).then_inc(q["onat_ready"], 1)

                    def nsa_maxima(m, heads):
                        for h in heads:
                            v.wait_ge(q["sc_ps"], 4 * m + h + 1)
                            v.tensor_reduce(nm[:, 4 * m + h:4 * m + h + 1], PS[2 + h % 2][:, 0:P * (m // 2 + 1)], AX_X,
                                            ALU.max, negate=True).then_inc(q["nm_ready"], 1)

                    nsa_maxima(0, range(H))
                    for m in range(2 * NT):
                        qt = m // 2
                        if m + 1 < 2 * NT:
                            nsa_maxima(m + 1, (0, 1))
                        if m:
                            v.wait_ge(q["pv_ps"], m)
                        for kb in range(qt + 1):
                            x = PTN[m] + kb
                            v.wait_ge(q["pt_ps"], x + 1)
                            nc.vector.tensor_copy(npt[:, kb, :], PS[4 + x % 2][:, :]).then_inc(q["pt_ready"], 1)
                        if m and m % 2 == 0:
                            combine(qt - 1)
                        if m + 1 < 2 * NT:
                            nsa_maxima(m + 1, (2, 3))
                        if m % 2 == 0:
                            v.wait_ge(q["pct_ps"], qt + 1)
                            nc.vector.tensor_copy(npct[0:NCMP, :], PS[7][0:NCMP, :]).then_inc(q["pct_ready"], 1)
                    combine(NT - 1)
                    for j in range(8):
                        v.wait_ge(q["o_high"], j + 1)
                        low(oL[:, j, :], mixed[j // 2][:, j % 2, :], oH[:, j, :]).then_inc(q["o_low"], 1)

                    def merged_low(dt):
                        v.wait_ge(q["merged_high"], dt + 1)
                        low(mL_[:, dt, :], mtmp[:, dt % 2, 0, :], mH[:, dt, :]).then_inc(q["merged_ready"], 1)

                    for dt in range(KT):
                        v.wait_ge(q["gate_tanh"], dt + 1)
                        if dt >= 2:
                            v.wait_ge(q["merged_ready"], dt - 1)
                        for m in range(4):
                            if m < 3:
                                v.wait_ge(q["br_ps"], 3 * dt + m + 1)
                            else:
                                v.wait_ge(q["slab_done"], SLAB[f"br{dt}"] + 1)
                            stt(mtmp[:, dt % 2, m, :], gload[:, dt % 4, m, :], 1.0, PS[2 + (4 * dt + m) % 6][:, :], A_, M)\
                                .then_inc(q["br_taken"], 1)
                        if dt:
                            merged_low(dt - 1)
                        low_to(ahead(SLAB[f"br{dt}"]))
                    merged_low(KT - 1)
                    for dt in range(KT):
                        v.wait_ge(q["slab_done"], SLAB[f"out{dt}"] + 1)
                        stt(xT[:, dt, :], PS[dt % 2][:, :], 0.5, xT[:, dt, :], M, A_).then_inc(q["xo_ready"], 1)
                        low_to(ahead(SLAB[f"out{dt}"]))
                    v.wait_ge(q["rstd_ready"], 2)
                    for k in range(KT + 1):
                        if k < KT:
                            stt(hs2[:, k, :], xT[:, k, :], prm("fn")[:, k:k + 1], rs2, M, M).then_inc(q["h_tmp"], 1)
                        if k:
                            v.wait_ge(q["h_high"], KT + k)
                            low(hL[:, k - 1, :], hs2[:, k - 1, :], hH[:, k - 1, :]).then_inc(q["h_ready"], 1)
                    for f in range(FT):
                        v.wait_ge(q["fg_tanh"], f + 1)
                        stt(fa[:, f % 2, :], ft[:, f % 2, :], 1.0, PS[2 * (f % 4)][:, :], A_, M).then_inc(q["ga_ready"], 1)
                        low_to(ahead(SLAB[f"fg{f}"]))
                        v.wait_ge(q["ga_ready"], f + 1)
                        if f >= 2:
                            v.wait_ge(q["hid_ready"], f - 1)
                        v.wait_ge(q["slab_done"], SLAB[f"fu{f}"] + 1)
                        stt(fh[:, f % 2, :], fa[:, f % 2, :], 0.5, PS[2 * (f % 4) + 1][:, :], M, M).then_inc(q["hid_tmp"], 1)
                        v.wait_ge(q["hid_high"], f + 1)
                        low(hidL[:, f, :], fh[:, f % 2, :], hidH[:, f, :]).then_inc(q["hid_ready"], 1)
                        low_to(ahead(SLAB[f"fu{f}"]))
                    for dt in range(KT):
                        for j in range(3):
                            low_to(ahead(SLAB[f"dn{dt}_{j}"]))
                        v.wait_ge(q["slab_done"], SLAB[f"dn{dt}_2"] + 1)
                        tt_(xT[:, dt, :], xT[:, dt, :], PS[4 + dt % 4][:, :], A_).then_inc(q["dn_taken"], 1)

                @block.gpsimd
                def _(g):
                    tt_, M, A_, SU = nc.gpsimd.tensor_tensor, ALU.mult, ALU.add, ALU.subtract
                    split = [0]

                    def low_to(end):
                        while split[0] < end:
                            i = split[0]
                            split[0] += 1
                            if NAMES[i] in RAW:
                                continue
                            g.wait_ge(q["w_high"], ORD[i] + 1)
                            tt_(wL[:, ORD[i] % SPLIT], raw[:, i % RING], wH[:, ORD[i] % SPLIT].bitcast(F32), SU)\
                                .then_inc(slab_taken[i % RING], 1)

                    def low_of(unit):
                        low_to(last_slab(min(unit, len(FILLERS) - 1)) + 1)

                    low_of(0)
                    g.wait_ge(q["proj_taken"], 1 + len(FIRST))
                    g.wait_ge(q["pack_loaded"], 16)
                    for src, dst, pos in ((t2k, bk, prm("posk")), (t2v, bv, prm("posv"))):
                        for x in range(2):
                            view = src[:, 16 * x:16 * x + 496].rearrange("p (n b t) -> p b n t", b=8, t=2)[:, :, :, 0]
                            tt_(dst[:, 8 * x:8 * x + 8, :], view,
                                pos[:, 8 * x:8 * x + 8].unsqueeze(2).broadcast_to([P, 8, NCMP]), A_)\
                                .then_inc(q["blocks_ready"], 1)
                    low_of(BEFORE_GROW + 2)
                    g.wait_ge(q["sig_ready"], 1)
                    for b in range(4):
                        u = slice(4 * b, 4 * b + 4)
                        g.wait_ge(q["dexp_ready"], 2 * b + 2)
                        tt_(mL[:, u, :], mL[:, u, :], cst("gt").unsqueeze(1).broadcast_to([P, 4, P]), M)\
                            .then_inc(q["dmask_ready"], 1)
                        tt_(mY[:, u, :], mY[:, u, :], cst("le").unsqueeze(1).broadcast_to([P, 4, P]), M)\
                            .then_inc(q["dmask_ready"], 1)
                        g.wait_ge(q["dmask_ready"], 3 * b + 2)
                        t0, par = 2 * (b // 2), b % 2
                        for x in range(2):
                            be = sig[:, t0 + x, 12 + par:15 + par:2] if par == 0 else sig[:, t0 + x, 13:16:2]
                            last = tt_(mL[:, 4 * b + 2 * x:4 * b + 2 * x + 2, :], mL[:, 4 * b + 2 * x:4 * b + 2 * x + 2, :],
                                       be.unsqueeze(2).broadcast_to([P, 2, P]), M)
                        last.then_inc(q["dmask_ready"], 1)
                        if b == 1:
                            low_of(BEFORE_GROW + 3)
                    low_of(BEFORE_SKK + 2)
                    for i in (split[0] - 2, split[0] - 1):
                        g.wait_ge(slab_taken[i % RING], i // RING + 1)
                    g.wait_ge(q["grow_exp"], 4)
                    g.wait_ge(q["qk_ready"], 4)
                    g.wait_ge(q["dmask_ready"], 12)
                    for tt in range(NT):
                        for par in range(2):
                            r = slice(HD * par, HD * par + HD)
                            u = unit(tt, par)
                            if tt + par:
                                g.wait_ge(q["qd_ready"], 2 * tt + par)
                            tt_(qd[r, :, P * tt:P * tt + P], cv[r, 0:2, P * tt:P * tt + P], mT[r, u:u + 2, :], M)\
                                .then_inc(q["qd_ready"], 1)
                    g.wait_ge(q["qd_ready"], 8)
                    low_of(BEFORE_S5 + 2)
                    def s5_sums_in(i):
                        m1, m2, m3, m4 = (s5_m(i, j) for j in range(4))
                        g.wait_ge(q["m_ready"], i + 1)
                        tt_(m1, m1, m2, A_).then_inc(q["w_ready"], 1)
                        tt_(m3, m3, m4, SU).then_inc(q["w_ready"], 1)

                    s5_sums_in(0)
                    for i in range(8):
                        if i < 7:
                            s5_sums_in(i + 1)
                        low_of(min(BEFORE_S5 + sum(FILL["s5"][:i + 1]) + 1, GLU_AT - 1))
                        m1, m2, m3, m4 = (s5_m(i, j) for j in range(4))
                        g.wait_ge(q["n_ready"], 4 * i + 2)
                        tt_(m1, m1, m2, SU).then_inc(q["x_ready"], 1)
                        g.wait_ge(q["n_ready"], 4 * i + 4)
                        tt_(m3, m3, m4, A_).then_inc(q["x_ready"], 1)
                    low_of(BEFORE_NSA + 2)
                    for i in range(3):
                        g.wait_ge(q["qn_ready"], i + 1)
                        tt_(nqr[:, i, :], nqn[:, i, :], cosT[:, :], M).then_inc(q["t_cos"], 1)
                        g.wait_ge(q["t_cos"], i + 1)
                        g.wait_ge(q["t_sin"], i + 1)
                        if i < 2:
                            tt_(nqr[:, i, :], nqr[:, i, :], nts[:, i, :], A_).then_inc(q["rot_ready"], 1)
                        else:
                            for x in range(2):
                                r = slice(HD * x, HD * x + HD)
                                g.wait_ge(q["rot_ready"], 2 + x)
                                tt_(kdup[r, x, :], nqr[r, i, :], nts[r, i, :], A_).then_inc(q["rot_ready"], 1)
                    g.wait_ge(q["rot_ready"], 4)
                    low_to(POOL_END)
                    for dt in range(KT):
                        for m in range(1, 4):
                            g.wait_ge(q["br_taken"], 4 * dt + m + 1)
                            ins = tt_(mtmp[:, dt % 2, 0, :], mtmp[:, dt % 2, 0, :], mtmp[:, dt % 2, m, :], A_)
                            ins.then_inc(q["merged_sum"] if m == 3 else q["merged_part"], 1)
                            if m < 3:
                                g.wait_ge(q["merged_part"], 2 * dt + m)
            nc.all_engine_barrier(sems_to_clear=range(sems[0].num, sems[-1].num + 1))

        with nc.Block() as block:
            @block.sync
            def _(sp):
                sp.dma_start(a_out, xT[:, :, :]).then_inc(s_x, 16)
                sp.wait_ge(s_x, 32)


def _slab_cols(w, ranges):
    x = np.concatenate([w[:, a:a + n] for a, n in ranges], axis=1)
    return x.reshape(KT, P, -1).transpose(1, 0, 2)


def _stream(i, l):
    out = np.zeros((NSLAB, P, KT * P), np.float32)

    def put(name, x):
        x = x.reshape(P, -1)
        out[SLAB[name], :, :x.shape[1]] = x

    w_in = i["w_in"][l]
    put("small", _slab_cols(w_in, [(O_G, 12), (O_B, 4), (O_A, 4)]))
    for name, ranges in TILES:
        put(name, _slab_cols(w_in, ranges))
    v = _slab_cols(w_in, [(O_SB + 512, 256)])
    put("sbv0", v[:, 0:4])
    put("sbv1", v[:, 4:8])
    for kv in "kv":
        w1 = i[f"nsa_cmp_{kv}_w1"][l].reshape(16, P, 256).transpose(1, 0, 2)
        for j in range(4):
            put(f"c{kv}{j}", w1[:, 4 * j:4 * j + 4])
    w2k = i["nsa_cmp_k_w2"][l].reshape(2, P, HD).transpose(1, 0, 2)
    w2v = i["nsa_cmp_v_w2"][l].reshape(2, P, HD).transpose(1, 0, 2)
    put("cw2", np.concatenate([np.concatenate([w2k, w2k], axis=2).reshape(P, 256), w2v.reshape(P, 128)], axis=1))
    put("glu", i["s5_glu_w"][l].reshape(2, P, 512).transpose(1, 0, 2))
    for g in range(4 * KT):
        put(f"gate{g}", _slab_cols(w_in, [(O_GATE + D * (g % 4) + P * (g // 4), P)]))
    br = i["w_branch"][l].reshape(4, 2, P, D).transpose(2, 0, 1, 3)
    for dt in range(KT):
        c = slice(P * dt, P * dt + P)
        put(f"br{dt}", np.ascontiguousarray(br[:, :, :, c]))
        put(f"out{dt}", _slab_cols(i["w_out"][l], [(P * dt, P)]))
        dn = i["w_down"][l][:, c].reshape(FT, P, P).transpose(1, 0, 2)
        for j in range(3):
            put(f"dn{dt}_{j}", dn[:, KT * j:KT * j + KT])
    for f in range(FT):
        put(f"fg{f}", _slab_cols(i["w_gate"][l], [(P * f, P)]))
        put(f"fu{f}", _slab_cols(i["w_up"][l], [(P * f, P)]))
    return out


def _pack(i, l):
    out = np.zeros((P, NPK), np.float32)

    def put(name, x):
        at, n = PK[name]
        out[:, at:at + n] = x.reshape(P, n)

    two = lambda x: np.concatenate([x, x])
    put("an", i["attn_norm"][l].reshape(KT, P).T)
    put("fn", i["ffn_norm"][l].reshape(KT, P).T)
    put("qn", two(i["nsa_q_norm"][l]))
    kn = i["nsa_k_norm"][l]
    put("kn12", np.concatenate([kn[1], kn[2]]))
    put("kn0", two(kn[0]))
    put("on", two(i["gdn_o_norm"][l]))
    for name, x in (("posk", i["nsa_cmp_pos"][l, 0]), ("posv", i["nsa_cmp_pos"][l, 1])):
        put(name, x.reshape(16, P).T)

    def states(x):
        return np.moveaxis(x.reshape((8, P) + x.shape[2:]), 0, 1)

    put("lre", states(i["s5_lam_re"][l]))
    put("lim", states(i["s5_lam_im"][l]))
    put("ldt", states(np.repeat(i["s5_log_dt"][l][:, None], HD, axis=1)))
    put("bre", states(i["s5_b_re"][l]))
    put("bim", states(i["s5_b_im"][l]))
    for name in ("cre", "cim"):
        c = states(i[f"s5_c_{name[1:]}"][l].transpose(0, 2, 1))
        pad = np.zeros((P, 8, 32), np.float32)
        pad[0:HD, :, 0:16] = c[0:HD]
        pad[HD:P, :, 16:32] = c[HD:P]
        put(name, pad)
    put("dsk", i["s5_d"][l].reshape(2, P).T)
    put("cw", i["gdn_conv_w"][l].T.reshape(6, P, 4).transpose(1, 0, 2))
    for name, x in (("alog", i["gdn_a_log"][l]), ("dtb", i["gdn_dt_bias"][l])):
        put(name, np.broadcast_to(np.tile(x, NT), (P, 4 * NT)))
    return out


def _constants():
    out = np.zeros((P, NCK), np.float32)

    def put(name, x):
        at, n = CK[name]
        out[:, at:at + n] = np.asarray(x, np.float32).reshape(P, n)

    r, c = np.arange(P)[:, None], np.arange(P)[None, :]
    put("ident", r == c)
    put("ones", np.ones((P, P)))
    put("blk", r // HD == c // HD)
    put("le", r <= c)
    put("ge", r >= c)
    put("lt", r < c)
    put("gt", r > c)
    put("negq", np.where(c > r, NEG, 0.0))
    put("negk", np.where(r >= c, NEG, 0.0))
    lev = np.zeros((P, 7, P))
    for n in range(7):
        s = 1 << n
        lev[:, n] = (r // (2 * s) == c // (2 * s)) & (r % (2 * s) < s) & (c % (2 * s) >= s)
    put("lev", lev)
    rot = np.zeros((P, P))
    for b in (0, HD):
        for m in range(8):
            rot[b + m + 8, b + m] = -1.0
            rot[b + m, b + m + 8] = 1.0
    put("rot", rot)
    half = 8
    f = np.float32(500000.0) ** (-np.arange(half, dtype=np.float32) / np.float32(half))
    freq = np.zeros(P, np.float32)
    for b in (0, 8, HD, HD + 8):
        freq[b:b + 8] = f
    put("freq", freq)
    t = P * np.arange(NT)[None, :, None] + np.arange(P)[:, None, None]
    ok = 16 * np.arange(NCMP)[None, None, :] + 31 <= t
    put("c01", ok)
    put("cneg", np.where(ok, 0.0, NEG))
    put("t", np.broadcast_to(np.arange(P), (P, P)))
    put("tc", np.broadcast_to(P * np.repeat(np.arange(NT), 8), (P, 8 * NT)))
    return out


def kernel(**inputs):
    import concourse.bacc as bacc
    from concourse.bass_utils import run_bass_kernel_spmd

    i = {k: np.asarray(v) for k, v in inputs.items()}
    arrays = {
        "x": np.ascontiguousarray(i["x"][0].T.reshape(KT, P, S).transpose(1, 0, 2)),
        "pos": np.ascontiguousarray(np.broadcast_to(i["positions"].reshape(1, S), (P, S))),
        "constants": _constants(),
        "params": np.stack([_pack(i, l) for l in range(DEPTH)]),
        "weights": np.stack([_stream(i, l) for l in range(DEPTH)]),
    }
    nc = bacc.Bacc("TRN2", target_bir_lowering=False, num_devices=1)
    args = [nc.dram_tensor(n, a.shape, mybir.dt.from_np(a.dtype), kind="ExternalInput").ap() for n, a in arrays.items()]
    args.append(nc.dram_tensor("out", (P, KT, S), F32, kind="ExternalOutput").ap())
    args.insert(-1, nc.dram_tensor("gates", (KT, P, 4, S), F32, kind="Internal").ap())
    program(nc, *args)
    got = run_bass_kernel_spmd(nc, [arrays], core_ids=[0]).results[0]["out"]
    return np.ascontiguousarray(np.asarray(got).transpose(1, 0, 2).reshape(D, S).T)[None]
```
